# Optimizing a Trainium2 kernel written in Bass

```python
import math
import jax
import jax.numpy as jnp
from jax import lax
import numpy as np

D_MODEL = 1024
BATCH = 1
SEQ = 256
DEPTH = 2

MIX_WIDTH = D_MODEL
SSD_HEADS = 8
SSD_HEAD_DIM = 64
SSD_INNER = SSD_HEADS * SSD_HEAD_DIM
SSD_GROUPS = 2
SSD_STATE = 128
SSD_CONV = 4
SSD_CHUNK = 256
SSD_XBC = SSD_INNER + 2 * SSD_GROUPS * SSD_STATE
SC_HEADS = 4
SC_HEAD_DIM = 64
SC_WIDTH = SC_HEADS * SC_HEAD_DIM
SC_CONV = 3
NSA_HEADS = 4
NSA_HEAD_DIM = 64
NSA_WIDTH = NSA_HEADS * NSA_HEAD_DIM
NSA_KV = NSA_HEAD_DIM
CMP_BLOCK = 32
CMP_STRIDE = 16
CMP_HIDDEN = 128
SEL_BLOCK = 64
SEL_TOPK = 16
SEL_LOCAL = 2
WINDOW = 512
Q_BLOCK = 128
ROPE_THETA = 10000.0
D_FF = 2752
FFN_CONV = 3
EPS = 1e-6
NEG = -1e30
FORCE = 1e9
IN_SIZES = (SSD_INNER, SSD_XBC, SSD_HEADS, SC_WIDTH, SC_WIDTH, SC_WIDTH, NSA_WIDTH,
            NSA_KV, NSA_KV, NSA_KV, NSA_KV, NSA_KV, NSA_KV, 3 * NSA_HEADS)
N_IN = sum(IN_SIZES)


def rmsnorm(x, w):
    xf = x.astype(jnp.float32)
    y = xf * lax.rsqrt(jnp.mean(xf * xf, axis=-1, keepdims=True) + EPS)
    return (y * w.astype(jnp.float32)).astype(x.dtype)

def causal_dwconv(u, w, b=None):
    width = w.shape[0]
    s_len = u.shape[1]
    up = jnp.pad(u, ((0, 0), (width - 1, 0), (0, 0)))
    out = up[:, 0:s_len] * w[0]
    for j in range(1, width):
        out = out + up[:, j:j + s_len] * w[j]
    if b is not None:
        out = out + b
    return out

def rope_tables(s_len):
    half = NSA_HEAD_DIM // 2
    inv = 1.0 / (ROPE_THETA ** (jnp.arange(half, dtype=jnp.float32) / half))
    ang = jnp.arange(s_len, dtype=jnp.float32)[:, None] * inv[None, :]
    return jnp.cos(ang), jnp.sin(ang)

def apply_rope(x, cos, sin):
    x1, x2 = jnp.split(x, 2, axis=-1)
    c = cos[None, :, None, :].astype(x.dtype)
    s = sin[None, :, None, :].astype(x.dtype)
    return jnp.concatenate([x1 * c - x2 * s, x2 * c + x1 * s], axis=-1)

def masked_softmax(s, mask):
    s = jnp.where(mask, s.astype(jnp.float32), NEG)
    m = jnp.max(s, axis=-1, keepdims=True)
    p = jnp.exp(s - m) * mask
    return p / jnp.maximum(jnp.sum(p, axis=-1, keepdims=True), 1e-20)

def ssd_mixer(z, xbc, dt_raw, conv_w, conv_b, dt_bias, a_log, d_skip, norm_w):
    f32 = jnp.float32
    bsz, s_len, _ = z.shape
    n_k = SSD_HEADS // SSD_GROUPS
    xbc = jax.nn.silu(causal_dwconv(xbc, conv_w, conv_b))
    xs, b_in, c_in = jnp.split(xbc, [SSD_INNER, SSD_INNER + SSD_GROUPS * SSD_STATE], axis=-1)
    dt = jax.nn.softplus((dt_raw + dt_bias).astype(f32))
    a_neg = -jnp.exp(a_log.astype(f32)).reshape(SSD_GROUPS, n_k)
    pad = (-s_len) % SSD_CHUNK
    s_pad = s_len + pad
    n_c = s_pad // SSD_CHUNK

    def chunked(t, *tail):
        t = jnp.pad(t.astype(f32), ((0, 0), (0, pad), (0, 0)))
        return t.reshape(bsz, n_c, SSD_CHUNK, *tail)

    x_c = chunked(xs, SSD_GROUPS, n_k, SSD_HEAD_DIM)
    dt_c = chunked(dt, SSD_GROUPS, n_k)
    b_c = chunked(b_in, SSD_GROUPS, SSD_STATE)
    c_c = chunked(c_in, SSD_GROUPS, SSD_STATE)
    xdt = x_c * dt_c[..., None]
    a = jnp.transpose(dt_c * a_neg, (0, 3, 4, 1, 2))
    a_cs = jnp.cumsum(a, axis=-1)
    causal = jnp.tril(jnp.ones((SSD_CHUNK, SSD_CHUNK), dtype=bool))
    seg = a_cs[..., :, None] - a_cs[..., None, :]
    decay = jnp.exp(jnp.where(causal, seg, -jnp.inf))
    cb = jnp.einsum('bclgn,bcsgn->bgcls', c_c, b_c)
    y_diag = jnp.einsum('bgkcls,bcsgkp->bclgkp', decay * cb[:, :, None], xdt)
    decay_to_end = jnp.exp(a_cs[..., -1:] - a_cs)
    chunk_states = jnp.einsum('bclgn,bgkcl,bclgkp->cbgkpn', b_c, decay_to_end, xdt)
    chunk_decay = jnp.moveaxis(jnp.exp(a_cs[..., -1]), -1, 0)

    def step(h, inp):
        s_new, d_c = inp
        return h * d_c[..., None, None] + s_new, h

    h0 = jnp.zeros((bsz, SSD_GROUPS, n_k, SSD_HEAD_DIM, SSD_STATE), f32)
    _, prev_states = lax.scan(step, h0, (chunk_states, chunk_decay))
    y_off = jnp.einsum('bclgn,cbgkpn,bgkcl->bclgkp', c_c, prev_states, jnp.exp(a_cs))
    y = y_diag + y_off + x_c * d_skip.astype(f32).reshape(SSD_GROUPS, n_k)[:, :, None]
    y = y.reshape(bsz, s_pad, SSD_INNER)[:, :s_len]
    y = y * jax.nn.silu(z.astype(f32))
    return rmsnorm(y, norm_w).astype(z.dtype)

def compress_block(t, pos, w1, w2):
    bsz, s_len, dk = t.shape
    n_cmp = (s_len - CMP_BLOCK) // CMP_STRIDE + 1
    idx = np.arange(n_cmp)[:, None] * CMP_STRIDE + np.arange(CMP_BLOCK)[None, :]
    blocks = (t[:, idx] + pos).reshape(bsz, n_cmp, CMP_BLOCK * dk)
    return jax.nn.gelu(blocks @ w1) @ w2

def nsa_mixer(q, k_cmp, v_cmp, k_sel, v_sel, k_win, v_win, gate_logits, cos, sin,
              kpos, kw1, kw2, vpos, vw1, vw2):
    bsz, s_len, _ = q.shape
    dk = NSA_HEAD_DIM
    q = apply_rope(q.reshape(bsz, s_len, NSA_HEADS, dk), cos, sin) * (dk ** -0.5)

    def rope_k(t):
        return apply_rope(t[:, :, None, :], cos, sin)[:, :, 0, :]

    kc = compress_block(rope_k(k_cmp), kpos, kw1, kw2)
    vc = compress_block(v_cmp, vpos, vw1, vw2)
    n_cmp = kc.shape[1]
    n_slc = s_len // SEL_BLOCK
    top = min(SEL_TOPK, n_slc)
    cmp_start = np.arange(n_cmp) * CMP_STRIDE
    slc_start = np.arange(n_slc) * SEL_BLOCK
    cmp_end = jnp.asarray(cmp_start + CMP_BLOCK - 1, jnp.int32)
    overlap = jnp.asarray(((cmp_start[:, None] < slc_start[None, :] + SEL_BLOCK)
                           & (cmp_start[:, None] + CMP_BLOCK > slc_start[None, :])).astype(np.float32))
    ks_blocks = rope_k(k_sel).reshape(bsz, n_slc, SEL_BLOCK, dk)
    vs_blocks = v_sel.reshape(bsz, n_slc, SEL_BLOCK, dk)
    win_pad = ((0, 0), (WINDOW, 0), (0, 0))
    kw = jnp.pad(rope_k(k_win), win_pad)
    vw = jnp.pad(v_win, win_pad)
    gates = jax.nn.sigmoid(gate_logits.astype(jnp.float32)).reshape(bsz, s_len, NSA_HEADS, 3)
    n_qb = s_len // Q_BLOCK

    def to_blocks(t):
        return jnp.moveaxis(t.reshape(bsz, n_qb, Q_BLOCK, *t.shape[2:]), 1, 0)

    blk = jnp.arange(n_slc)
    offs = jnp.arange(SEL_BLOCK)
    gather = jax.vmap(lambda blocks, idx: blocks[idx])

    def block_fn(args):
        qb, gb, qi = args
        t = qi * Q_BLOCK + jnp.arange(Q_BLOCK)
        p_c = masked_softmax(jnp.einsum('bqhd,bnd->bhqn', qb, kc), cmp_end[None, :] <= t[:, None])
        o_c = jnp.einsum('bhqn,bnd->bqhd', p_c, vc)
        imp = jnp.einsum('bhqn,nj->bqj', p_c, overlap)
        cur = (t // SEL_BLOCK)[:, None]
        valid = blk[None, :] <= cur
        forced = (blk[None, :] == 0) | (valid & (blk[None, :] > cur - SEL_LOCAL))
        imp = jnp.where(forced, FORCE, jnp.where(valid, imp, NEG))
        _, sel = lax.top_k(imp, top)
        ks = gather(ks_blocks, sel).reshape(bsz, Q_BLOCK, top * SEL_BLOCK, dk)
        vs = gather(vs_blocks, sel).reshape(bsz, Q_BLOCK, top * SEL_BLOCK, dk)
        tok = (sel[..., None] * SEL_BLOCK + offs).reshape(bsz, Q_BLOCK, top * SEL_BLOCK)
        m_s = (tok <= t[None, :, None])[:, None]
        p_s = masked_softmax(jnp.einsum('bqhd,bqnd->bhqn', qb, ks), m_s)
        o_s = jnp.einsum('bhqn,bqnd->bqhd', p_s, vs)
        start = qi * Q_BLOCK
        kwb = lax.dynamic_slice_in_dim(kw, start, Q_BLOCK + WINDOW, axis=1)
        vwb = lax.dynamic_slice_in_dim(vw, start, Q_BLOCK + WINDOW, axis=1)
        kp = start - WINDOW + jnp.arange(Q_BLOCK + WINDOW)
        m_w = (kp[None, :] >= 0) & (kp[None, :] <= t[:, None]) & (kp[None, :] > t[:, None] - WINDOW)
        p_w = masked_softmax(jnp.einsum('bqhd,bkd->bhqk', qb, kwb), m_w)
        o_w = jnp.einsum('bhqk,bkd->bqhd', p_w, vwb)
        return o_c * gb[..., 0:1] + o_s * gb[..., 1:2] + o_w * gb[..., 2:3]

    out = lax.map(block_fn, (to_blocks(q), to_blocks(gates), jnp.arange(n_qb)))
    return jnp.moveaxis(out, 0, 1).reshape(bsz, s_len, NSA_WIDTH).astype(q.dtype)

def first_inputs(seed: int = 0) -> dict:
    key = jax.random.key(seed)
    ks = jax.random.split(key, 24)
    f32 = jnp.float32
    nl = DEPTH
    cmp_in = CMP_BLOCK * NSA_HEAD_DIM

    def nrm(k, shape, scale):
        return jax.random.normal(k, shape, f32) * scale

    dt0 = jnp.exp(jax.random.uniform(ks[5], (nl, SSD_HEADS), f32, math.log(1e-3), math.log(1e-1)))
    return {
        'x': nrm(ks[0], (BATCH, SEQ, D_MODEL), 1.0),
        'attn_norm_w': 1.0 + nrm(ks[1], (nl, D_MODEL), 0.02),
        'w_in': nrm(ks[2], (nl, D_MODEL, N_IN), D_MODEL ** -0.5),
        'ssd_conv_w': nrm(ks[3], (nl, SSD_CONV, SSD_XBC), SSD_CONV ** -0.5),
        'ssd_conv_b': nrm(ks[4], (nl, SSD_XBC), 0.02),
        'ssd_dt_bias': dt0 + jnp.log(-jnp.expm1(-dt0)),
        'ssd_a_log': jnp.log(jax.random.uniform(ks[6], (nl, SSD_HEADS), f32, 1.0, 16.0)),
        'ssd_d': 1.0 + nrm(ks[7], (nl, SSD_HEADS), 0.02),
        'ssd_norm_w': 1.0 + nrm(ks[8], (nl, SSD_INNER), 0.02),
        'sc_conv_w': nrm(ks[9], (nl, SC_CONV, SC_WIDTH), SC_CONV ** -0.5),
        'cmp_k_pos': nrm(ks[10], (nl, CMP_BLOCK, NSA_HEAD_DIM), 0.02),
        'cmp_k_w1': nrm(ks[11], (nl, cmp_in, CMP_HIDDEN), cmp_in ** -0.5),
        'cmp_k_w2': nrm(ks[12], (nl, CMP_HIDDEN, NSA_HEAD_DIM), CMP_HIDDEN ** -0.5),
        'cmp_v_pos': nrm(ks[13], (nl, CMP_BLOCK, NSA_HEAD_DIM), 0.02),
        'cmp_v_w1': nrm(ks[14], (nl, cmp_in, CMP_HIDDEN), cmp_in ** -0.5),
        'cmp_v_w2': nrm(ks[15], (nl, CMP_HIDDEN, NSA_HEAD_DIM), CMP_HIDDEN ** -0.5),
        'w_out': nrm(ks[16], (nl, MIX_WIDTH, D_MODEL), MIX_WIDTH ** -0.5),
        'ffn_norm_w': 1.0 + nrm(ks[17], (nl, D_MODEL), 0.02),
        'ffn_w_up': nrm(ks[18], (nl, D_MODEL, 2 * D_FF), D_MODEL ** -0.5),
        'ffn_conv_w': nrm(ks[19], (nl, FFN_CONV, 2 * D_FF), FFN_CONV ** -0.5),
        'ffn_conv_b': nrm(ks[20], (nl, 2 * D_FF), 0.02),
        'ffn_w_down': nrm(ks[21], (nl, D_FF, D_MODEL), D_FF ** -0.5),
        'final_norm_w': 1.0 + nrm(ks[22], (D_MODEL,), 0.02),
    }

def first_block(x, attn_norm_w, w_in, ssd_conv_w, ssd_conv_b, ssd_dt_bias, ssd_a_log, ssd_d,
              ssd_norm_w, sc_conv_w, cmp_k_pos, cmp_k_w1, cmp_k_w2, cmp_v_pos, cmp_v_w1, cmp_v_w2,
              w_out, ffn_norm_w, ffn_w_up, ffn_conv_w, ffn_conv_b, ffn_w_down, final_norm_w):
    s_len = x.shape[1]
    cos, sin = rope_tables(s_len)
    split_at = np.cumsum(np.array(IN_SIZES))[:-1].tolist()
    for l in range(DEPTH):
        h = rmsnorm(x, attn_norm_w[l])
        proj = h @ w_in[l]
        (z, xbc, dt_raw, sc_b, sc_c, sc_h, q, k_c, v_c, k_s, v_s, k_w, v_w,
         g_nsa) = jnp.split(proj, split_at, axis=-1)
        y_ssd = ssd_mixer(z, xbc, dt_raw, ssd_conv_w[l], ssd_conv_b[l], ssd_dt_bias[l],
                          ssd_a_log[l], ssd_d[l], ssd_norm_w[l])
        y_sc = sc_b * causal_dwconv(sc_c * sc_h, sc_conv_w[l])
        y_nsa = nsa_mixer(q, k_c, v_c, k_s, v_s, k_w, v_w, g_nsa, cos, sin,
                          cmp_k_pos[l], cmp_k_w1[l], cmp_k_w2[l],
                          cmp_v_pos[l], cmp_v_w1[l], cmp_v_w2[l])
        x = x + jnp.concatenate([y_ssd, y_sc, y_nsa], axis=-1) @ w_out[l]
        h = rmsnorm(x, ffn_norm_w[l])
        u = causal_dwconv(h @ ffn_w_up[l], ffn_conv_w[l], ffn_conv_b[l])
        gate, val = jnp.split(u, 2, axis=-1)
        x = x + (jax.nn.silu(gate) * val) @ ffn_w_down[l]
    return rmsnorm(x, final_norm_w)


GRID_W = 64
CTX_LEN = 256
N_MIXERS = 4
N_MOD = 9
D_FF_2 = 2816
ROPE_BASE = 10000.0
ROPE_DIM = 64
NEG_INF = -1e30

MLA_HEADS = 8
MLA_Q_RANK = 512
MLA_KV_RANK = 256
MLA_NOPE = 128
MLA_ROPE = ROPE_DIM
MLA_V = 128

SWA_Q_HEADS = 16
SWA_KV_HEADS = 4
SWA_GROUP = SWA_Q_HEADS // SWA_KV_HEADS
SWA_HEAD_DIM = ROPE_DIM
SWA_WINDOW = 128

NA_HEADS = 16
NA_HEAD_DIM = D_MODEL // NA_HEADS
NA_KH = 8
NA_KW = 16

DIFF_HEADS = 8
DIFF_HEAD_DIM = ROPE_DIM


def rms_norm(x, g):
    xf = x.astype(jnp.float32)
    y = xf * lax.rsqrt(jnp.mean(xf * xf, axis=-1, keepdims=True) + EPS)
    return (y * g.astype(jnp.float32)).astype(x.dtype)

def modulate(h, shift, scale):
    return h * (1.0 + scale) + shift

def swiglu(h, w_in, w_out):
    g, u = jnp.split(h @ w_in, 2, axis=-1)
    return (jax.nn.silu(g) * u) @ w_out

def axial_rope_tables(L, dim):
    t = jnp.arange(L, dtype=jnp.int32)
    row = (t // GRID_W).astype(jnp.float32)
    col = (t % GRID_W).astype(jnp.float32)
    n_freq = dim // 4
    inv = jnp.exp(-math.log(ROPE_BASE) * jnp.arange(n_freq, dtype=jnp.float32) / n_freq)
    ang = jnp.concatenate([row[:, None] * inv, col[:, None] * inv], axis=-1)
    return jnp.cos(ang), jnp.sin(ang)

def apply_rope_2(x, cos, sin):
    half = x.shape[-1] // 2
    x1 = x[..., :half].astype(jnp.float32)
    x2 = x[..., half:].astype(jnp.float32)
    return jnp.concatenate([x1 * cos - x2 * sin, x1 * sin + x2 * cos], axis=-1).astype(x.dtype)

def softmax32(s):
    return jax.nn.softmax(s.astype(jnp.float32), axis=-1)

def joint_softmax(*scores):
    sizes = [s.shape[-1] for s in scores]
    p = softmax32(jnp.concatenate([s.astype(jnp.float32) for s in scores], axis=-1))
    cuts = [int(v) for v in np.cumsum(sizes)[:-1]]
    return jnp.split(p, cuts, axis=-1)

def to_blocks(t):
    lead = t.shape[:-2]
    L, d = t.shape[-2], t.shape[-1]
    t = t.reshape(lead + (L // Q_BLOCK, Q_BLOCK, d))
    return jnp.moveaxis(t, -3, 0)

def from_blocks(t):
    t = jnp.moveaxis(t, 0, -3)
    lead = t.shape[:-3]
    nb, qb, d = t.shape[-3], t.shape[-2], t.shape[-1]
    return t.reshape(lead + (nb * qb, d))

def merge_heads(o):
    B, H, N, d = o.shape
    return o.transpose(0, 2, 1, 3).reshape(B, N, H * d)

def pv(eq, p, v):
    return jnp.einsum(eq, p.astype(v.dtype), v)

def mla_mixer(hx, hc, w_down, q_norm, kv_norm, w_uq, w_ukv, w_o, cos, sin, ctx_out):
    H = MLA_HEADS
    scale = (MLA_NOPE + MLA_ROPE) ** -0.5

    def project(h):
        B, N, _ = h.shape
        d = h @ w_down
        cq = rms_norm(d[..., :MLA_Q_RANK], q_norm)
        ckv = rms_norm(d[..., MLA_Q_RANK:MLA_Q_RANK + MLA_KV_RANK], kv_norm)
        k_rope = d[..., MLA_Q_RANK + MLA_KV_RANK:]
        q = (cq @ w_uq).reshape(B, N, H, MLA_NOPE + MLA_ROPE).transpose(0, 2, 1, 3)
        kv = (ckv @ w_ukv).reshape(B, N, H, MLA_NOPE + MLA_V).transpose(0, 2, 1, 3)
        return q[..., :MLA_NOPE], q[..., MLA_NOPE:], kv[..., :MLA_NOPE], k_rope, kv[..., MLA_NOPE:]

    qn_x, qr_x, kn_x, kr_x, v_x = project(hx)
    qn_c, qr_c, kn_c, kr_c, v_c = project(hc)
    qr_x_rot = apply_rope_2(qr_x, cos, sin)
    kr_x_rot = apply_rope_2(kr_x, cos, sin)

    def scores(qn, qr, kn, kr):
        s = jnp.einsum('bhqd,bhkd->bhqk', qn, kn) + jnp.einsum('bhqr,bkr->bhqk', qr, kr)
        return s.astype(jnp.float32) * scale

    def block(args):
        qn, qr_rot, qr_pl = args
        p_x, p_c = joint_softmax(scores(qn, qr_rot, kn_x, kr_x_rot), scores(qn, qr_pl, kn_c, kr_c))
        return pv('bhqk,bhkd->bhqd', p_x, v_x) + pv('bhqk,bhkd->bhqd', p_c, v_c)

    o_x = from_blocks(lax.map(block, (to_blocks(qn_x), to_blocks(qr_x_rot), to_blocks(qr_x))))
    out_x = merge_heads(o_x) @ w_o
    out_c = None
    if ctx_out:
        p = softmax32(scores(qn_c, qr_c, kn_c, kr_c))
        out_c = merge_heads(pv('bhqk,bhkd->bhqd', p, v_c)) @ w_o
    return out_x, out_c

def swa_mixer(hx, hc, w_qkv, sink, w_o, cos, sin, ctx_out):
    Hk, G, Dh = SWA_KV_HEADS, SWA_GROUP, SWA_HEAD_DIM
    scale = Dh ** -0.5

    def project(h):
        B, N, _ = h.shape
        p = h @ w_qkv
        q = p[..., :Hk * G * Dh].reshape(B, N, Hk, G, Dh).transpose(0, 2, 3, 1, 4)
        k = p[..., Hk * G * Dh:(Hk * G + Hk) * Dh].reshape(B, N, Hk, Dh).transpose(0, 2, 1, 3)
        v = p[..., (Hk * G + Hk) * Dh:].reshape(B, N, Hk, Dh).transpose(0, 2, 1, 3)
        return q, k, v

    B, L, _ = hx.shape
    C = hc.shape[1]
    q_x, k_x, v_x = project(hx)
    q_c, k_c, v_c = project(hc)
    q_x_rot = apply_rope_2(q_x, cos, sin)
    k_x_rot = apply_rope_2(k_x, cos, sin)
    pad = ((0, 0), (0, 0), (SWA_WINDOW, SWA_WINDOW), (0, 0))
    k_pad = jnp.pad(k_x_rot, pad)
    v_pad = jnp.pad(v_x, pad)
    span = Q_BLOCK + 2 * SWA_WINDOW
    qi = jnp.arange(Q_BLOCK)
    kj = jnp.arange(span)
    sink_b = sink.reshape(Hk, G)[None, :, :, None, None].astype(jnp.float32)

    def ctx_scores(q):
        return jnp.einsum('bkgqd,bkcd->bkgqc', q, k_c).astype(jnp.float32) * scale

    def block(args):
        n, q_rot, q_pl = args
        start = n * Q_BLOCK
        k_b = lax.dynamic_slice_in_dim(k_pad, start, span, axis=2)
        v_b = lax.dynamic_slice_in_dim(v_pad, start, span, axis=2)
        qpos = start + qi
        kpos = start - SWA_WINDOW + kj
        valid = ((jnp.abs(kpos[None, :] - qpos[:, None]) <= SWA_WINDOW)
                 & (kpos[None, :] >= 0) & (kpos[None, :] < L))
        s_w = jnp.einsum('bkgqd,bkjd->bkgqj', q_rot, k_b).astype(jnp.float32) * scale
        s_w = jnp.where(valid, s_w, NEG_INF)
        s_c = ctx_scores(q_pl)
        s_s = jnp.broadcast_to(sink_b, s_c.shape[:-1] + (1,))
        p_w, p_c, _ = joint_softmax(s_w, s_c, s_s)
        return pv('bkgqj,bkjd->bkgqd', p_w, v_b) + pv('bkgqc,bkcd->bkgqd', p_c, v_c)

    nb = L // Q_BLOCK
    o = from_blocks(lax.map(block, (jnp.arange(nb), to_blocks(q_x_rot), to_blocks(q_x))))
    out_x = o.transpose(0, 3, 1, 2, 4).reshape(B, L, Hk * G * Dh) @ w_o
    out_c = None
    if ctx_out:
        s_c = ctx_scores(q_c)
        s_s = jnp.broadcast_to(sink_b, s_c.shape[:-1] + (1,))
        p_c, _ = joint_softmax(s_c, s_s)
        o_c = pv('bkgqc,bkcd->bkgqd', p_c, v_c)
        out_c = o_c.transpose(0, 3, 1, 2, 4).reshape(B, C, Hk * G * Dh) @ w_o
    return out_x, out_c

def na_mixer(hx, hc, w_qkv, rpb, w_o, ctx_out):
    H, Dh = NA_HEADS, NA_HEAD_DIM
    scale = Dh ** -0.5

    def project(h):
        B, N, _ = h.shape
        p = (h @ w_qkv).reshape(B, N, 3, H, Dh).transpose(2, 0, 3, 1, 4)
        return p[0], p[1], p[2]

    B, L, _ = hx.shape
    rows = L // GRID_W
    kh = min(NA_KH, rows)
    kw = NA_KW
    q_x, k_x, v_x = project(hx)
    q_c, k_c, v_c = project(hc)
    col = jnp.arange(GRID_W)
    col_start = jnp.clip(col - kw // 2, 0, GRID_W - kw)
    key_cols = col_start[:, None] + jnp.arange(kw)[None, :]
    col_off = key_cols - col[:, None] + (NA_KW - 1)

    def block(args):
        r, q_row = args
        row_start = jnp.clip(r - kh // 2, 0, rows - kh)
        key_rows = row_start + jnp.arange(kh)
        idx = (key_rows[None, :, None] * GRID_W + key_cols[:, None, :]).reshape(-1)
        k_g = jnp.take(k_x, idx, axis=2).reshape(B, H, GRID_W, kh * kw, Dh)
        v_g = jnp.take(v_x, idx, axis=2).reshape(B, H, GRID_W, kh * kw, Dh)
        row_off = key_rows - r + (NA_KH - 1)
        bias = rpb[:, row_off[None, :, None], col_off[:, None, :]]
        bias = bias.reshape(H, GRID_W, kh * kw).astype(jnp.float32)
        s_n = jnp.einsum('bhqd,bhqkd->bhqk', q_row, k_g).astype(jnp.float32) * scale + bias[None]
        s_c = jnp.einsum('bhqd,bhcd->bhqc', q_row, k_c).astype(jnp.float32) * scale
        p_n, p_c = joint_softmax(s_n, s_c)
        return pv('bhqk,bhqkd->bhqd', p_n, v_g) + pv('bhqc,bhcd->bhqd', p_c, v_c)

    q_rows = q_x.reshape(B, H, rows, GRID_W, Dh).transpose(2, 0, 1, 3, 4)
    o = lax.map(block, (jnp.arange(rows), q_rows))
    out_x = o.transpose(1, 0, 3, 2, 4).reshape(B, L, H * Dh) @ w_o
    out_c = None
    if ctx_out:
        p = softmax32(jnp.einsum('bhqd,bhcd->bhqc', q_c, k_c).astype(jnp.float32) * scale)
        out_c = merge_heads(pv('bhqc,bhcd->bhqd', p, v_c)) @ w_o
    return out_x, out_c

def diff_mixer(hx, hc, w_qkv, lam_params, norm_g, w_o, cos, sin, lam_init, ctx_out):
    H, Dh = DIFF_HEADS, DIFF_HEAD_DIM
    scale = Dh ** -0.5

    def project(h):
        B, N, _ = h.shape
        p = h @ w_qkv
        q = p[..., :H * 2 * Dh].reshape(B, N, H, 2, Dh).transpose(0, 2, 3, 1, 4)
        k = p[..., H * 2 * Dh:H * 4 * Dh].reshape(B, N, H, 2, Dh).transpose(0, 2, 3, 1, 4)
        v = p[..., H * 4 * Dh:].reshape(B, N, H, 2 * Dh).transpose(0, 2, 1, 3)
        return q, k, v

    q_x, k_x, v_x = project(hx)
    q_c, k_c, v_c = project(hc)
    q_x_rot = apply_rope_2(q_x, cos, sin)
    k_x_rot = apply_rope_2(k_x, cos, sin)
    lp = lam_params.astype(jnp.float32)
    lam = jnp.exp(jnp.sum(lp[0] * lp[1])) - jnp.exp(jnp.sum(lp[2] * lp[3])) + lam_init

    def scores(q, k):
        return jnp.einsum('bhiqd,bhikd->bhiqk', q, k).astype(jnp.float32) * scale

    def block(args):
        q_rot, q_pl = args
        p_x, p_c = joint_softmax(scores(q_rot, k_x_rot), scores(q_pl, k_c))
        a_x = p_x[:, :, 0] - lam * p_x[:, :, 1]
        a_c = p_c[:, :, 0] - lam * p_c[:, :, 1]
        return pv('bhqk,bhkd->bhqd', a_x, v_x) + pv('bhqk,bhkd->bhqd', a_c, v_c)

    def finish(o):
        return merge_heads(rms_norm(o, norm_g) * (1.0 - lam_init)) @ w_o

    o_x = from_blocks(lax.map(block, (to_blocks(q_x_rot), to_blocks(q_x))))
    out_x = finish(o_x)
    out_c = None
    if ctx_out:
        p = softmax32(scores(q_c, k_c))
        out_c = finish(pv('bhqk,bhkd->bhqd', p[:, :, 0] - lam * p[:, :, 1], v_c))
    return out_x, out_c

def second_inputs(seed: int = 0) -> dict:
    key = jax.random.key(seed)
    keys = jax.random.split(key, 32)
    counter = [0]

    def normal(shape, std):
        k = keys[counter[0]]
        counter[0] += 1
        return jax.random.normal(k, shape, jnp.float32) * std

    def gain(shape):
        return 1.0 + normal(shape, 0.02)

    nA, nB, nC, nD = [len(range(m, DEPTH, N_MIXERS)) for m in range(N_MIXERS)]
    D = D_MODEL
    return {
        'x': normal((BATCH, SEQ, D), 1.0),
        'c': normal((BATCH, D), 1.0),
        'ctx': normal((BATCH, CTX_LEN, D), 1.0),
        'c_ctx': normal((D,), 1.0),
        'mod_w': normal((DEPTH, D, N_MOD * D), 0.5 * D ** -0.5),
        'mod_b': normal((DEPTH, N_MOD * D), 0.02),
        'norm_g': gain((DEPTH, 3, D)),
        'final_norm_g': gain((D,)),
        'ffn_w_in': normal((DEPTH, 2, D, 2 * D_FF_2), D ** -0.5),
        'ffn_w_out': normal((DEPTH, 2, D_FF_2, D), D_FF_2 ** -0.5),
        'mla_w_down': normal((nA, D, MLA_Q_RANK + MLA_KV_RANK + MLA_ROPE), D ** -0.5),
        'mla_q_norm': gain((nA, MLA_Q_RANK)),
        'mla_kv_norm': gain((nA, MLA_KV_RANK)),
        'mla_w_uq': normal((nA, MLA_Q_RANK, MLA_HEADS * (MLA_NOPE + MLA_ROPE)), MLA_Q_RANK ** -0.5),
        'mla_w_ukv': normal((nA, MLA_KV_RANK, MLA_HEADS * (MLA_NOPE + MLA_V)), MLA_KV_RANK ** -0.5),
        'mla_w_o': normal((nA, MLA_HEADS * MLA_V, D), (MLA_HEADS * MLA_V) ** -0.5),
        'swa_w_qkv': normal((nB, D, (SWA_Q_HEADS + 2 * SWA_KV_HEADS) * SWA_HEAD_DIM), D ** -0.5),
        'swa_sink': normal((nB, SWA_Q_HEADS), 0.5),
        'swa_w_o': normal((nB, SWA_Q_HEADS * SWA_HEAD_DIM, D), (SWA_Q_HEADS * SWA_HEAD_DIM) ** -0.5),
        'na_w_qkv': normal((nC, D, 3 * NA_HEADS * NA_HEAD_DIM), D ** -0.5),
        'na_rpb': normal((nC, NA_HEADS, 2 * NA_KH - 1, 2 * NA_KW - 1), 0.2),
        'na_w_o': normal((nC, NA_HEADS * NA_HEAD_DIM, D), (NA_HEADS * NA_HEAD_DIM) ** -0.5),
        'diff_w_qkv': normal((nD, D, 6 * DIFF_HEADS * DIFF_HEAD_DIM), D ** -0.5),
        'diff_lambda': normal((nD, 4, DIFF_HEAD_DIM), 0.1),
        'diff_norm_g': gain((nD, 2 * DIFF_HEAD_DIM)),
        'diff_w_o': normal((nD, 2 * DIFF_HEADS * DIFF_HEAD_DIM, D), (2 * DIFF_HEADS * DIFF_HEAD_DIM) ** -0.5),
    }

def second_block(x, c, ctx, c_ctx, mod_w, mod_b, norm_g, final_norm_g, ffn_w_in, ffn_w_out,
              mla_w_down, mla_q_norm, mla_kv_norm, mla_w_uq, mla_w_ukv, mla_w_o,
              swa_w_qkv, swa_sink, swa_w_o, na_w_qkv, na_rpb, na_w_o,
              diff_w_qkv, diff_lambda, diff_norm_g, diff_w_o):
    L = x.shape[1]
    cos, sin = axial_rope_tables(L, ROPE_DIM)
    xc = ctx
    cond_x = jax.nn.silu(c)
    cond_c = jax.nn.silu(c_ctx)
    for layer in range(DEPTH):
        kind = layer % N_MIXERS
        j = layer // N_MIXERS
        last = layer == DEPTH - 1
        mx = jnp.split((cond_x @ mod_w[layer] + mod_b[layer])[:, None, :], N_MOD, axis=-1)
        mc = jnp.split(cond_c @ mod_w[layer] + mod_b[layer], N_MOD, axis=-1)

        x = x + 0.5 * mx[2] * swiglu(modulate(rms_norm(x, norm_g[layer, 0]), mx[0], mx[1]),
                                     ffn_w_in[layer, 0], ffn_w_out[layer, 0])
        xc = xc + 0.5 * mc[2] * swiglu(modulate(rms_norm(xc, norm_g[layer, 0]), mc[0], mc[1]),
                                       ffn_w_in[layer, 0], ffn_w_out[layer, 0])

        hx = modulate(rms_norm(x, norm_g[layer, 1]), mx[3], mx[4])
        hc = modulate(rms_norm(xc, norm_g[layer, 1]), mc[3], mc[4])
        if kind == 0:
            ox, oc = mla_mixer(hx, hc, mla_w_down[j], mla_q_norm[j], mla_kv_norm[j], mla_w_uq[j],
                               mla_w_ukv[j], mla_w_o[j], cos, sin, not last)
        elif kind == 1:
            ox, oc = swa_mixer(hx, hc, swa_w_qkv[j], swa_sink[j], swa_w_o[j], cos, sin, not last)
        elif kind == 2:
            ox, oc = na_mixer(hx, hc, na_w_qkv[j], na_rpb[j], na_w_o[j], not last)
        else:
            lam_init = 0.8 - 0.6 * math.exp(-0.3 * layer)
            ox, oc = diff_mixer(hx, hc, diff_w_qkv[j], diff_lambda[j], diff_norm_g[j], diff_w_o[j],
                                cos, sin, lam_init, not last)
        x = x + mx[5] * ox

        x = x + 0.5 * mx[8] * swiglu(modulate(rms_norm(x, norm_g[layer, 2]), mx[6], mx[7]),
                                     ffn_w_in[layer, 1], ffn_w_out[layer, 1])
        if not last:
            xc = xc + mc[5] * oc
            xc = xc + 0.5 * mc[8] * swiglu(modulate(rms_norm(xc, norm_g[layer, 2]), mc[6], mc[7]),
                                           ffn_w_in[layer, 1], ffn_w_out[layer, 1])
    return rms_norm(x, final_norm_g)


def setup_inputs(seed=0):
    out = dict(first_inputs(seed))
    for name, value in second_inputs(seed + 1).items():
        if name != "x":
            out[name + "_2"] = value
    return out


def reference(
    x, attn_norm_w, w_in, ssd_conv_w, ssd_conv_b, ssd_dt_bias, ssd_a_log, ssd_d, ssd_norm_w,
    sc_conv_w, cmp_k_pos, cmp_k_w1, cmp_k_w2, cmp_v_pos, cmp_v_w1, cmp_v_w2, w_out, ffn_norm_w,
    ffn_w_up, ffn_conv_w, ffn_conv_b, ffn_w_down, final_norm_w, c_2, ctx_2, c_ctx_2, mod_w_2,
    mod_b_2, norm_g_2, final_norm_g_2, ffn_w_in_2, ffn_w_out_2, mla_w_down_2, mla_q_norm_2,
    mla_kv_norm_2, mla_w_uq_2, mla_w_ukv_2, mla_w_o_2, swa_w_qkv_2, swa_sink_2, swa_w_o_2,
    na_w_qkv_2, na_rpb_2, na_w_o_2, diff_w_qkv_2, diff_lambda_2, diff_norm_g_2, diff_w_o_2,
):
    x = first_block(
        x, attn_norm_w, w_in, ssd_conv_w, ssd_conv_b, ssd_dt_bias, ssd_a_log, ssd_d, ssd_norm_w,
        sc_conv_w, cmp_k_pos, cmp_k_w1, cmp_k_w2, cmp_v_pos, cmp_v_w1, cmp_v_w2, w_out,
        ffn_norm_w, ffn_w_up, ffn_conv_w, ffn_conv_b, ffn_w_down, final_norm_w,
    )
    return second_block(
        x, c_2, ctx_2, c_ctx_2, mod_w_2, mod_b_2, norm_g_2, final_norm_g_2, ffn_w_in_2,
        ffn_w_out_2, mla_w_down_2, mla_q_norm_2, mla_kv_norm_2, mla_w_uq_2, mla_w_ukv_2,
        mla_w_o_2, swa_w_qkv_2, swa_sink_2, swa_w_o_2, na_w_qkv_2, na_rpb_2, na_w_o_2,
        diff_w_qkv_2, diff_lambda_2, diff_norm_g_2, diff_w_o_2,
    )


_drawn_inputs = setup_inputs


def setup_inputs(seed=0):
    import zlib

    import numpy as np

    out = dict(_drawn_inputs(seed))
    spreads = {}
    factors = {'ssd_d': 5.875,
     'ssd_norm_w': 3.509,
     'cmp_k_pos': 8.0,
     'cmp_v_pos': 8.0,
     'ffn_norm_w': 3.17,
     'ffn_conv_b': 3.16,
     'final_norm_w': 2.776,
     'mod_b_2': 2.872,
     'norm_g_2': 8.0,
     'final_norm_g_2': 2.802,
     'mla_q_norm_2': 8.0,
     'mla_kv_norm_2': 8.0,
     'swa_sink_2': 8.0}
    for name, (base, spread) in spreads.items():
        noise = np.random.default_rng([zlib.crc32(name.encode()), seed]).standard_normal(out[name].shape)
        drawn = base * np.exp(spread * noise) if base else spread * noise
        out[name] = jnp.asarray(drawn.astype(out[name].dtype))
    for name, factor in factors.items():
        out[name] = (out[name] * factor).astype(out[name].dtype)
    return out
```

```python
from contextlib import ExitStack

import concourse.bass as bass
import numpy as np
from concourse import mybir

F32 = mybir.dt.float32
ALU = mybir.AluOpType
ACT = mybir.ActivationFunctionType
AXX = mybir.AxisListType.X

P = 128
DM = 1024
KD = DM // P
T = 256
EPS = 1e-6
NEG = -1e30
LAYERS = 2

HEADS, HDIM, GROUPS, STATE = 8, 64, 2, 128
INNER = HEADS * HDIM
XBC = INNER + 2 * GROUPS * STATE
SC = 256
FF1, FF1_TILES = 2752, 22
CMP_BLOCK, CMP_STRIDE, N_CMP = 32, 16, 15
TM = HEADS + 64 + 64 + 12
U_KCVC, U_KS, U_KW, U_Q, U_SCB, U_SCC, U_SCH, U_XBC, U_Z, U_TILES = 0, 1, 2, 3, 5, 7, 9, 11, 19, 23
PAD = 3
UW = PAD + T

FF2_TILES = 22
N_MOD = 9
MLA_HEADS, SWA_HEADS, SWA_KV = 8, 16, 4

RING = 4
PANEL = 3072
MODW = 384
MOD_PANELS = LAYERS * N_MOD * DM // MODW

STREAM = [("mod", MOD_PANELS, KD * MODW)]
for _l in range(LAYERS):
    STREAM += [(f"l{_l}_in0", 1, KD * (P + TM)), (f"l{_l}_in", 11, 2 * KD * P), (f"l{_l}_cmp", 2, 16 * P),
               (f"l{_l}_out", 4, 2 * KD * P), (f"l{_l}_up", FF1_TILES, 2 * KD * P), (f"l{_l}_down", KD, FF1_TILES * P)]
STREAM += [("m0_upa", FF2_TILES, 2 * KD * P), ("m0_downa", KD, FF2_TILES * P),
           ("mla_down", 4, 2 * KD * P), ("mla_pair", 4, 2560), ("mla_o", 4, 2 * KD * P),
           ("m0_upb", FF2_TILES, 2 * KD * P), ("m0_downb", KD, FF2_TILES * P),
           ("m1_upa", FF2_TILES, 2 * KD * P), ("m1_downa", KD, FF2_TILES * P),
           ("swa_qkv", 7, 2 * KD * P), ("swa_o", 4, 2 * KD * P),
           ("m1_upb", FF2_TILES, 2 * KD * P), ("m1_downb", KD, FF2_TILES * P)]
FIRST_PANEL, _at = {}, 0
for _name, _count, _ in STREAM:
    FIRST_PANEL[_name] = _at
    _at += _count


def table(widths):
    out, at = {}, 0
    for name, w in widths:
        out[name] = (at, w)
        at += w
    return out, at


PARAMS, PARAM_W = table(
    [(f"{n}{l}", w) for l in range(LAYERS) for n, w in (
        ("attn_norm", KD), ("ffn_norm", KD), ("conv_w", 32), ("conv_b", 8), ("dt_bias", HEADS), ("a_log", HEADS),
        ("d_skip", 4), ("ssd_norm", 4), ("sc_w", 6), ("pos", CMP_BLOCK), ("k_w2", P), ("v_w2", 64),
        ("ffn_conv", FF1_TILES * 8))]
    + [("final1", KD), ("cond", KD * 2), ("mod_norm", LAYERS * 3 * KD), ("mod_b", LAYERS * N_MOD * KD),
       ("final2", KD), ("q_norm", 4), ("kv_norm", 2), ("sink", SWA_HEADS)])
CONSTS, CONST_W = table([("ident", P), ("tri", 2 * T), ("rot", P), ("cos1", T), ("sin1", T), ("cos2", T), ("sin2", T),
                         ("causal", 2 * T), ("decay_mask", 384), ("cmp_add", 32), ("cmp_keep", 32),
                         ("window", 2 * T), ("head_pick", HEADS * P)])


class Tally:

    def __init__(self):
        self.at = {}

    def take(self, name, n):
        base = self.at.get(name, 0)
        self.at[name] = base + n
        return base


class Chain:

    def __init__(self, eng, sem):
        self.eng, self.sem, self.n, self.extra = eng, sem, 0, 0

    def __call__(self, ins):
        self.n += 1
        ins.then_inc(self.sem, 1)
        self.eng.wait_ge(self.sem, self.extra + self.n)


def turns(eng, count, unroll, body, chain=None, links=0, peel=0):
    full = count // unroll
    for n in range(peel * unroll):
        body(n, n % unroll, n // unroll)
    at = chain.n if chain else 0
    with eng.Fori(peel, full) as i:
        if chain:
            chain.extra = (i - peel) * (links * unroll) if peel else i * (links * unroll)
        for j in range(unroll):
            body(i * unroll + j, j, i)
    if chain:
        assert chain.n - at == links * unroll
        chain.n, chain.extra = at + links * unroll * (full - peel), 0
    for n in range(full * unroll, count):
        body(n, n % unroll, n // unroll)


def two_blocks(nc, xT, ctxT, params_d, consts_d, weights, out_d):
    ctx = ExitStack()
    with ctx:
        def sb(name, shape):
            return ctx.enter_context(nc.sbuf_tensor("sb_" + name, shape, F32))

        sems = {}

        def S(name):
            if name not in sems:
                sems[name] = ctx.enter_context(nc.semaphore(name))
            return sems[name]

        ring = [sb(f"ring{s}", [P, PANEL]) for s in range(RING)]
        res = sb("res", [P, KD, 2 * T])
        h = sb("h", [P, KD, 2 * T])
        mid = sb("mid", [P, 22 * 512])
        params = sb("params", [P, PARAM_W])
        consts = sb("consts", [P, CONST_W])
        modT = sb("modT", [P, LAYERS * N_MOD * KD, 2])
        cond = sb("cond", [P, KD * 2])
        mod_row = sb("mod_row", [2, 2, MODW])
        sq = sb("sq", [P, 2, 2 * T])
        eps = sb("eps", [P, 1])
        root_warm = sb("root_warm", [P, 1])
        rms_of = sb("rms_of", [P, 2 * T])
        rstd = sb("rstd", [P, 2 * T])
        inv = {n: sb(f"inv{n}", [P, P]) for n in (1024, 512, 256)}
        ucv = sb("ucv", [P, 2, 2, 2 + T])
        cva = sb("cva", [P, 2, T])
        sil = sb("sil", [P, 2, 2 * T])
        sbS = sb("sbS", [P, 2, 512])
        sbP = sb("sbP", [P, 2, 512])
        sbPT = sb("sbPT", [P, 2, 512])
        sbPC = sb("sbPC", [P, 2, 16])
        sbPCT = sb("sbPCT", [16, 2, P])
        stat = sb("stat", [P, 2, 16])
        tm = sb("tm", [P, 2, TM])
        gate = sb("gate", [P, 2, 12])
        dtw = sb("dtw", [P, 8, 16])
        ea = sb("ea", [P, HEADS])
        acs = sb("acs", [P, 2, HEADS])
        acsT = sb("acsT", [HEADS, T])
        cbT = sb("cbT", [P, GROUPS, 384])
        tpos = sb("tpos", [P, CMP_BLOCK, N_CMP])
        hid = sb("hid", [P, 2, N_CMP])
        kc = sb("kc", [P, N_CMP])
        vc = sb("vc", [N_CMP, 64])
        ropet = sb("ropet", [P, 2, 2 * T])
        bank = [ctx.enter_context(nc.psum_tensor(f"bank{b}", [P, 512], F32)) for b in range(8)]

        def par(name, a=0, b=None):
            at, w = PARAMS[name]
            return params[:, at + a:at + (w if b is None else b)]

        def con(name, a=0, b=None):
            at, w = CONSTS[name]
            return consts[:, at + a:at + (w if b is None else b)]

        def region(at, *shape):
            n = int(np.prod(shape))
            v = mid[:, at:at + n]
            return (v.rearrange("p (a b) -> p a b", a=shape[0]) if len(shape) == 2 else v), at + n

        ident = con("ident")
        ff = mid[:, :].rearrange("p (n t) -> p n t", n=22)
        U, at = region(0, U_TILES, UW)
        xc, at = region(at, 8, T)
        xdt, at = region(at, 2, INNER)
        yss, at = region(at, 4, T)
        krq, at = region(at, 4, T)
        dpj, at = region(0, 7, 512)
        pairs = []
        for _ in range(2):
            qn, at = region(at, 2, 512)
            qr, at = region(at, 512)
            qrot, at = region(at, T)
            kn, at = region(at, 2, 512)
            vv, at = region(at, 4, T)
            pairs.append((qn, qr, qrot, kn, vv))
        sq_q, at = region(0, 8, T)
        sq_qrot, at = region(at, 8, T)
        sq_k, at = region(at, SWA_KV, 512)
        sq_v, at = region(at, 4, T)
        kvr = sb("kvr", [P, T])
        yT = h[:, :, 0:T]

        def mod(l, c, k, s):
            q = (l * N_MOD + c) * KD + k
            return modT[:, q, s:s + 1]

        def streams(n):
            return [(s, s * T) for s in range(n // T)]

        block = ctx.enter_context(nc.Block())

        @block.sync
        def _(sp):
            sp.dma_start(params[:, :], params_d).then_inc(S("params_in"), 16)
            sp.dma_start(consts[:, :], consts_d).then_inc(S("consts_in"), 16)
            sp.dma_start(res[:, :, 0:T], xT).then_inc(S("x_in"), 16)
            sp.dma_start(res[:, :, T:2 * T], ctxT).then_inc(S("ctx_in"), 16)
            sp.sem_inc(S("panels_used"), RING)
            for name, count, width in STREAM:
                g0 = FIRST_PANEL[name]

                def load(n, j, i):
                    sp.wait_ge(S("panels_used"), n + (g0 + 1))
                    slot = (g0 + j) % RING
                    sp.dma_start(ring[slot][:, 0:width], weights[name][n]).then_inc(S(f"landed{slot}"), 16)

                if count >= 2 * RING:
                    turns(sp, count, RING, load)
                else:
                    for n in range(count):
                        load(n, n % RING, n // RING)
            sp.wait_ge(S("final_out"), KD)
            sp.dma_start(out_d, h[:, :, 0:T]).then_inc(S("stored"), 16)
            sp.wait_ge(S("stored"), 16)

        @block.gpsimd
        def _(pool):
            for n in inv:
                nc.gpsimd.memset(inv[n][:, :], 1.0 / n).then_inc(S("fills"), 1)
            nc.gpsimd.memset(eps[:, :], EPS).then_inc(S("fills"), 1)
            nc.gpsimd.memset(ucv[:, :, :, 0:2], 0.0).then_inc(S("fills"), 1)

        @block.tensor
        def _(pe):
            tally = Tally()
            take = tally.take

            def mm(out, lhsT, rhs, start, stop):
                return nc.tensor.matmul(out, lhsT, rhs, start=start, stop=stop, skip_group_check=True)

            def panel(name, n, j, i):
                g = FIRST_PANEL[name] + j
                pe.wait_ge(S(f"landed{g % RING}"), i * 16 + (g // RING + 1) * 16)
                return ring[g % RING]

            def panel_at(name, n):
                return panel(name, n, n % RING, n // RING)

            def norm(K, N, const):
                b = take("norm_sq", K)
                c = take("rms_done", 1)
                if c:
                    pe.wait_ge(S("rms_done"), c)
                for k in range(K):
                    pe.wait_ge(S("norm_sq"), b + k + 1)
                    last = mm(bank[7][:, 0:N], inv[const][:, :], sq[:, k % 2, 0:N], k == 0, k == K - 1)
                    last.then_inc(S("norm_sum"), 1)

            pe.wait_ge(S("cond_ready"), 1)
            pe.wait_ge(S("consts_in"), 16)

            def mod_cols(n, j):
                pe.wait_ge(S("mod_row"), n + 1)
                pe.wait_ge(S("mod_vec"), n + 1)
                for t in range(3):
                    last = mm(bank[2 + j % 2][:, 2 * t:2 * t + 2], mod_row[0:2, j % 2, t * P:(t + 1) * P],
                              ident[0:2, 0:2], True, True)
                last.then_inc(S("mod_cols"), 1)

            pe.sem_inc(S("mod_vec"), 2)

            def mod_panel(n, j, i):
                w = panel("mod", n, j, i)
                if not (isinstance(n, int) and n < 2):
                    pe.wait_ge(S("mod_row"), n - 1)
                for k in range(KD):
                    last = mm(bank[j % 2][0:2, 0:MODW], cond[:, 2 * k:2 * k + 2], w[:, k * MODW:(k + 1) * MODW],
                              k == 0, k == KD - 1)
                last.then_inc(S("panels_used"), 1)
                if not (isinstance(n, int) and n == 0):
                    mod_cols(n - 1, (j - 1) % RING)

            turns(pe, MOD_PANELS, RING, mod_panel, peel=1)
            mod_cols(MOD_PANELS - 1, (MOD_PANELS - 1) % 2)

            def project(name, N, K=KD):
                b = take("res_done", KD)
                for n in range(KD // 2):
                    w = panel_at(name, n)
                    for t in range(2):
                        m = 2 * n + t
                        if m >= 2:
                            pe.wait_ge(S("res_done"), b + m - 1)
                        for k in range(K):
                            last = mm(bank[4 + t][:, 0:N], w[:, (t * K + k) * P:(t * K + k + 1) * P],
                                      h[:, k, 0:N], k == 0, k == K - 1)
                        last.then_inc(S("panels_used" if t else "half_panel"), 1)

            def down(name, N):
                b = take("res_done", KD)
                for_first = b

                def tile(n, j, i):
                    w = panel(name, n, j, i)
                    if not (isinstance(n, int) and n < 2):
                        pe.wait_ge(S("res_done"), n + (for_first - 1))
                    for k in range(22):
                        last = mm(bank[4 + j % 2][:, 0:N], w[:, k * P:(k + 1) * P], ff[:, k, 0:N], k == 0, k == 21)
                    last.then_inc(S("panels_used"), 1)

                turns(pe, KD, RING, tile, peel=1)

            def ffn1(name):
                b = take("up_evac", FF1_TILES)
                hb = take("norm_h", KD)
                pe.wait_ge(S("norm_h"), hb + KD)

                def tile(n, j, i):
                    w = panel(name + "_up", n, j, i)
                    if not (isinstance(n, int) and n < 2):
                        pe.wait_ge(S("up_evac"), n + (b - 1))
                    for half in range(2):
                        for k in range(KD):
                            last = mm(bank[j % 2][:, half * T:(half + 1) * T],
                                      w[:, (half * KD + k) * P:(half * KD + k + 1) * P], h[:, k, 0:T],
                                      k == 0, k == KD - 1)
                    last.then_inc(S("panels_used"), 1)

                turns(pe, FF1_TILES, RING, tile, peel=1)
                m = take("ff_mid", FF1_TILES)
                pe.wait_ge(S("ff_mid"), m + FF1_TILES)
                down(name + "_down", T)

            def ffn2(up, dn, N):
                hb = take("norm_shifted", KD * (N // T))
                pe.wait_ge(S("norm_shifted"), hb + KD * (N // T))
                m = take("ff_mid", FF2_TILES)

                def tile(n, j, i):
                    w = panel(up, n, j, i)
                    if not (isinstance(n, int) and n < 2):
                        pe.wait_ge(S("ff_mid"), n + (m - 1))
                    for half in range(2):
                        for k in range(KD):
                            last = mm(bank[2 * (j % 2) + half][:, 0:N],
                                      w[:, (half * KD + k) * P:(half * KD + k + 1) * P], h[:, k, 0:N],
                                      k == 0, k == KD - 1)
                    last.then_inc(S("panels_used"), 1)

                turns(pe, FF2_TILES, RING, tile, peel=1)
                pe.wait_ge(S("ff_mid"), m + FF2_TILES)
                down(dn, N)

            def attention(units, scores, flips, products, shared=False):
                b = take("att_scores", units)

                def ahead(u):
                    if u >= 2:
                        pe.wait_ge(S("att_exp"), b + u - 1)
                    if u >= 2 and shared:
                        pe.wait_ge(S("att_turned"), b + u - 1)
                    scores(u).then_inc(S("att_scores"), 1)

                def turn(u):
                    pe.wait_ge(S("att_probs"), b + u + 1)
                    if u >= 2:
                        pe.wait_ge(S("att_turned"), b + u - 1)
                    flips(u).then_inc(S("att_flips"), 1)

                def product(u):
                    pe.wait_ge(S("att_turned"), b + u + 1)
                    if u >= 2:
                        pe.wait_ge(S("att_out"), b + u - 1)
                    products(u).then_inc(S("att_prod"), 1)

                return ahead, turn, product

            def mixers(l):
                L = f"l{l}"
                norm(KD, T, 1024)
                hb = take("norm_h", KD)
                pe.wait_ge(S("norm_h"), hb + KD)
                w = panel_at(L + "_in0", 0)
                for k in range(KD):
                    mm(bank[6][:, 0:T], w[:, k * P:(k + 1) * P], h[:, k, 0:T], k == 0, k == KD - 1)
                wt = w[:, KD * P:KD * (P + TM)].rearrange("p (k c) -> p k c", k=KD)
                for tb in range(2):
                    for k in range(KD):
                        last = mm(bank[2 + tb][:, 0:TM], h[:, k, tb * P:(tb + 1) * P], wt[:, k, :],
                                  k == 0, k == KD - 1)
                last.then_inc(S("panels_used"), 1)
                e = take("in_evac", 13)

                def pair(n, j, i):
                    wp = panel(L + "_in", n, j, i)
                    if not (isinstance(n, int) and n < 2):
                        pe.wait_ge(S("in_evac"), n + (e + 1))
                    for t in range(2):
                        for k in range(KD):
                            last = mm(bank[j % 2][:, t * T:(t + 1) * T], wp[:, (t * KD + k) * P:(t * KD + k + 1) * P],
                                      h[:, k, 0:T], k == 0, k == KD - 1)
                    last.then_inc(S("panels_used"), 1)

                turns(pe, 11, RING, pair, peel=1)
                pe.wait_ge(S("in_evac"), e + 4)
                for t in range(5):
                    last = mm(bank[[2, 2, 3, 3, 4][t]][:, (t % 2) * T:(t % 2 + 1) * T], con("rot"),
                              U[:, t, PAD:UW], True, True)
                last.then_inc(S("rotated"), 1)
                a = dtw[:, 7, :].rearrange("p (b h) -> p b h", b=2)
                d = take("dt_ready", 1)
                pe.wait_ge(S("dt_ready"), d + 1)
                tri = con("tri").rearrange("p (b t) -> p b t", b=2)
                mm(bank[5][:, 0:HEADS], tri[:, 0, 0:P], a[:, 0, :], True, True)
                mm(bank[5][:, 8:16], tri[:, 0, P:T], a[:, 0, :], True, False)
                mm(bank[5][:, 8:16], tri[:, 1, P:T], a[:, 1, :], False, True)
                mm(bank[5][0:HEADS, T:2 * T], a[:, 0, :], tri[:, 0, :], True, False)
                mm(bank[5][0:HEADS, T:2 * T], a[:, 1, :], tri[:, 1, :], False, True).then_inc(S("cumulated"), 1)
                tk = take("tpos_ready", 1)
                pe.wait_ge(S("tpos_ready"), tk + 1)
                for c in range(2):
                    w = panel_at(L + "_cmp", c)
                    for r in range(2):
                        rows = slice(64 * r, 64 * r + 64)
                        for jj in range(16):
                            j = 16 * c + jj
                            last = mm(bank[6 + r][:, 0:N_CMP], w[rows, jj * P:(jj + 1) * P], tpos[rows, j, :],
                                      j == 0, j == CMP_BLOCK - 1)
                    last.then_inc(S("panels_used"), 1)
                hd = take("hid_ready", 2)
                pe.wait_ge(S("hid_ready"), hd + 2)
                mm(bank[6][:, 0:N_CMP], par(f"k_w2{l}"), hid[:, 0, :], True, True)
                mm(bank[6][0:N_CMP, 64:128], hid[:, 1, :], par(f"v_w2{l}"), True, True).then_inc(S("cmp_kv"), 1)
                x = take("xbc_ready", 8)
                pe.wait_ge(S("xbc_ready"), x + 8)
                for tb in range(2):
                    for t in range(4):
                        last = nc.tensor.transpose(bank[2 + tb][:, t * P:(t + 1) * P], xc[:, t, tb * P:(tb + 1) * P],
                                                   ident)
                last.then_inc(S("x_turned"), 1)
                for g in range(GROUPS):
                    B, C = xc[:, 4 + g, :], xc[:, 6 + g, :]
                    mm(bank[g][:, 0:T], B[:, 0:P], C, True, True)
                    last = mm(bank[g][:, T:384], B[:, P:T], C[:, P:T], True, True)
                last.then_inc(S("cb_ready"), 1)
                s = take("ssm_start", 1)
                pe.wait_ge(S("ssm_start"), s + 1)

                def where(u):
                    hh, b = u // 2, u % 2
                    return slice(64 * (hh % 2), 64 * (hh % 2) + 64), hh, b

                def scores(u):
                    rows, hh, b = where(u)
                    q = krq[rows, 2 + hh // 2, b * P:(b + 1) * P]
                    mm(bank[2 + u % 2][:, 0:N_CMP], q, kc[rows, :], True, True)
                    mm(bank[u % 2][:, 0:T], q, krq[rows, 0, :], True, True)
                    return mm(bank[u % 2][:, T:2 * T], q, krq[rows, 1, :], True, True)

                def flips(u):
                    nc.tensor.transpose(bank[2 + u % 2][0:N_CMP, P:2 * P], sbPC[:, u % 2, 0:N_CMP], ident)
                    for c in range(4):
                        last = nc.tensor.transpose(bank[4 + u % 2][:, c * P:(c + 1) * P],
                                                   sbP[:, u % 2, c * P:(c + 1) * P], ident)
                    return last

                def products(u):
                    rows, hh, b = where(u)
                    o = bank[6 + u % 2][rows, 0:P]
                    mm(o, vc[:, :], sbPCT[0:N_CMP, u % 2, :], True, False)
                    for c in range(4):
                        v = tm[:, c % 2, 8 + 64 * (c // 2):72 + 64 * (c // 2)]
                        last = mm(o, v, sbPT[:, u % 2, c * P:(c + 1) * P], False, c == 3)
                    return last

                ahead, turn, product = attention(8, scores, flips, products, shared=True)
                ahead(0)
                for u in range(9):
                    if u < 7:
                        ahead(u + 1)
                    if u < 8:
                        turn(u)
                    if u >= 1:
                        product(u - 1)
                y = take("ssd_y", HEADS)
                yo = take("ssd_out", 4)
                at_start = take("att_out", 8)
                pe.wait_ge(S("att_out"), at_start + 8)

                def spread(hh):
                    if hh >= 2:
                        pe.wait_ge(S("ssd_diff"), y + hh - 1)
                    mm(bank[hh % 2][:, 0:T], con("head_pick", hh * P, (hh + 1) * P)[0:HEADS, :], acsT[:, :],
                       True, True).then_inc(S("ssd_spread"), 1)

                spread(0)
                spread(1)
                for hh in range(HEADS):
                    pe.wait_ge(S("ssd_mat"), y + hh + 1)
                    t = hh // 2
                    rows = slice(64 * (hh % 2), 64 * (hh % 2) + 64)
                    o = bank[2 + t % 2]
                    if hh % 2 == 0 and t >= 2:
                        pe.wait_ge(S("ssd_out"), yo + t - 1)
                    mm(o[rows, 0:T], xdt[:, 0, hh * 64:(hh + 1) * 64], sbP[:, hh % 2, 0:T], True, False)
                    mm(o[rows, P:T], xdt[:, 1, hh * 64:(hh + 1) * 64], sbP[:, hh % 2, T:384], False,
                       True).then_inc(S("ssd_y"), 1)
                    if hh + 2 < HEADS:
                        spread(hh + 2)
                norm(4, T, 512)
                m = take("mixed", 6)
                pe.wait_ge(S("mixed"), m + 6)
                project(L + "_out", T)

            pe.wait_ge(S("fills"), 5)
            for l in range(LAYERS):
                mixers(l)
                norm(KD, T, 1024)
                ffn1(f"l{l}")
            norm(KD, T, 1024)
            norm(KD, 2 * T, 1024)
            ffn2("m0_upa", "m0_downa", 2 * T)
            norm(KD, 2 * T, 1024)
            hb = take("norm_shifted", 2 * KD)
            pe.wait_ge(S("norm_shifted"), hb + 2 * KD)
            d = take("lat_evac", 4)
            for n in range(4):
                w = panel_at("mla_down", n)
                if n >= 2:
                    pe.wait_ge(S("lat_evac"), d + n - 1)
                for t in range(2 if n < 3 else 1):
                    for k in range(KD):
                        last = mm(bank[2 * (n % 2) + t][:, :], w[:, (t * KD + k) * P:(t * KD + k + 1) * P], h[:, k, :],
                                  k == 0, k == KD - 1)
                last.then_inc(S("panels_used"), 1)
            pe.wait_ge(S("lat_evac"), d + 4)
            mm(bank[4][:, 0:T], con("rot"), dpj[:, 6, 0:T], True, True).then_inc(S("rotated"), 1)
            norm(4, 2 * T, 512)
            norm(2, 2 * T, 256)
            pe.wait_ge(S("lat_normed"), 6)

            def pair_tiles(p):
                w = panel_at("mla_pair", p)
                qn, qr, qrot, kn, vv = pairs[p % 2]

                def free(t):
                    if t >= 2:
                        pe.wait_ge(S("pair_evac"), 7 * p + t - 1)
                    elif p:
                        pe.wait_ge(S("pair_evac"), 7 * p)
                        if t == 1:
                            pe.wait_ge(S("pair_rope"), p)

                for t in range(5):
                    free(t)
                    K, at0, src = (4, t * 512, 0) if t < 3 else (2, 1536 + (t - 3) * 256, 4)
                    for k in range(K):
                        last = mm(bank[2 + t % 2][:, :], w[:, at0 + k * P:at0 + (k + 1) * P], dpj[:, src + k, :],
                                  k == 0, k == K - 1)
                    last.then_inc(S("pair_tile"), 1)
                for t in range(5, 7):
                    free(t)
                    for tb in range(2):
                        b4 = 2 * (t - 5) + tb
                        for k in range(2):
                            last = mm(bank[2 + t % 2][:, tb * T:(tb + 1) * T], dpj[:, 4 + k, b4 * P:(b4 + 1) * P],
                                      w[:, 2048 + k * T:2048 + (k + 1) * T], k == 0, k == 1)
                    last.then_inc(S("pair_tile" if t == 5 else "panels_used"), 1)

            def pair_rot(p):
                qn, qr, qrot, kn, vv = pairs[p % 2]
                pe.wait_ge(S("pair_evac"), 7 * p + 6)
                mm(bank[3][:, 0:T], con("rot"), qr[:, 0:T], True, True).then_inc(S("pair_rot"), 1)

            def mla_scores(u):
                p, hh, b = u // 8, u // 4 % 2, u % 4
                qn, qr, qrot, kn, vv = pairs[p % 2]
                rows, q = slice(64 * hh, 64 * hh + 64), slice(b * P, (b + 1) * P)
                if u % 8 == 0:
                    pe.wait_ge(S("pair_rope"), p + 1)
                    pe.wait_ge(S("pair_evac"), 7 * p + 7)
                A = bank[u % 2]
                if b < 2:
                    mm(A[:, :], qn[:, hh, q], kn[:, hh, :], True, False)
                    mm(A[:, 0:T], qrot[rows, q], dpj[rows, 6, 0:T], False, False)
                    return mm(A[:, T:2 * T], qr[rows, q], dpj[rows, 6, T:2 * T], False, True)
                mm(A[:, 0:T], qn[:, hh, q], kn[:, hh, T:2 * T], True, False)
                return mm(A[:, 0:T], qr[rows, q], dpj[rows, 6, T:2 * T], False, True)

            def mla_flips(u):
                for c in range(4 if u % 4 < 2 else 2):
                    last = nc.tensor.transpose(bank[4 + u % 2][:, c * P:(c + 1) * P],
                                               sbP[:, u % 2, c * P:(c + 1) * P], ident)
                return last

            def mla_products(u):
                p, hh, b = u // 8, u // 4 % 2, u % 4
                qn, qr, qrot, kn, vv = pairs[p % 2]
                nk = 4 if b < 2 else 2
                for c in range(nk):
                    last = mm(bank[6 + u % 2][:, 0:P], vv[:, c + 4 - nk, hh * P:(hh + 1) * P],
                              sbPT[:, u % 2, c * P:(c + 1) * P], c == 0, c == nk - 1)
                return last

            kr = take("key_rope", 1)
            pe.wait_ge(S("key_rope"), kr + 1)
            pair_tiles(0)
            pair_rot(0)
            ahead, turn, product = attention(32, mla_scores, mla_flips, mla_products)
            ahead(0)
            for u in range(33):
                if u % 8 == 1 and u // 8 < 3:
                    pair_tiles(u // 8 + 1)
                if u % 8 == 3 and u // 8 < 3:
                    pair_rot(u // 8 + 1)
                if u < 31:
                    ahead(u + 1)
                if u < 32:
                    turn(u)
                if u >= 1:
                    product(u - 1)
            o = take("att_out", 32)
            pe.wait_ge(S("att_out"), o + 32)
            project("mla_o", 2 * T)
            norm(KD, 2 * T, 1024)
            ffn2("m0_upb", "m0_downb", 2 * T)
            norm(KD, 2 * T, 1024)
            ffn2("m1_upa", "m1_downa", 2 * T)
            norm(KD, 2 * T, 1024)
            hb = take("norm_shifted", 2 * KD)
            pe.wait_ge(S("norm_shifted"), hb + 2 * KD)
            for n in range(7):
                w = panel_at("swa_qkv", n)
                if 2 <= n <= 4:
                    pe.wait_ge(S("swa_evac"), min(n - 1 + n // 4, 4))
                for t in range(2):
                    if n < 4:
                        for k in range(KD):
                            last = mm(bank[n % 2][:, t * T:(t + 1) * T], w[:, (t * KD + k) * P:(t * KD + k + 1) * P],
                                      h[:, k, 0:T], k == 0, k == KD - 1)
                    elif n < 6:
                        for k in range(KD):
                            last = mm(bank[2 * (n % 2) + t][:, :], w[:, (t * KD + k) * P:(t * KD + k + 1) * P],
                                      h[:, k, :], k == 0, k == KD - 1)
                    else:
                        for tb in range(2):
                            c = 2 * t + tb
                            for k in range(KD):
                                last = mm(bank[4 + t][:, tb * T:(tb + 1) * T], h[:, k, c * P:(c + 1) * P],
                                          w[:, k * T:(k + 1) * T], k == 0, k == KD - 1)
                last.then_inc(S("panels_used"), 1)
            for g in range(6):
                b = 6 + g % 2
                if g >= 2:
                    pe.wait_ge(S("swa_rope"), g - 1)
                for t in range(2):
                    src = sq_q[:, 2 * g + t, :] if g < 4 else sq_k[:, 2 * (g - 4) + t, 0:T]
                    pe.wait_ge(S("swa_evac"), g + 1)
                    last = mm(bank[b][:, t * T:(t + 1) * T], con("rot"), src, True, True)
                last.then_inc(S("swa_rot"), 1)
            pe.wait_ge(S("swa_evac"), 7)
            pe.wait_ge(S("swa_rope"), 6)

            def swa_scores(u):
                hh, b = u // 2, u % 2
                rows, q = slice(64 * (hh % 2), 64 * (hh % 2) + 64), slice(b * P, (b + 1) * P)
                A = bank[u % 2]
                mm(A[:, 0:T], sq_qrot[rows, hh // 2, q], sq_k[rows, hh // 4, 0:T], True, True)
                return mm(A[:, T:2 * T], sq_q[rows, hh // 2, q], sq_k[rows, hh // 4, T:2 * T], True, True)

            def swa_flips(u):
                for c in range(4):
                    last = nc.tensor.transpose(bank[4 + u % 2][:, c * P:(c + 1) * P],
                                               sbP[:, u % 2, c * P:(c + 1) * P], ident)
                return last

            def swa_products(u):
                hh, b = u // 2, u % 2
                rows = slice(64 * (hh % 2), 64 * (hh % 2) + 64)
                for c in range(4):
                    last = mm(bank[6 + u % 2][rows, 0:P], sq_v[:, c, (hh // 4) * 64:(hh // 4 + 1) * 64],
                              sbPT[:, u % 2, c * P:(c + 1) * P], c == 0, c == 3)
                return last

            ahead, turn, product = attention(32, swa_scores, swa_flips, swa_products)
            ahead(0)
            for u in range(33):
                if u < 31:
                    ahead(u + 1)
                if u < 32:
                    turn(u)
                if u >= 1:
                    product(u - 1)
            o = take("att_out", 32)
            pe.wait_ge(S("att_out"), o + 32)
            project("swa_o", T)
            norm(KD, T, 1024)
            ffn2("m1_upb", "m1_downb", T)
            norm(KD, T, 1024)

        @block.scalar
        def _(act):
            take = Tally().take
            panels = FIRST_PANEL

            def run(out, in_, func, **kw):
                return nc.scalar.activation(out, in_, func, **kw)

            def panel_done(name, n):
                act.wait_ge(S("panels_used"), n + (panels[name] + RING + 1))

            def squares(K, src, N, ready=None):
                b = take("norm_sum", K)
                run(root_warm[:, :], eps[:, :], ACT.Sqrt)
                for k in range(K):
                    if ready:
                        ready(k)
                    if b + k >= 2:
                        act.wait_ge(S("norm_sum"), b + k - 1)
                    run(sq[:, k % 2, 0:N], src(k), ACT.Square).then_inc(S("norm_sq"), 1)
                act.wait_ge(S("norm_sum"), b + K)
                c = take("rms_done", 1)
                if c:
                    act.wait_ge(S("rstd_ready"), c)
                run(rms_of[:, 0:N], bank[7][:, 0:N], ACT.Sqrt, bias=eps[:, :]).then_inc(S("rms_done"), 1)

            def res_tile(N):
                b = take("res_done", KD)
                return lambda k: act.wait_ge(S("res_done"), b + k + 1)

            def res_norm(N, ready):
                squares(KD, lambda k: res[:, k, 0:N], N, ready)

            def shifts(l, c, N):
                b = take("norm_scaled", KD * (N // T))
                n = 0
                for k in range(KD):
                    for s, at in streams(N):
                        n += 1
                        act.wait_ge(S("norm_scaled"), b + n)
                        run(h[:, k, at:at + T], h[:, k, at:at + T], ACT.Identity,
                            bias=mod(l, c, k, s)).then_inc(S("norm_shifted"), 1)

            def ffn1(name):
                b = take("ff_mid", FF1_TILES)
                g = take("gate_ready", FF1_TILES)
                u = take("up_evac", FF1_TILES)

                def tile(n, j, i):
                    panel_done(name + "_up", n)
                    if not (isinstance(n, int) and n < 2):
                        act.wait_ge(S("ff_mid"), n + (b - 1))
                    run(ucv[:, j % 2, :, 2:2 + T], bank[j % 2][:, :].rearrange("p (a t) -> p a t", a=2),
                        ACT.Copy).then_inc(S("up_evac"), 1)
                    act.wait_ge(S("gate_ready"), n + (g + 1))
                    run(sil[:, j % 2, 0:T], cva[:, 0, :], ACT.Silu).then_inc(S("gate_act"), 1)

                turns(act, FF1_TILES, 2, tile, peel=1)

            def ffn2(name, N):
                b = take("ff_mid", FF2_TILES)

                def tile(n, j, i):
                    panel_done(name, n)
                    if not (isinstance(n, int) and n < 2):
                        act.wait_ge(S("ff_mid"), n + (b - 1))
                    run(sil[:, j % 2, 0:N], bank[2 * (j % 2)][:, 0:N], ACT.Silu).then_inc(S("gate_act"), 1)

                turns(act, FF2_TILES, 2, tile, peel=1)

            def mixers(l, ready):
                L = f"l{l}"
                res_norm(T, ready)
                panel_done(L + "_in0", 0)
                run(U[:, U_KCVC, PAD:UW], bank[6][:, 0:T], ACT.Copy).then_inc(S("in_evac"), 1)
                for tb in range(2):
                    last = run(tm[:, tb, :], bank[2 + tb][:, 0:TM], ACT.Copy)
                last.then_inc(S("in_evac"), 1)

                def pair(n, j, i):
                    panel_done(L + "_in", n)
                    run(U[:, bass.ds(n * 2 + 1, 2), PAD:UW], bank[j % 2][:, :].rearrange("p (a t) -> p a t", a=2),
                        ACT.Copy).then_inc(S("in_evac"), 1)

                e = take("in_evac", 13)
                turns(act, 11, 2, pair)
                act.wait_ge(S("in_evac"), e + 13)
                x = take("dt_raw", 1)
                act.wait_ge(S("dt_raw"), x + 1)
                run(dtw[:, 1, :], dtw[:, 0, :], ACT.Exp, scale=-1.0).then_inc(S("dt_exp"), 1)
                run(gate[:, :, :], tm[:, :, 136:148], ACT.Exp, scale=-1.0).then_inc(S("dt_exp"), 1)
                run(ea[:, :], par(f"a_log{l}"), ACT.Exp).then_inc(S("dt_exp"), 1)
                x = take("xbc_conv", 8)
                for t in range(8):
                    act.wait_ge(S("xbc_conv"), x + t + 1)
                    run(xc[:, t, :], xc[:, t, :], ACT.Silu).then_inc(S("xbc_ready"), 1)
                run(U[:, U_Z:U_Z + 4, PAD:UW], U[:, U_Z:U_Z + 4, PAD:UW], ACT.Silu).then_inc(S("z_ready"), 1)
                panel_done(L + "_cmp", 1)
                for r in range(2):
                    run(hid[:, r, :], bank[6 + r][:, 0:N_CMP], ACT.Gelu_apprx_tanh).then_inc(S("hid_ready"), 1)
                b = take("att", 8)

                def exps(u):
                    act.wait_ge(S("att_max"), b + u + 1)
                    if u >= 2:
                        act.wait_ge(S("att_flips"), b + u - 1)
                    for r in range(2):
                        run(sbP[:, u % 2, r * T:(r + 1) * T], sbS[:, u % 2, r * T:(r + 1) * T], ACT.Exp,
                            bias=stat[:, u % 2, 3 + r:4 + r], scale=0.125, accum_out=stat[:, u % 2, 6 + r:7 + r])
                    run(sbPC[:, u % 2, 0:N_CMP], sbPC[:, u % 2, 0:N_CMP], ACT.Exp,
                        bias=stat[:, u % 2, 5:6], scale=0.125).then_inc(S("att_exp"), 1)

                def copies(u):
                    act.wait_ge(S("att_flips"), b + u + 1)
                    if u >= 2:
                        act.wait_ge(S("att_prod"), b + u - 1)
                    run(sbPCT[0:N_CMP, u % 2, :], bank[2 + u % 2][0:N_CMP, P:2 * P], ACT.Copy)
                    run(sbPT[:, u % 2, :], bank[4 + u % 2][:, :], ACT.Copy).then_inc(S("att_turned"), 1)

                exps(0)
                for u in range(8):
                    if u < 7:
                        exps(u + 1)
                    copies(u)
                y = take("ssd", HEADS)
                for hh in range(HEADS):
                    act.wait_ge(S("ssd_diff"), y + hh + 1)
                    if hh >= 2:
                        act.wait_ge(S("ssd_y"), y + hh - 1)
                    run(sbP[:, hh % 2, 0:384], sbS[:, hh % 2, 0:384], ACT.Exp).then_inc(S("ssd_exp"), 1)
                o = take("ssd_out", 4)
                squares(4, lambda k: yss[:, k, :], T, lambda k: act.wait_ge(S("ssd_out"), o + k + 1))

            act.wait_ge(S("fills"), 5)
            act.wait_ge(S("params_in"), 16)
            run(cond[:, :], par("cond"), ACT.Silu).then_inc(S("cond_ready"), 1)

            def mod_row_copy(n, j, i):
                panel_done("mod", n)
                if not (isinstance(n, int) and n < 2):
                    act.wait_ge(S("mod_cols"), n - 1)
                run(mod_row[0:2, j % 2, :], bank[j % 2][0:2, 0:MODW], ACT.Copy).then_inc(S("mod_row"), 1)

            turns(act, MOD_PANELS, 2, mod_row_copy, peel=1)
            act.wait_ge(S("x_in"), 16)
            ready = None
            for l in range(LAYERS):
                mixers(l, ready)
                res_norm(T, res_tile(T))
                ffn1(f"l{l}")
                ready = res_tile(T)
            res_norm(T, ready)
            act.wait_ge(S("ctx_in"), 16)
            fb = take("final1", KD)
            res_norm(2 * T, lambda k: act.wait_ge(S("final1"), fb + k + 1))
            shifts(0, 0, 2 * T)
            ffn2("m0_upa", 2 * T)
            res_norm(2 * T, res_tile(2 * T))
            shifts(0, 3, 2 * T)
            for n in range(4):
                panel_done("mla_down", n)
                for t in range(2 if n < 3 else 1):
                    last = run(dpj[:, 2 * n + t, :], bank[2 * (n % 2) + t][:, :], ACT.Copy)
                last.then_inc(S("lat_evac"), 1)
            act.wait_ge(S("lat_evac"), 4)
            squares(4, lambda k: dpj[:, k, :], 2 * T)
            squares(2, lambda k: dpj[:, 4 + k, :], 2 * T)

            def pair_evac(p):
                qn, qr, qrot, kn, vv = pairs[p % 2]
                dst = [qn[:, 0, :], qn[:, 1, :], qr, kn[:, 0, :], kn[:, 1, :], vv[:, 0:2, :], vv[:, 2:4, :]]
                for t in range(7):
                    if t < 6:
                        act.wait_ge(S("pair_tile"), 6 * p + t + 1)
                    else:
                        panel_done("mla_pair", p)
                    src = bank[2 + t % 2][:, :]
                    if t >= 5:
                        src = src.rearrange("p (a t) -> p a t", a=2)
                    run(dst[t], src, ACT.Copy).then_inc(S("pair_evac"), 1)

            def attention(b, units, width, scores_at, scale, between=None):
                def exps(u):
                    act.wait_ge(S("att_max"), b + u + 1)
                    if u >= 2:
                        act.wait_ge(S("att_flips"), b + u - 1)
                    W = width(u)
                    run(sbP[:, u % 2, 0:W], scores_at(u)[:, 0:W], ACT.Exp, bias=stat[:, u % 2, 1:2], scale=scale,
                        accum_out=stat[:, u % 2, 2:3]).then_inc(S("att_exp"), 1)

                def copies(u):
                    act.wait_ge(S("att_flips"), b + u + 1)
                    if u >= 2:
                        act.wait_ge(S("att_prod"), b + u - 1)
                    W = width(u)
                    run(sbPT[:, u % 2, 0:W], bank[4 + u % 2][:, 0:W], ACT.Copy).then_inc(S("att_turned"), 1)

                exps(0)
                for u in range(units):
                    if between:
                        between(u)
                    if u < units - 1:
                        exps(u + 1)
                    copies(u)

            pair_evac(0)
            attention(take("att", 32), 32, lambda u: 512 if u % 4 < 2 else 256, lambda u: bank[u % 2], 192 ** -0.5,
                      lambda u: pair_evac(u // 8 + 1) if u % 8 == 1 and u // 8 < 3 else None)
            res_norm(2 * T, res_tile(2 * T))
            shifts(0, 6, 2 * T)
            ffn2("m0_upb", 2 * T)
            res_norm(2 * T, res_tile(2 * T))
            shifts(1, 0, 2 * T)
            ffn2("m1_upa", 2 * T)
            res_norm(2 * T, res_tile(2 * T))
            shifts(1, 3, 2 * T)
            for n in range(7):
                panel_done("swa_qkv", n)
                if n < 4:
                    last = run(sq_q[:, 2 * n:2 * n + 2, :], bank[n % 2][:, :].rearrange("p (a t) -> p a t", a=2), ACT.Copy)
                elif n < 6:
                    for t in range(2):
                        last = run(sq_k[:, 2 * (n - 4) + t, :], bank[2 * (n % 2) + t][:, :], ACT.Copy)
                else:
                    for t in range(2):
                        last = run(sq_v[:, 2 * t:2 * t + 2, :], bank[4 + t][:, :].rearrange("p (a t) -> p a t", a=2),
                                   ACT.Copy)
                last.then_inc(S("swa_evac"), 1)
            b = take("att", 32)

            def swa_exps(u):
                act.wait_ge(S("att_max"), b + u + 1)
                if u >= 2:
                    act.wait_ge(S("att_flips"), b + u - 1)
                run(sbP[:, u % 2, :], sbS[:, u % 2, :], ACT.Exp, bias=stat[:, u % 2, 1:2], scale=0.125,
                    accum_out=stat[:, u % 2, 2:3])
                run(stat[:, u % 2, 3:4], par("sink", u // 2, u // 2 + 1), ACT.Exp,
                    bias=stat[:, u % 2, 1:2]).then_inc(S("att_exp"), 1)

            def swa_copies(u):
                act.wait_ge(S("att_flips"), b + u + 1)
                if u >= 2:
                    act.wait_ge(S("att_prod"), b + u - 1)
                run(sbPT[:, u % 2, :], bank[4 + u % 2][:, :], ACT.Copy).then_inc(S("att_turned"), 1)

            swa_exps(0)
            for u in range(32):
                if u < 31:
                    swa_exps(u + 1)
                swa_copies(u)
            res_norm(T, res_tile(T))
            shifts(1, 6, T)
            ffn2("m1_upb", T)
            res_norm(T, res_tile(T))

        @block.vector
        def _(dve):
            take = Tally().take
            link = Chain(dve, S("dve_step"))
            V = nc.vector

            def panel_done(name, n):
                dve.wait_ge(S("panels_used"), n + (FIRST_PANEL[name] + RING + 1))

            def rms(K, N):
                c = take("rms_done", 1)
                dve.wait_ge(S("rms_done"), c + 1)
                V.reciprocal(rstd[:, 0:N], rms_of[:, 0:N]).then_inc(S("rstd_ready"), 1)
                dve.wait_ge(S("rstd_ready"), c + 1)

            def normed(K, N, src, dst, gain, sem):
                rms(K, N)
                for k in range(K):
                    V.scalar_tensor_tensor(dst(k), src(k), gain(k), rstd[:, 0:N], ALU.mult,
                                           ALU.mult).then_inc(S(sem), 1)

            def norm_mod(l, c, N):
                rms(KD, N)
                for k in range(KD):
                    for s, at in streams(N):
                        V.scalar_tensor_tensor(h[:, k, at:at + T], res[:, k, at:at + T], mod(l, c + 1, k, s),
                                               rstd[:, at:at + T], ALU.mult, ALU.mult).then_inc(S("norm_scaled"), 1)

            def residual_plain(k, src):
                return V.tensor_tensor(res[:, k, 0:T], src, res[:, k, 0:T], ALU.add)

            def residual_mod(k, b, l, c, N):
                for s, at in streams(N):
                    last = V.scalar_tensor_tensor(res[:, k, at:at + T], bank[b][:, at:at + T], mod(l, c, k, s),
                                                  res[:, k, at:at + T], ALU.mult, ALU.add)
                return last

            def project(name, N, l=None, c=None):
                hp = take("half_panel", KD // 2)
                for k in range(KD):
                    if k % 2 == 0:
                        dve.wait_ge(S("half_panel"), hp + k // 2 + 1)
                    else:
                        panel_done(name, k // 2)
                    ins = residual_plain(k, bank[4 + k % 2][:, 0:N]) if c is None else residual_mod(k, 4 + k % 2, l, c, N)
                    ins.then_inc(S("res_done"), 1)

            def down(name, N, l=None, c=None):
                def tile(n, j, i):
                    panel_done(name, n)
                    b = 4 + j % 2
                    if c is None:
                        r = res[:, bass.ds(n, 1), 0:T]
                        V.tensor_tensor(r, bank[b][:, 0:T].unsqueeze(1), r, ALU.add).then_inc(S("res_done"), 1)
                        return
                    for s, at in streams(N):
                        r = res[:, bass.ds(n, 1), at:at + T]
                        g = modT[:, bass.ds(n + (l * N_MOD + c) * KD, 1), s]
                        last = V.scalar_tensor_tensor(r, bank[b][:, at:at + T].unsqueeze(1), g, r, ALU.mult, ALU.add)
                    last.then_inc(S("res_done"), 1)

                turns(dve, KD, 2, tile)

            def ffn1(l):
                name = f"l{l}"
                ub = take("up_evac", FF1_TILES)
                ga = take("gate_act", FF1_TILES)
                mb = take("ff_mid", FF1_TILES)
                w0 = PARAMS[f"ffn_conv{l}"][0]

                def tile(n, j, i):
                    dve.wait_ge(S("up_evac"), n + (ub + 1))
                    if not (isinstance(n, int) and n == 0):
                        dve.wait_ge(S("ff_mid"), n + mb)
                    for half in (1, 0):
                        u = ucv[:, j % 2, half, :]
                        c = cva[:, half, :]

                        def w(x):
                            return params[:, bass.ds(n * 8 + (w0 + 4 * half + x), 1)]

                        link(V.tensor_scalar(c, u[:, 2:2 + T], w(2), w(3), ALU.mult, ALU.add))
                        link(V.scalar_tensor_tensor(c, u[:, 1:1 + T], w(1), c, ALU.mult, ALU.add))
                        ins = V.scalar_tensor_tensor(c, u[:, 0:T], w(0), c, ALU.mult, ALU.add)
                        if half:
                            link(ins)
                        else:
                            ins.then_inc(S("gate_ready"), 1)
                    dve.wait_ge(S("gate_act"), n + (ga + 1))
                    V.tensor_tensor(ff[:, bass.ds(n, 1), 0:T], sil[:, j % 2, 0:T].unsqueeze(1),
                                    cva[:, 1, :].unsqueeze(1), ALU.mult).then_inc(S("ff_mid"), 1)

                turns(dve, FF1_TILES, 2, tile, chain=link, links=5, peel=1)
                down(name + "_down", T)

            def ffn2(up, dn, N, l, c):
                ga = take("gate_act", FF2_TILES)
                take("ff_mid", FF2_TILES)

                def tile(n, j, i):
                    dve.wait_ge(S("gate_act"), n + (ga + 1))
                    V.tensor_tensor(ff[:, bass.ds(n, 1), 0:N], sil[:, j % 2, 0:N].unsqueeze(1),
                                    bank[2 * (j % 2) + 1][:, 0:N].unsqueeze(1), ALU.mult).then_inc(S("ff_mid"), 1)

                turns(dve, FF2_TILES, 2, tile)
                down(dn, N, l, c)

            def rope(out, x, rot, cos, sin, n, sem):
                r = ropet[:, 0, 0:n * T].rearrange("p (a t) -> p a t", a=n)
                c = cos.unsqueeze(1).to_broadcast([P, n, T]) if n > 1 else cos.unsqueeze(1)
                s = sin.unsqueeze(1).to_broadcast([P, n, T]) if n > 1 else sin.unsqueeze(1)
                link(V.tensor_tensor(r, rot, s, ALU.mult))
                x2 = ropet[:, 1, 0:n * T].rearrange("p (a t) -> p a t", a=n)
                link(V.tensor_tensor(x2, x, c, ALU.mult))
                V.tensor_tensor(out, r, x2, ALU.add).then_inc(S(sem), 1)
                dve.wait_ge(S(sem), take(sem, 1) + 1)

            def mixers(l):
                normed(KD, T, lambda k: res[:, k, 0:T], lambda k: h[:, k, 0:T],
                       lambda k: par(f"attn_norm{l}", k, k + 1), "norm_h")
                e = take("in_evac", 13)
                dve.wait_ge(S("in_evac"), e + 1)
                link(V.memset(U[:, U_SCC:U_Z, 0:PAD], 0.0))
                dve.wait_ge(S("in_evac"), e + 2)
                x = dtw[:, 2, :]
                b2 = par(f"dt_bias{l}").unsqueeze(1).to_broadcast([P, 2, HEADS])
                link(V.tensor_tensor(x.rearrange("p (b h) -> p b h", b=2), tm[:, :, 0:HEADS], b2, ALU.add))
                V.scalar_tensor_tensor(dtw[:, 0, :], x, -1.0, x, ALU.mult, ALU.max).then_inc(S("dt_raw"), 1)
                ro = take("rotated", 1)
                xb = dtw
                dve.wait_ge(S("in_evac"), e + 13)
                for t in range(8):
                    c = xc[:, t, :]
                    w = par(f"conv_w{l}", 4 * t, 4 * t + 4)
                    u = U[:, U_XBC + t, :]
                    link(V.tensor_scalar(c, u[:, 3:3 + T], w[:, 3:4], par(f"conv_b{l}", t, t + 1), ALU.mult, ALU.add))
                    link(V.scalar_tensor_tensor(c, u[:, 2:2 + T], w[:, 2:3], c, ALU.mult, ALU.add))
                    link(V.scalar_tensor_tensor(c, u[:, 1:1 + T], w[:, 1:2], c, ALU.mult, ALU.add))
                    V.scalar_tensor_tensor(c, u[:, 0:T], w[:, 0:1], c, ALU.mult, ALU.add).then_inc(S("xbc_conv"), 1)
                de = take("dt_exp", 3)
                dve.wait_ge(S("dt_exp"), de + 3)
                ex, z, z2, p, dt = (dtw[:, i, :] for i in (1, 3, 4, 5, 6))
                link(V.tensor_scalar(z, ex, 2.0, None, ALU.add))
                link(V.reciprocal(z, z))
                link(V.tensor_tensor(z, z, ex, ALU.mult))
                link(V.tensor_tensor(z2, z, z, ALU.mult))
                link(V.tensor_scalar(p, z2, 1.0 / 17, None, ALU.mult))
                for c in (15, 13, 11, 9, 7, 5, 3):
                    link(V.scalar_tensor_tensor(p, p, 1.0 / c, z2, ALU.add, ALU.mult))
                link(V.scalar_tensor_tensor(p, p, 1.0, z, ALU.add, ALU.mult))
                link(V.tensor_scalar(x, x, 0.0, None, ALU.max))
                link(V.scalar_tensor_tensor(dt, p, 2.0, x, ALU.mult, ALU.add))
                e2 = ea[:, :].unsqueeze(1).to_broadcast([P, 2, HEADS])
                V.scalar_tensor_tensor(dtw[:, 7, :].rearrange("p (b h) -> p b h", b=2),
                                       dt.rearrange("p (b h) -> p b h", b=2), -1.0, e2, ALU.mult,
                                       ALU.mult).then_inc(S("dt_ready"), 1)
                link(V.tensor_scalar(gate[:, :, :], gate[:, :, :], 1.0, None, ALU.add))
                link(V.reciprocal(gate[:, :, :], gate[:, :, :]))
                dve.wait_ge(S("rotated"), ro + 1)
                for lo, n, b, out in ((0, 2, 2, None), (2, 2, 3, None), (4, 1, 4, None)):
                    r = bank[b][:, 0:n * T].rearrange("p (a t) -> p a t", a=n)
                    sin = con("sin1").unsqueeze(1).to_broadcast([P, n, T])
                    cos = con("cos1").unsqueeze(1).to_broadcast([P, n, T])
                    rs = ropet[:, 0, 0:n * T].rearrange("p (a t) -> p a t", a=n)
                    xs = ropet[:, 1, 0:n * T].rearrange("p (a t) -> p a t", a=n)
                    link(V.tensor_tensor(rs, r, sin, ALU.mult))
                    link(V.tensor_tensor(xs, U[:, lo:lo + n, PAD:UW], cos, ALU.mult))
                    if lo == 0:
                        link(V.tensor_tensor(kvr[0:64, :], rs[0:64, 0, :], xs[0:64, 0, :], ALU.add))
                        link(V.tensor_copy(kvr[64:128, :], U[64:128, U_KCVC, PAD:UW]))
                        link(V.tensor_tensor(krq[:, 0, :], rs[:, 1, :], xs[:, 1, :], ALU.add))
                    else:
                        link(V.tensor_tensor(krq[:, lo - 1:lo - 1 + n, :], rs, xs, ALU.add))
                tok = kvr[:, :].rearrange("p (n j) -> p j n", j=CMP_STRIDE)
                pos = par(f"pos{l}")
                for half in range(2):
                    ph = pos[:, 16 * half:16 * half + 16].unsqueeze(2).to_broadcast([P, 16, N_CMP])
                    ins = V.tensor_tensor(tpos[:, 16 * half:16 * half + 16, :], tok[:, :, half:half + N_CMP], ph, ALU.add)
                    if half:
                        ins.then_inc(S("tpos_ready"), 1)
                cu = take("cumulated", 1)
                dve.wait_ge(S("cumulated"), cu + 1)
                V.tensor_copy(acs[:, :, :], bank[5][:, 0:16].rearrange("p (b h) -> p b h", b=2))
                link(V.tensor_copy(acsT[:, :], bank[5][0:HEADS, T:2 * T]))
                ck = take("cmp_kv", 1)
                dve.wait_ge(S("cmp_kv"), ck + 1)
                V.tensor_copy(kc[:, :], bank[6][:, 0:N_CMP])
                link(V.tensor_copy(vc[:, :], bank[6][0:N_CMP, 64:128]))
                xt = take("x_turned", 1)
                dve.wait_ge(S("x_turned"), xt + 1)
                for tb in range(2):
                    d8 = dt.rearrange("p (b h) -> p b h", b=2)[:, tb, :].unsqueeze(2).to_broadcast([P, HEADS, 64])
                    V.tensor_tensor(xdt[:, tb, :].rearrange("p (h d) -> p h d", h=HEADS),
                                    bank[2 + tb][:, :].rearrange("p (h d) -> p h d", h=HEADS), d8, ALU.mult)
                cb = take("cb_ready", 1)
                dve.wait_ge(S("cb_ready"), cb + 1)
                for g in range(GROUPS):
                    last = V.tensor_copy(cbT[:, g, :], bank[g][:, 0:384])
                last.then_inc(S("ssm_start"), 1)
                for t in range(2):
                    cc = U[:, U_SCC + t, :]
                    w = par(f"sc_w{l}", 3 * t, 3 * t + 3)
                    o = yT[:, 4 + t, :]
                    link(V.tensor_tensor(cc[:, PAD:UW], cc[:, PAD:UW], U[:, U_SCH + t, PAD:UW], ALU.mult))
                    link(V.tensor_scalar(o, cc[:, 3:3 + T], w[:, 2:3], None, ALU.mult))
                    link(V.scalar_tensor_tensor(o, cc[:, 2:2 + T], w[:, 1:2], o, ALU.mult, ALU.add))
                    link(V.scalar_tensor_tensor(o, cc[:, 1:1 + T], w[:, 0:1], o, ALU.mult, ALU.add))
                    V.tensor_tensor(o, o, U[:, U_SCB + t, PAD:UW], ALU.mult).then_inc(S("mixed"), 1)
                b = take("att", 8)
                causal = con("causal").rearrange("p (b t) -> p b t", b=2)
                cadd = con("cmp_add").rearrange("p (b t) -> p b t", b=2)
                keep = con("cmp_keep").rearrange("p (b t) -> p b t", b=2)

                def maxes(u):
                    dve.wait_ge(S("att_scores"), b + u + 1)
                    s, q = stat[:, u % 2, :], u % 2
                    for r in range(2):
                        V.tensor_tensor_reduce(sbS[:, q, r * T:(r + 1) * T], bank[q][:, r * T:(r + 1) * T],
                                               causal[:, u % 2, :], 1.0, -3e38, ALU.add, ALU.max, s[:, r:r + 1])
                    link(V.tensor_tensor_reduce(sbPC[:, q, 0:N_CMP], bank[2 + q][:, 0:N_CMP], cadd[:, u % 2, 0:N_CMP],
                                                1.0, -3e38, ALU.add, ALU.max, s[:, 2:3]))
                    V.tensor_scalar(s[:, 3:6], s[:, 0:3], -0.125, None, ALU.mult).then_inc(S("att_max"), 1)

                def probs(u):
                    dve.wait_ge(S("att_exp"), b + u + 1)
                    s, q, hh = stat[:, u % 2, :], u % 2, u // 2
                    link(V.tensor_tensor_reduce(sbPC[:, q, 0:N_CMP], sbPC[:, q, 0:N_CMP], keep[:, u % 2, 0:N_CMP],
                                                1.0, 0.0, ALU.mult, ALU.add, s[:, 8:9]))
                    link(V.tensor_scalar(s[:, 8:9], s[:, 8:9], 1e-20, None, ALU.max))
                    link(V.reciprocal(s[:, 9:12], s[:, 6:9]))
                    g = gate[:, u % 2, 3 * hh:3 * hh + 3]
                    V.tensor_tensor(s[:, 12:14], s[:, 9:11], g[:, 1:3], ALU.mult)
                    link(V.tensor_tensor(s[:, 14:15], s[:, 11:12], g[:, 0:1], ALU.mult))
                    V.tensor_scalar(sbPC[:, q, 0:N_CMP], sbPC[:, q, 0:N_CMP], s[:, 14:15], None, ALU.mult)
                    V.tensor_scalar(sbP[:, q, 0:T], sbP[:, q, 0:T], s[:, 12:13], None, ALU.mult)
                    V.tensor_scalar(sbP[:, q, T:2 * T], sbP[:, q, T:2 * T], s[:, 13:14], None,
                                    ALU.mult).then_inc(S("att_probs"), 1)

                def outs(u):
                    dve.wait_ge(S("att_prod"), b + u + 1)
                    hh = u // 2
                    rows = slice(64 * (hh % 2), 64 * (hh % 2) + 64)
                    V.tensor_copy(yT[rows, 6 + hh // 2, (u % 2) * P:(u % 2 + 1) * P],
                                  bank[6 + u % 2][rows, 0:P]).then_inc(S("att_out"), 1)

                maxes(0)
                for u in range(9):
                    if u < 7:
                        maxes(u + 1)
                    if u < 8:
                        probs(u)
                    if u >= 1:
                        outs(u - 1)
                y = take("ssd", HEADS)
                mask = con("decay_mask")

                def diff(hh):
                    dve.wait_ge(S("ssd_spread"), y + hh + 1)
                    if hh >= 2:
                        dve.wait_ge(S("ssd_exp"), y + hh - 1)
                    o = sbS[:, hh % 2, :]
                    V.scalar_tensor_tensor(o[:, 0:T], bank[hh % 2][:, 0:T], acs[:, 0, hh:hh + 1], mask[:, 0:T],
                                           ALU.subtract, ALU.add)
                    V.scalar_tensor_tensor(o[:, T:384], bank[hh % 2][:, P:T], acs[:, 1, hh:hh + 1], mask[:, T:384],
                                           ALU.subtract, ALU.add).then_inc(S("ssd_diff"), 1)

                def mats(hh):
                    dve.wait_ge(S("ssd_exp"), y + hh + 1)
                    V.tensor_tensor(sbP[:, hh % 2, 0:384], sbP[:, hh % 2, 0:384], cbT[:, hh // 4, :],
                                    ALU.mult).then_inc(S("ssd_mat"), 1)

                def out(t):
                    dve.wait_ge(S("ssd_y"), y + 2 * t + 2)
                    link(V.scalar_tensor_tensor(yss[:, t, :], xc[:, t, :], par(f"d_skip{l}", t, t + 1),
                                                bank[2 + t % 2][:, 0:T], ALU.mult, ALU.add))
                    V.tensor_tensor(yss[:, t, :], yss[:, t, :], U[:, U_Z + t, PAD:UW], ALU.mult).then_inc(S("ssd_out"), 1)

                zr = take("z_ready", 1)
                dve.wait_ge(S("z_ready"), zr + 1)
                diff(0)
                for hh in range(HEADS):
                    if hh + 1 < HEADS:
                        diff(hh + 1)
                    mats(hh)
                    if hh % 2 == 0 and hh:
                        out(hh // 2 - 1)
                out(3)
                rms(4, T)
                for k in range(4):
                    V.scalar_tensor_tensor(yT[:, k, :], yss[:, k, :], par(f"ssd_norm{l}", k, k + 1), rstd[:, 0:T],
                                           ALU.mult, ALU.mult).then_inc(S("mixed"), 1)
                project(f"l{l}_out", T)

            dve.wait_ge(S("params_in"), 16)
            dve.wait_ge(S("consts_in"), 16)
            mb = PARAMS["mod_b"][0]

            def mod_vec(n, j, i):
                dve.wait_ge(S("mod_cols"), n + 1)
                V.tensor_tensor(modT[:, bass.ds(n * 3, 3), :], bank[2 + j % 2][:, 0:6].rearrange("p (q s) -> p q s", s=2),
                                params[:, bass.ds(n * 3 + mb, 3)].unsqueeze(2).to_broadcast([P, 3, 2]),
                                ALU.add).then_inc(S("mod_vec"), 1)

            turns(dve, MOD_PANELS, 2, mod_vec)
            dve.wait_ge(S("mod_vec"), MOD_PANELS + 2)
            for l in range(LAYERS):
                for j in range(3):
                    q = (l * N_MOD + 3 * j + 1) * KD
                    g = par("mod_norm", (3 * l + j) * KD, (3 * l + j + 1) * KD).unsqueeze(2).to_broadcast([P, KD, 2])
                    link(V.scalar_tensor_tensor(modT[:, q:q + KD, :], modT[:, q:q + KD, :], 1.0, g, ALU.add, ALU.mult))
                    if j != 1:
                        link(V.tensor_scalar(modT[:, q + KD:q + 2 * KD, :], modT[:, q + KD:q + 2 * KD, :], 0.5, None,
                                             ALU.mult))
            dve.wait_ge(S("x_in"), 16)
            dve.wait_ge(S("ctx_in"), 16)
            for l in range(LAYERS):
                mixers(l)
                normed(KD, T, lambda k: res[:, k, 0:T], lambda k: h[:, k, 0:T],
                       lambda k: par(f"ffn_norm{l}", k, k + 1), "norm_h")
                ffn1(l)
            normed(KD, T, lambda k: res[:, k, 0:T], lambda k: res[:, k, 0:T], lambda k: par("final1", k, k + 1), "final1")
            norm_mod(0, 0, 2 * T)
            ffn2("m0_upa", "m0_downa", 2 * T, 0, 2)
            norm_mod(0, 3, 2 * T)
            dve.wait_ge(S("rotated"), LAYERS + 1)
            rope(dpj[:, 6:7, 0:T], dpj[:, 6:7, 0:T], bank[4][:, 0:T].unsqueeze(1), con("cos2"), con("sin2"), 1, "key_rope")
            normed(4, 2 * T, lambda k: dpj[:, k, :], lambda k: dpj[:, k, :], lambda k: par("q_norm", k, k + 1), "lat_normed")
            dve.wait_ge(S("lat_normed"), 4)
            normed(2, 2 * T, lambda k: dpj[:, 4 + k, :], lambda k: dpj[:, 4 + k, :],
                   lambda k: par("kv_norm", k, k + 1), "lat_normed")

            def pair_rope(p):
                qn, qr, qrot, kn, vv = pairs[p % 2]
                dve.wait_ge(S("pair_rot"), p + 1)
                rope(qrot.unsqueeze(1), qr[:, 0:T].unsqueeze(1), bank[3][:, 0:T].unsqueeze(1), con("cos2"), con("sin2"),
                     1, "pair_rope")

            def attention(units, maxes, total, outs, width, between=None):
                b = take("att", units)

                def probs(u):
                    dve.wait_ge(S("att_exp"), b + u + 1)
                    W, q = width(u), u % 2
                    link(V.reciprocal(stat[:, q, 4:5], total(u)))
                    V.tensor_scalar(sbP[:, q, 0:W], sbP[:, q, 0:W], stat[:, q, 4:5], None,
                                    ALU.mult).then_inc(S("att_probs"), 1)

                maxes(0, b)
                for u in range(units + 1):
                    if between:
                        between(u)
                    if u < units - 1:
                        maxes(u + 1, b)
                    if u < units:
                        probs(u)
                    if u >= 1:
                        outs(u - 1, b)

            def mla_max(u, b):
                dve.wait_ge(S("att_scores"), b + u + 1)
                q = u % 2
                link(V.tensor_reduce(stat[:, q, 0:1], bank[q][:, 0:512 if u % 4 < 2 else 256], AXX, ALU.max))
                V.tensor_scalar(stat[:, q, 1:2], stat[:, q, 0:1], -(192 ** -0.5), None, ALU.mult).then_inc(S("att_max"), 1)

            def mla_out(u, b):
                dve.wait_ge(S("att_prod"), b + u + 1)
                V.tensor_copy(h[:, u // 4, (u % 4) * P:(u % 4 + 1) * P], bank[6 + u % 2][:, 0:P]).then_inc(S("att_out"), 1)

            pair_rope(0)
            attention(32, mla_max, lambda u: stat[:, u % 2, 2:3], mla_out, lambda u: 512 if u % 4 < 2 else 256,
                      lambda u: pair_rope(u // 8 + 1) if u % 8 == 3 and u // 8 < 3 else None)
            project("mla_o", 2 * T, 0, 5)
            norm_mod(0, 6, 2 * T)
            ffn2("m0_upb", "m0_downb", 2 * T, 0, 8)
            norm_mod(1, 0, 2 * T)
            ffn2("m1_upa", "m1_downa", 2 * T, 1, 2)
            norm_mod(1, 3, 2 * T)
            for g in range(6):
                dve.wait_ge(S("swa_rot"), g + 1)
                rot = bank[6 + g % 2][:, :].rearrange("p (a t) -> p a t", a=2)
                if g < 4:
                    src, dst = sq_q[:, 2 * g:2 * g + 2, :], sq_qrot[:, 2 * g:2 * g + 2, :]
                else:
                    src = dst = sq_k[:, 2 * (g - 4):2 * (g - 4) + 2, 0:T]
                rope(dst, src, rot, con("cos2"), con("sin2"), 2, "swa_rope")
            window = con("window").rearrange("p (b t) -> p b t", b=2)

            def swa_max(u, b):
                dve.wait_ge(S("att_scores"), b + u + 1)
                q = u % 2
                s = stat[:, q, :]
                V.tensor_tensor_reduce(sbS[:, q, 0:T], bank[q][:, 0:T], window[:, u % 2, :], 1.0, -3e38, ALU.add,
                                       ALU.max, s[:, 5:6])
                V.tensor_copy(sbS[:, q, T:2 * T], bank[q][:, T:2 * T])
                link(V.tensor_reduce(s[:, 6:7], bank[q][:, T:2 * T], AXX, ALU.max))
                link(V.tensor_tensor(s[:, 0:1], s[:, 5:6], s[:, 6:7], ALU.max))
                link(V.tensor_scalar(s[:, 0:1], s[:, 0:1], 0.125, par("sink", u // 2, u // 2 + 1), ALU.mult, ALU.max))
                V.tensor_scalar(s[:, 1:2], s[:, 0:1], -1.0, None, ALU.mult).then_inc(S("att_max"), 1)

            def swa_total(u):
                s = stat[:, u % 2, :]
                link(V.tensor_tensor(s[:, 7:8], s[:, 2:3], s[:, 3:4], ALU.add))
                return s[:, 7:8]

            def swa_out(u, b):
                dve.wait_ge(S("att_prod"), b + u + 1)
                hh = u // 2
                rows = slice(64 * (hh % 2), 64 * (hh % 2) + 64)
                V.tensor_copy(h[rows, hh // 2, (u % 2) * P:(u % 2 + 1) * P], bank[6 + u % 2][rows, 0:P]).then_inc(S("att_out"), 1)

            attention(32, swa_max, swa_total, swa_out, lambda u: 512)
            project("swa_o", T, 1, 5)
            norm_mod(1, 6, T)
            ffn2("m1_upb", "m1_downb", T, 1, 8)
            normed(KD, T, lambda k: res[:, k, 0:T], lambda k: h[:, k, 0:T], lambda k: par("final2", k, k + 1), "final_out")


def tiles_of(w):
    K, M = w.shape
    k, m = -(-K // P), -(-M // P)
    full = np.zeros((k * P, m * P), np.float32)
    full[:K, :M] = w
    return full.reshape(k, P, m, P).transpose(2, 1, 0, 3)


def pair_panels(t):
    if len(t) % 2:
        t = np.concatenate([t, np.zeros_like(t[:1])])
    n, p, k, m = t.shape
    return t.reshape(n // 2, 2, p, k, m).transpose(0, 2, 1, 3, 4).reshape(n // 2, p, 2 * k * m)


def columns(v):
    v = np.asarray(v)
    n = -(-v.shape[-1] // P) * P
    out = np.zeros(v.shape[:-1] + (n,), np.float32)
    out[..., :v.shape[-1]] = v
    return np.moveaxis(out.reshape(v.shape[:-1] + (n // P, P)), -1, 0)


def constants():
    c = np.zeros((P, CONST_W), np.float32)

    def put(name, v):
        at, w = CONSTS[name]
        v = np.asarray(v, np.float32)
        c[:v.shape[0], at:at + w] = v.reshape(v.shape[0], -1)

    i, t = np.arange(P), np.arange(T)
    put("ident", np.eye(P))
    tok = np.arange(2)[None, :, None] * P + i[:, None, None]
    put("tri", tok <= t)
    put("rot", (i[:, None] ^ 32) == i[None, :])
    f32 = np.float32
    half = 32
    inv1 = f32(1.0) / (f32(10000.0) ** (np.arange(half, dtype=f32) / f32(half)))
    ang1 = t.astype(f32)[:, None] * inv1[None, :]
    n = 16
    inv2 = np.exp(f32(-np.log(10000.0)) * np.arange(n, dtype=f32) / f32(n)).astype(f32)
    ang2 = np.concatenate([(t // 64).astype(f32)[:, None] * inv2, (t % 64).astype(f32)[:, None] * inv2], -1)
    for name, ang in (("1", ang1), ("2", ang2)):
        ang = ang.astype(f32).T
        put("cos" + name, np.tile(np.cos(ang), (4, 1)))
        s = np.sin(ang)
        put("sin" + name, np.concatenate([-s, s, -s, s]))
    put("causal", np.where(t <= tok, 0, NEG))
    m = np.where(tok <= t, 0, NEG)
    put("decay_mask", np.concatenate([m[:, 0], m[:, 1, P:]], -1))
    end = np.arange(16) * CMP_STRIDE + CMP_BLOCK - 1
    put("cmp_add", np.where(end <= tok, 0, NEG))
    put("cmp_keep", end <= tok)
    put("window", np.where(np.abs(t - tok) <= 128, 0, NEG))
    put("head_pick", np.repeat(np.eye(HEADS), P, axis=1))
    return c


def kernel(**inputs):
    import concourse.bacc as bacc
    from concourse.bass_utils import run_bass_kernel_spmd

    a = {k: np.asarray(v) for k, v in inputs.items()}
    par = np.zeros((P, PARAM_W), np.float32)

    def put(name, v):
        at, w = PARAMS[name]
        par[:v.shape[0], at:at + w] = v.reshape(v.shape[0], -1)

    def rows(v):
        return np.broadcast_to(v, (P,) + v.shape)

    w = {}
    w["mod"] = a["mod_w_2"].reshape(LAYERS, KD, P, N_MOD * DM // MODW, MODW).transpose(0, 3, 2, 1, 4).reshape(
        MOD_PANELS, P, KD * MODW)
    for l in range(LAYERS):
        wi = a["w_in"][l]
        cuts = np.cumsum([INNER, XBC, HEADS, SC, SC, SC, 256] + [64] * 6 + [12])
        z, xbc, dt, scb, scc, sch, q, kc, vc, ks, vs, kw, vw, g = np.split(wi, cuts[:-1], axis=1)
        t = tiles_of(np.concatenate([kc, vc, ks, ks, kw, kw, q, scb, scc, sch, xbc, z], axis=1))
        tmw = np.concatenate([dt, vs, vw, g], axis=1).reshape(KD, P, TM).transpose(1, 0, 2).reshape(P, KD * TM)
        w[f"l{l}_in0"] = np.concatenate([t[0].reshape(P, KD * P), tmw], axis=1)[None]
        w[f"l{l}_in"] = pair_panels(t[1:])
        kv = np.concatenate([a["cmp_k_w1"][l].reshape(CMP_BLOCK, 64, P), a["cmp_v_w1"][l].reshape(CMP_BLOCK, 64, P)], axis=1)
        w[f"l{l}_cmp"] = kv.reshape(2, 16, P, P).transpose(0, 2, 1, 3).reshape(2, P, 16 * P)
        w[f"l{l}_out"] = pair_panels(tiles_of(a["w_out"][l]))
        g, v = tiles_of(a["ffn_w_up"][l][:, :FF1]), tiles_of(a["ffn_w_up"][l][:, FF1:])
        w[f"l{l}_up"] = pair_panels(np.stack([g, v], 1).reshape((2 * FF1_TILES,) + g.shape[1:]))
        w[f"l{l}_down"] = tiles_of(a["ffn_w_down"][l]).reshape(KD, P, FF1_TILES * P)
        put(f"attn_norm{l}", columns(a["attn_norm_w"][l]))
        put(f"ffn_norm{l}", columns(a["ffn_norm_w"][l]))
        put(f"conv_w{l}", columns(a["ssd_conv_w"][l]).transpose(0, 2, 1))
        put(f"conv_b{l}", columns(a["ssd_conv_b"][l]))
        put(f"dt_bias{l}", rows(a["ssd_dt_bias"][l]))
        put(f"a_log{l}", rows(a["ssd_a_log"][l]))
        put(f"d_skip{l}", columns(np.repeat(a["ssd_d"][l], HDIM)))
        put(f"ssd_norm{l}", columns(a["ssd_norm_w"][l]))
        put(f"sc_w{l}", columns(a["sc_conv_w"][l]).transpose(0, 2, 1))
        put(f"pos{l}", np.concatenate([a["cmp_k_pos"][l].T, a["cmp_v_pos"][l].T]))
        put(f"k_w2{l}", np.concatenate([a["cmp_k_w2"][l]] * 2, axis=1))
        put(f"v_w2{l}", a["cmp_v_w2"][l])
        cw = np.concatenate([a["ffn_conv_w"][l], a["ffn_conv_b"][l][None]])
        cw = np.stack([columns(cw[:, :FF1]), columns(cw[:, FF1:])], 1)
        put(f"ffn_conv{l}", cw.transpose(0, 3, 1, 2))
        for j, s in enumerate("ab"):
            wi = a["ffn_w_in_2"][l, j]
            g, v = tiles_of(wi[:, :FF2_TILES * P]), tiles_of(wi[:, FF2_TILES * P:])
            w[f"m{l}_up{s}"] = pair_panels(np.stack([g, v], 1).reshape((2 * FF2_TILES,) + g.shape[1:]))
            w[f"m{l}_down{s}"] = tiles_of(a["ffn_w_out_2"][l, j]).reshape(KD, P, FF2_TILES * P)
    put("final1", columns(a["final_norm_w"]))
    put("cond", np.stack([columns(a["c_2"][0]), columns(a["c_ctx_2"])], -1))
    put("mod_norm", columns(a["norm_g_2"]))
    put("mod_b", columns(a["mod_b_2"]))
    put("final2", columns(a["final_norm_g_2"]))
    put("q_norm", columns(a["mla_q_norm_2"][0]))
    put("kv_norm", columns(a["mla_kv_norm_2"][0]))
    put("sink", rows(a["swa_sink_2"][0]))
    wd = a["mla_w_down_2"][0]
    w["mla_down"] = pair_panels(tiles_of(np.concatenate([wd, wd[:, 768:]], axis=1)))
    uq = a["mla_w_uq_2"][0].reshape(4, P, MLA_HEADS, 192)
    ukv = a["mla_w_ukv_2"][0].reshape(2, P, MLA_HEADS, 256)
    panels = []
    for p in range(4):
        hs = (2 * p, 2 * p + 1)
        qn = [uq[:, :, x, :128].transpose(1, 0, 2).reshape(P, -1) for x in hs]
        qr = [np.concatenate([uq[:, :, x, 128:] for x in hs], -1).transpose(1, 0, 2).reshape(P, -1)]
        kn = [ukv[:, :, x, :128].transpose(1, 0, 2).reshape(P, -1) for x in hs]
        vv = [np.concatenate([ukv[:, :, x, 128:] for x in hs], -1).transpose(1, 0, 2).reshape(P, -1)]
        panels.append(np.concatenate(qn + qr + kn + vv, axis=1))
    w["mla_pair"] = np.stack(panels)
    w["mla_o"] = pair_panels(tiles_of(a["mla_w_o_2"][0]))
    qkv = a["swa_w_qkv_2"][0]
    k = qkv[:, 1024:1280].reshape(DM, SWA_KV, 1, 64)
    k = np.concatenate([k, k], axis=2).reshape(DM, SWA_KV * P)
    v = qkv[:, 1280:].reshape(KD, P, T).transpose(1, 0, 2).reshape(1, P, KD * T)
    w["swa_qkv"] = np.concatenate([pair_panels(tiles_of(np.concatenate([qkv[:, :1024], k], axis=1))), v])
    w["swa_o"] = pair_panels(tiles_of(a["swa_w_o_2"][0]))

    def tokens(x):
        return np.ascontiguousarray(x.reshape(T, KD, P).transpose(2, 1, 0))

    arrays = {"x": tokens(a["x"]), "ctx": tokens(a["ctx_2"]), "params": par, "consts": constants()}
    for name, count, width in STREAM:
        arrays["w_" + name] = np.ascontiguousarray(w[name])
        assert arrays["w_" + name].shape == (count, P, width), name
    nc = bacc.Bacc("TRN2", target_bir_lowering=False, num_devices=1)
    t = {n: nc.dram_tensor(n, v.shape, F32, kind="ExternalInput").ap() for n, v in arrays.items()}
    out = nc.dram_tensor("out", (P, KD, T), F32, kind="ExternalOutput").ap()
    two_blocks(nc, t["x"], t["ctx"], t["params"], t["consts"], {n: t["w_" + n] for n, _, _ in STREAM}, out)
    r = run_bass_kernel_spmd(nc, [arrays], core_ids=[0])
    y = np.asarray(r.results[0]["out"])
    return y.transpose(2, 1, 0).reshape(1, T, DM)
```

```python
from contextlib import ExitStack

import concourse.bass as bass
import numpy as np
from concourse import mybir

F32 = mybir.dt.float32
F32R = mybir.dt.float32r
ALU = mybir.AluOpType
ACT = mybir.ActivationFunctionType
AXX = mybir.AxisListType.X

P = 128
DM = 1024
KD = DM // P
T = 256
EPS = 1e-6
NEG = -1e30
LAYERS = 2

HEADS, HDIM, GROUPS, STATE = 8, 64, 2, 128
INNER = HEADS * HDIM
XBC = INNER + 2 * GROUPS * STATE
SC = 256
FF1, FF1_TILES = 2752, 22
CMP_BLOCK, CMP_STRIDE, N_CMP = 32, 16, 15
TM = HEADS + 64 + 64 + 12
U_KCVC, U_KS, U_KW, U_Q, U_SCB, U_SCC, U_SCH, U_XBC, U_Z, U_TILES = 0, 1, 2, 3, 5, 7, 9, 11, 19, 23
PAD = 3
UW = PAD + T

FF2_TILES = 22
N_MOD = 9
MLA_HEADS, SWA_HEADS, SWA_KV = 8, 16, 4

RAW = 4
HALVES = 2
PANEL = 2048
MODW = 256
MOD_PANELS = LAYERS * N_MOD * DM // MODW
HALF_FF = 11
DOWN = HALF_FF * P

STREAM = [("mod", MOD_PANELS, PANEL, True)]
for _l in range(LAYERS):
    STREAM += [(f"l{_l}_in", 13, PANEL, True), (f"l{_l}_cmp", 2, PANEL, False), (f"l{_l}_out", 4, PANEL, True),
               (f"l{_l}_up", FF1_TILES, PANEL, True), (f"l{_l}_down", 2 * KD, DOWN, True)]


def ffn_stream(name):
    return [(name + "_up0", HALF_FF, PANEL, True), (name + "_down0", KD, DOWN, True),
            (name + "_up1", HALF_FF, PANEL, True), (name + "_down1", KD, DOWN, True)]


STREAM += ffn_stream("m0a") + [("mla_down", 4, PANEL, True), ("mla_pair", 8, 1536, False), ("mla_o", 4, PANEL, True)]
STREAM += ffn_stream("m0b") + ffn_stream("m1a") + [("swa_qkv", 7, PANEL, True), ("swa_o", 4, PANEL, True)]
STREAM += [("m1b_up", FF2_TILES, PANEL, True), ("m1b_down", 2 * KD, DOWN, True)]
FIRST_RAW, FIRST_SPLIT, WIDTH, _raw, _split = {}, {}, {}, 0, 0
for _name, _count, _width, _is_split in STREAM:
    FIRST_RAW[_name], FIRST_SPLIT[_name], WIDTH[_name] = _raw, _split, _width
    _raw += _count
    _split += _count * _is_split

NORMS = ([(KD, T), (4, T), (KD, T)] * LAYERS + [(KD, T)]
         + [(KD, 2 * T)] * 2 + [(4, 2 * T), (2, 2 * T)] + [(KD, 2 * T)] * 3 + [(KD, T)] * 2)


def table(widths):
    out, at = {}, 0
    for name, w in widths:
        out[name] = (at, w)
        at += w
    return out, at


PARAMS, PARAM_W = table(
    [(f"{n}{l}", w) for l in range(LAYERS) for n, w in (
        ("attn_norm", KD), ("ffn_norm", KD), ("conv_w", 32), ("conv_b", 8), ("dt_bias", HEADS), ("a_log", HEADS),
        ("d_skip", 4), ("ssd_norm", 4), ("sc_w", 6), ("pos", CMP_BLOCK), ("k_w2", P), ("v_w2", 64),
        ("ffn_conv", FF1_TILES * 8))]
    + [("final1", KD), ("cond", KD * 2), ("mod_norm", LAYERS * 3 * KD), ("mod_b", LAYERS * N_MOD * KD),
       ("final2", KD), ("q_norm", 4), ("kv_norm", 2), ("sink", SWA_HEADS)])
CONSTS, CONST_W = table([("ident", P), ("tri", 2 * T), ("rot", P), ("cos1", T), ("sin1", T), ("cos2", T), ("sin2", T),
                         ("causal", 2 * T), ("decay_mask", 384), ("cmp_add", 32), ("cmp_keep", 32),
                         ("window", 2 * T), ("fold", 2)])


class Tally:

    def __init__(self):
        self.at = {}

    def take(self, name, n):
        base = self.at.get(name, 0)
        self.at[name] = base + n
        return base


class Chain:

    def __init__(self, eng, sem):
        self.eng, self.sem, self.n, self.extra = eng, sem, 0, 0

    def __call__(self, ins):
        self.n += 1
        ins.then_inc(self.sem, 1)
        self.eng.wait_ge(self.sem, self.extra + self.n)


def turns(eng, count, unroll, body, chain=None, links=0, peel=0, tail=0):
    full = (count - tail) // unroll
    for n in range(peel * unroll):
        body(n, n % unroll, n // unroll)
    at = chain.n if chain else 0
    with eng.Fori(peel, full) as i:
        if chain:
            chain.extra = (i - peel) * (links * unroll) if peel else i * (links * unroll)
        for j in range(unroll):
            body(i * unroll + j, j, i)
    if chain:
        assert chain.n - at == links * unroll
        chain.n, chain.extra = at + links * unroll * (full - peel), 0
    for n in range(full * unroll, count):
        body(n, n % unroll, n // unroll)


def fixed(n):
    return isinstance(n, int)


def raw_slot(name, j):
    return (FIRST_RAW[name] + j) % RAW


def landed_value(name, j, i):
    return i * 16 + (FIRST_RAW[name] + j) // RAW * 16 + 16


def half_slot(name, j):
    return (FIRST_SPLIT[name] + j) % HALVES


def two_blocks(nc, xT, ctxT, params_d, consts_d, weights, out_d):
    ctx = ExitStack()
    with ctx:
        bytes_at = [nc.sbuf_base + 31 & ~31]

        def sb(name, shape, dt=F32, at=None):
            off = bytes_at[0] if at is None else at
            size = 4 * int(np.prod(shape[1:])) + 31 & ~31
            if at is None:
                bytes_at[0] += size
            assert off + size <= nc.sbuf_usable_end, name
            return nc.alloc_sbuf_tensor_at("sb_" + name, shape, dt, offset=off)

        sems = {}

        def S(name):
            if name not in sems:
                sems[name] = ctx.enter_context(nc.semaphore(name))
            return sems[name]

        raw = [sb(f"raw{s}", [P, PANEL]) for s in range(RAW)]
        w_hi = [sb(f"w_hi{s}", [P, PANEL], F32R) for s in range(HALVES)]
        w_lo = [sb(f"w_lo{s}", [P, PANEL], F32R) for s in range(HALVES)]
        res = sb("res", [P, KD, 2 * T])
        H = bytes_at[0]
        bytes_at[0] += 32768
        h_wide = [sb(f"h_{n}", [P, KD, 2 * T], F32R, at=H + 16384 * i) for i, n in enumerate(("hi", "lo"))]
        h_thin = [sb(f"hx_{n}", [P, KD, T], F32R, at=H + 8192 * i) for i, n in enumerate(("hi", "lo"))]
        ropet = sb("ropet", [P, 2, 2 * T], at=H + 16384)
        cbT = sb("cbT", [P, GROUPS, 384], at=H + 20480)
        tpos = sb("tpos", [P, CMP_BLOCK, N_CMP], at=H + 23552)
        kvr = sb("kvr", [P, T], at=H + 25600)
        sct = sb("sct", [P, 2, T], at=H + 26624)
        cond_w = sb("cond_w", [P, KD, P], F32R, at=H)
        M = bytes_at[0]
        bytes_at[0] += 4 * 22 * 512
        f_hi = sb("f_hi", [P, HALF_FF * 512], F32R, at=M)
        f_lo = sb("f_lo", [P, HALF_FF * 512], F32R, at=M + 4 * HALF_FF * 512)
        mid = sb("mid", [P, 22 * 512], at=M)
        normed_f = sb("normed", [P, KD, 2 * T], at=M)
        params = sb("params", [P, PARAM_W])
        consts = sb("consts", [P, CONST_W])
        modT = sb("modT", [P, LAYERS * N_MOD * KD, 2])
        cond = sb("cond", [P, KD, 2])
        mod_row = sb("mod_row", [4, 2, MODW])
        sq = sb("sq", [P, 2, 2 * T])
        sq_sum = sb("sq_sum", [P, 2 * T])
        eps = sb("eps", [P, 1])
        root_warm = sb("root_warm", [P, 1])
        rstd = sb("rstd", [P, 2 * T])
        inv = {n: sb(f"inv{n}", [P, P]) for n in (1024, 512, 256)}
        A = bytes_at[0]
        bytes_at[0] += 12288
        sbS = sb("sbS", [P, 2, 512], at=A)
        sbP = sb("sbP", [P, 2, 512], at=A + 4096)
        sbPT = sb("sbPT", [P, 2, 512], at=A + 8192)
        ropes = sb("ropes", [P, 2, T], at=A)
        sil = sb("sil", [P, 2, 2 * T], at=A)
        prod = sb("prod", [P, 2 * T], at=A + 4096)
        ucv = sb("ucv", [P, 2, 2, 2 + T], at=A + 6144)
        cva = sb("cva", [P, 2, 2, T])
        sbPC = sb("sbPC", [P, 2, 16])
        sbPCT = sb("sbPCT", [16, 2, P])
        stat = sb("stat", [P, 2, 16])
        tm = sb("tm", [P, 2, TM])
        gate = sb("gate", [P, 2, 12])
        dtw = sb("dtw", [P, 8, 16])
        ea = sb("ea", [P, HEADS])
        acs = sb("acs", [P, 2, HEADS])
        acsT = sb("acsT", [HEADS, T])
        hid = sb("hid", [P, 2, N_CMP])
        kc = sb("kc", [P, N_CMP])
        vc = sb("vc", [N_CMP, 64])
        bank = [ctx.enter_context(nc.psum_tensor(f"bank{b}", [P, 512], F32)) for b in range(8)]

        def par(name, a=0, b=None):
            at, w = PARAMS[name]
            return params[:, at + a:at + (w if b is None else b)]

        def con(name, a=0, b=None):
            at, w = CONSTS[name]
            return consts[:, at + a:at + (w if b is None else b)]

        def region(at, *shape):
            n = int(np.prod(shape))
            v = mid[:, at:at + n]
            return (v.rearrange("p (a b) -> p a b", a=shape[0]) if len(shape) == 2 else v), at + n

        ident = con("ident")
        U, at = region(0, U_TILES, UW)
        xc, at = region(at, 8, T)
        xdt, at = region(at, 2, INNER)
        yss, at = region(at, 4, T)
        krq, at = region(at, 4, T)
        dpj, at = region(0, 7, 512)
        pairs = []
        for _ in range(2):
            qn, at = region(at, 2, 512)
            qr, at = region(at, 512)
            qrot, at = region(at, T)
            kn, at = region(at, 2, 512)
            vv, at = region(at, 4, T)
            pairs.append((qn, qr, qrot, kn, vv))
        sq_q, at = region(0, 8, T)
        sq_qrot, at = region(at, 8, T)
        sq_k, at = region(at, SWA_KV, 512)
        sq_v, at = region(at, 4, T)

        def h_of(N):
            return h_wide if N > T else h_thin

        def hidden(half, N):
            return half[:, :].rearrange("p (n t) -> p n t", t=N)

        def mod(l, c, k, s):
            q = (l * N_MOD + c) * KD + k
            return modT[:, q, s:s + 1]

        def streams(n):
            return [(s, s * T) for s in range(n // T)]

        block = ctx.enter_context(nc.Block())

        @block.sync
        def _(sp):
            sp.dma_start(params[:, :], params_d).then_inc(S("params_in"), 16)
            sp.dma_start(consts[:, :], consts_d).then_inc(S("consts_in"), 16)
            sp.dma_start(res[:, :, 0:T], xT).then_inc(S("x_in"), 16)
            sp.dma_start(res[:, :, T:2 * T], ctxT).then_inc(S("ctx_in"), 16)
            sp.sem_inc(S("raw_free"), RAW)
            for name, count, width, _ in STREAM:
                def load(n, j, i):
                    sp.wait_ge(S("raw_free"), n + (FIRST_RAW[name] + 1))
                    slot = raw_slot(name, j)
                    sp.dma_start(raw[slot][:, 0:width], weights[name][n]).then_inc(S(f"landed{slot}"), 16)

                if count >= 2 * RAW:
                    turns(sp, count, RAW, load)
                else:
                    for n in range(count):
                        load(n, n, 0)
            sp.wait_ge(S("final_out"), KD)
            sp.dma_start(out_d, normed_f[:, :, 0:T]).then_inc(S("stored"), 16)
            sp.wait_ge(S("stored"), 16)

        @block.gpsimd
        def _(pool):
            for n in inv:
                nc.gpsimd.memset(inv[n][:, :], 1.0 / n).then_inc(S("fills"), 1)
            nc.gpsimd.memset(eps[:, :], EPS).then_inc(S("fills"), 1)
            nc.gpsimd.memset(cond_w[:, :, :].bitcast(F32), 0.0).then_inc(S("fills"), 1)
            squares_at, added = 0, 0
            for n, (K, N) in enumerate(NORMS):
                for k in range(1, K - 1):
                    pool.wait_ge(S("norm_sq"), squares_at + k + 1)
                    if added:
                        pool.wait_ge(S("sq_added"), added)
                    nc.gpsimd.tensor_tensor(sq_sum[:, 0:N], sq[:, k % 2, 0:N], sq_sum[:, 0:N],
                                            ALU.add).then_inc(S("sq_added"), 1)
                    added += 1
                squares_at += K

        @block.tensor
        def _(pe):
            tally = Tally()
            take = tally.take

            def mm(out, lhsT, rhs, start, stop):
                return nc.tensor.matmul(out, lhsT, rhs, start=start, stop=stop, skip_group_check=True)

            def mm3(out, w, x, start, stop):
                (wh, wl), (xh, xl) = w, x
                mm(out, wh, xh, start, False)
                mm(out, wh, xl, False, False)
                return mm(out, wl, xh, False, stop)

            def panel(name, j, i):
                pe.wait_ge(S("raw_free"), i * RAW + (FIRST_RAW[name] + j + 1 + RAW))
                slot = half_slot(name, j)
                return w_hi[slot], w_lo[slot]

            def whole(name, n):
                slot = raw_slot(name, n)
                pe.wait_ge(S(f"landed{slot}"), landed_value(name, n, 0))
                return raw[slot]

            def both(pair, *index):
                return tuple(x[index] for x in pair)

            def cols(w, a, n=P):
                return both(w, slice(None), slice(a, a + n))

            def norm(K, N, const):
                b = take("norm_sq", K)
                a = take("sq_added", max(K - 2, 0))
                c = take("rms_done", 1)
                if c:
                    pe.wait_ge(S("rms_done"), c)
                pe.wait_ge(S("norm_sq"), b + K - 1)
                if K > 2:
                    pe.wait_ge(S("sq_added"), a + K - 2)
                mm(bank[7][:, 0:N], inv[const][:, :], sq_sum[:, 0:N], True, False)
                pe.wait_ge(S("norm_sq"), b + K)
                mm(bank[7][:, 0:N], inv[const][:, :], sq[:, (K - 1) % 2, 0:N], False, True).then_inc(S("norm_sum"), 1)

            def split_input(N, K=KD):
                per = N // T
                b = take("norm_split", K * per)

                def ready(k=K - 1):
                    pe.wait_ge(S("norm_split"), b + (k + 1) * per)
                return ready

            pe.wait_ge(S("cond_ready"), 1)
            pe.wait_ge(S("consts_in"), 16)
            pe.sem_inc(S("mod_vec"), 2)

            def mod_cols(n, j):
                pe.wait_ge(S("mod_row"), n + 1)
                pe.wait_ge(S("mod_vec"), n + 1)
                for t in range(2):
                    last = mm(bank[2 + j % 2][:, 2 * t:2 * t + 2], mod_row[0:4, j % 2, t * P:(t + 1) * P],
                              con("fold")[0:4, :], True, True)
                last.then_inc(S("mod_cols"), 1)

            def mod_panel(n, j, i):
                w = panel("mod", j, i)
                if not (fixed(n) and n < 2):
                    pe.wait_ge(S("mod_row"), n - 1)
                for k in range(KD):
                    mm(bank[j % 2][:, 0:MODW], cond_w[:, k, :], w[0][:, k * MODW:(k + 1) * MODW], k == 0, False)
                    last = mm(bank[j % 2][:, 0:MODW], cond_w[:, k, :], w[1][:, k * MODW:(k + 1) * MODW], False,
                              k == KD - 1)
                last.then_inc(S("panels_used"), 1)
                if not (fixed(n) and n == 0):
                    mod_cols(n - 1, (j - 1) % RAW)

            turns(pe, MOD_PANELS, RAW, mod_panel, peel=1)
            mod_cols(MOD_PANELS - 1, (MOD_PANELS - 1) % 2)

            def project(name, N):
                b = take("res_done", KD)
                h = h_of(N)
                for n in range(KD // 2):
                    w = panel(name, n, 0)
                    for t in range(2):
                        m = 2 * n + t
                        if m >= 2:
                            pe.wait_ge(S("res_done"), b + m - 1)
                        for k in range(KD):
                            last = mm3(bank[4 + t][:, 0:N], cols(w, (t * KD + k) * P), both(h, slice(None), k),
                                       k == 0, k == KD - 1)
                        last.then_inc(S("panels_used" if t else "half_panel"), 1)

            def down(name, N):
                b = take("res_done", KD)
                f = [hidden(x, N) for x in (f_hi, f_lo)]
                per = 2 * T // N

                def tile(n, j, i):
                    w = panel(name, j, i)
                    m, part = j // per, j % per
                    if part == 0 and not (fixed(n) and n < 2 * per):
                        pe.wait_ge(S("res_done"), n // per + (b - 1) if fixed(n) else i * (RAW // per) + (m + b - 1))
                    for k in range(HALF_FF):
                        last = mm3(bank[4 + m % 2][:, 0:N], cols(w, k * P),
                                   both(f, slice(None), part * HALF_FF + k),
                                   part == 0 and k == 0, part == per - 1 and k == HALF_FF - 1)
                    last.then_inc(S("panels_used"), 1)

                turns(pe, KD * per, RAW, tile, peel=1)

            def up(name, count, N, sem, ready=None):
                b = take(sem, count)
                h = h_of(N)

                def tile(n, j, i):
                    w = panel(name, j, i)
                    if not (fixed(n) and n < 2):
                        pe.wait_ge(S(sem), n + (b - 1))
                    for half in range(2):
                        if sem == "up_evac":
                            o = bank[j % 2][:, half * T:(half + 1) * T]
                        else:
                            o = bank[2 * (j % 2) + half][:, 0:N]
                        for k in range(KD):
                            if ready and fixed(n) and n == 0 and half == 0:
                                ready(k)
                            last = mm3(o, cols(w, (half * KD + k) * P), both(h, slice(None), k), k == 0, k == KD - 1)
                    last.then_inc(S("panels_used"), 1)

                turns(pe, count, RAW, tile, peel=1)
                return b

            def ffn1(name):
                up(name + "_up", FF1_TILES, T, "up_evac", split_input(T))
                m = take("ff_mid", FF1_TILES)
                pe.wait_ge(S("ff_mid"), m + FF1_TILES)
                down(name + "_down", T)

            def ffn2(name, N):
                ready = split_input(N)
                if N == T:
                    b = up(name + "_up", FF2_TILES, N, "ff_mid", ready)
                    pe.wait_ge(S("ff_mid"), b + FF2_TILES)
                    down(name + "_down", N)
                    return
                for part in range(2):
                    b = up(f"{name}_up{part}", HALF_FF, N, "ff_mid", ready if part == 0 else None)
                    pe.wait_ge(S("ff_mid"), b + HALF_FF)
                    down(f"{name}_down{part}", N)

            def attention(units, scores, flips, products, shared=False):
                b = take("att_scores", units)

                def ahead(u):
                    if u >= 2:
                        pe.wait_ge(S("att_exp"), b + u - 1)
                    if u >= 2 and shared:
                        pe.wait_ge(S("att_turned"), b + u - 1)
                    scores(u).then_inc(S("att_scores"), 1)

                def turn(u):
                    pe.wait_ge(S("att_probs"), b + u + 1)
                    if u >= 2:
                        pe.wait_ge(S("att_turned"), b + u - 1)
                    flips(u).then_inc(S("att_flips"), 1)

                def product(u):
                    pe.wait_ge(S("att_turned"), b + u + 1)
                    if u >= 2:
                        pe.wait_ge(S("att_out"), b + u - 1)
                    products(u).then_inc(S("att_prod"), 1)

                return ahead, turn, product

            def mixers(l):
                L = f"l{l}"
                norm(KD, T, 1024)
                ready = split_input(T)
                h = h_thin
                w = panel(L + "_in", 0, 0)
                for tb in range(2):
                    for k in range(KD):
                        ready(k)
                        last = mm3(bank[2 + tb][:, 0:TM], both(h, slice(None), k, slice(tb * P, (tb + 1) * P)),
                                   cols(w, k * TM, TM), k == 0, k == KD - 1)
                last.then_inc(S("panels_used"), 1)
                e = take("in_evac", 13)

                def pair(n, j, i):
                    if fixed(n) and n == 0:
                        return
                    wp = panel(L + "_in", j, i)
                    if not (fixed(n) and n < 3):
                        pe.wait_ge(S("in_evac"), n + (e - 1))
                    for t in range(1 if fixed(n) and n == 12 else 2):
                        for k in range(KD):
                            last = mm3(bank[j % 2][:, t * T:(t + 1) * T], cols(wp, (t * KD + k) * P),
                                       both(h, slice(None), k), k == 0, k == KD - 1)
                    last.then_inc(S("panels_used"), 1)

                turns(pe, 13, RAW, pair, peel=1)
                pe.wait_ge(S("in_evac"), e + 4)
                for t in range(5):
                    last = mm(bank[[2, 2, 3, 3, 4][t]][:, (t % 2) * T:(t % 2 + 1) * T], con("rot"),
                              U[:, t, PAD:UW], True, True)
                last.then_inc(S("rotated"), 1)
                a = dtw[:, 7, :].rearrange("p (b h) -> p b h", b=2)
                d = take("dt_ready", 1)
                pe.wait_ge(S("dt_ready"), d + 1)
                tri = con("tri").rearrange("p (b t) -> p b t", b=2)
                mm(bank[5][:, 0:HEADS], tri[:, 0, 0:P], a[:, 0, :], True, True)
                mm(bank[5][:, 8:16], tri[:, 0, P:T], a[:, 0, :], True, False)
                mm(bank[5][:, 8:16], tri[:, 1, P:T], a[:, 1, :], False, True)
                mm(bank[5][0:HEADS, T:2 * T], a[:, 0, :], tri[:, 0, :], True, False)
                mm(bank[5][0:HEADS, T:2 * T], a[:, 1, :], tri[:, 1, :], False, True).then_inc(S("cumulated"), 1)
                tk = take("tpos_ready", 1)
                pe.wait_ge(S("tpos_ready"), tk + 1)
                for c in range(2):
                    w = whole(L + "_cmp", c)
                    for r in range(2):
                        rows = slice(64 * r, 64 * r + 64)
                        for jj in range(16):
                            j = 16 * c + jj
                            last = mm(bank[6 + r][:, 0:N_CMP], w[rows, jj * P:(jj + 1) * P], tpos[rows, j, :],
                                      j == 0, j == CMP_BLOCK - 1)
                    last.then_inc(S("raw_free"), 1)
                hd = take("hid_ready", 2)
                pe.wait_ge(S("hid_ready"), hd + 2)
                mm(bank[6][:, 0:N_CMP], par(f"k_w2{l}"), hid[:, 0, :], True, True)
                mm(bank[6][0:N_CMP, 64:128], hid[:, 1, :], par(f"v_w2{l}"), True, True).then_inc(S("cmp_kv"), 1)
                x = take("xbc_ready", 8)
                pe.wait_ge(S("xbc_ready"), x + 8)
                for tb in range(2):
                    for t in range(4):
                        last = nc.tensor.transpose(bank[2 + tb][:, t * P:(t + 1) * P], xc[:, t, tb * P:(tb + 1) * P],
                                                   ident)
                last.then_inc(S("x_turned"), 1)
                for g in range(GROUPS):
                    B, C = xc[:, 4 + g, :], xc[:, 6 + g, :]
                    mm(bank[g][:, 0:T], B[:, 0:P], C, True, True)
                    last = mm(bank[g][:, T:384], B[:, P:T], C[:, P:T], True, True)
                last.then_inc(S("cb_ready"), 1)
                s = take("ssm_start", 1)
                pe.wait_ge(S("ssm_start"), s + 1)

                def where(u):
                    hh, b = u // 2, u % 2
                    return slice(64 * (hh % 2), 64 * (hh % 2) + 64), hh, b

                def scores(u):
                    rows, hh, b = where(u)
                    q = krq[rows, 2 + hh // 2, b * P:(b + 1) * P]
                    mm(bank[2 + u % 2][:, 0:N_CMP], q, kc[rows, :], True, True)
                    mm(bank[u % 2][:, 0:T], q, krq[rows, 0, :], True, True)
                    return mm(bank[u % 2][:, T:2 * T], q, krq[rows, 1, :], True, True)

                def flips(u):
                    nc.tensor.transpose(bank[2 + u % 2][0:N_CMP, P:2 * P], sbPC[:, u % 2, 0:N_CMP], ident)
                    for c in range(4):
                        last = nc.tensor.transpose(bank[4 + u % 2][:, c * P:(c + 1) * P],
                                                   sbP[:, u % 2, c * P:(c + 1) * P], ident)
                    return last

                def products(u):
                    rows, hh, b = where(u)
                    o = bank[6 + u % 2][rows, 0:P]
                    mm(o, vc[:, :], sbPCT[0:N_CMP, u % 2, :], True, False)
                    for c in range(4):
                        v = tm[:, c % 2, 8 + 64 * (c // 2):72 + 64 * (c // 2)]
                        last = mm(o, v, sbPT[:, u % 2, c * P:(c + 1) * P], False, c == 3)
                    return last

                ahead, turn, product = attention(8, scores, flips, products, shared=True)
                ahead(0)
                for u in range(9):
                    if u < 7:
                        ahead(u + 1)
                    if u < 8:
                        turn(u)
                    if u >= 1:
                        product(u - 1)
                y = take("ssd_y", HEADS)
                yo = take("ssd_out", 4)
                at_start = take("att_out", 8)
                pe.wait_ge(S("att_out"), at_start + 8)

                def spread(hh):
                    if hh >= 2:
                        pe.wait_ge(S("ssd_diff"), y + hh - 1)
                    mm(bank[hh % 2][:, 0:T], ident[0:HEADS, hh:hh + 1].to_broadcast([HEADS, P]), acsT[:, :],
                       True, True).then_inc(S("ssd_spread"), 1)

                spread(0)
                spread(1)
                for hh in range(HEADS):
                    pe.wait_ge(S("ssd_mat"), y + hh + 1)
                    t = hh // 2
                    rows = slice(64 * (hh % 2), 64 * (hh % 2) + 64)
                    o = bank[2 + t % 2]
                    if hh % 2 == 0 and t >= 2:
                        pe.wait_ge(S("ssd_out"), yo + t - 1)
                    mm(o[rows, 0:T], xdt[:, 0, hh * 64:(hh + 1) * 64], sbP[:, hh % 2, 0:T], True, False)
                    mm(o[rows, P:T], xdt[:, 1, hh * 64:(hh + 1) * 64], sbP[:, hh % 2, T:384], False,
                       True).then_inc(S("ssd_y"), 1)
                    if hh + 2 < HEADS:
                        spread(hh + 2)
                norm(4, T, 512)
                m = take("mixed", 6)
                pe.wait_ge(S("mixed"), m + 6)
                project(L + "_out", T)

            pe.wait_ge(S("fills"), 5)
            for l in range(LAYERS):
                mixers(l)
                norm(KD, T, 1024)
                ffn1(f"l{l}")
            norm(KD, T, 1024)
            norm(KD, 2 * T, 1024)
            ffn2("m0a", 2 * T)
            norm(KD, 2 * T, 1024)
            split_input(2 * T)()
            h = h_wide
            d = take("lat_evac", 4)
            for n in range(4):
                w = panel("mla_down", n, 0)
                if n >= 2:
                    pe.wait_ge(S("lat_evac"), d + n - 1)
                for t in range(2 if n < 3 else 1):
                    for k in range(KD):
                        last = mm3(bank[2 * (n % 2) + t][:, :], cols(w, (t * KD + k) * P), both(h, slice(None), k),
                                   k == 0, k == KD - 1)
                last.then_inc(S("panels_used"), 1)
            pe.wait_ge(S("lat_evac"), d + 4)
            mm(bank[4][:, 0:T], con("rot"), dpj[:, 6, 0:T], True, True).then_inc(S("rotated"), 1)
            norm(4, 2 * T, 512)
            norm(2, 2 * T, 256)
            pe.wait_ge(S("lat_normed"), 6)

            def pair_tiles(p):
                w = whole("mla_pair", 2 * p)
                qn, qr, qrot, kn, vv = pairs[p % 2]

                def free(t):
                    if t >= 2:
                        pe.wait_ge(S("pair_evac"), 7 * p + t - 1)
                    elif p:
                        pe.wait_ge(S("pair_evac"), 7 * p)
                        if t == 1:
                            pe.wait_ge(S("pair_rope"), p)

                for t in range(5):
                    free(t)
                    if t == 3:
                        w = whole("mla_pair", 2 * p + 1)
                    K, at0, src = (4, t * 512, 0) if t < 3 else (2, (t - 3) * 256, 4)
                    for k in range(K):
                        last = mm(bank[2 + t % 2][:, :], w[:, at0 + k * P:at0 + (k + 1) * P], dpj[:, src + k, :],
                                  k == 0, k == K - 1)
                    last.then_inc(S("raw_free" if t == 2 else "pair_tile"), 1)
                for t in range(5, 7):
                    free(t)
                    for tb in range(2):
                        b4 = 2 * (t - 5) + tb
                        for k in range(2):
                            last = mm(bank[2 + t % 2][:, tb * T:(tb + 1) * T], dpj[:, 4 + k, b4 * P:(b4 + 1) * P],
                                      w[:, 512 + k * T:512 + (k + 1) * T], k == 0, k == 1)
                    last.then_inc(S("pair_tile" if t == 5 else "raw_free"), 1)

            def pair_rot(p):
                qn, qr, qrot, kn, vv = pairs[p % 2]
                pe.wait_ge(S("pair_evac"), 7 * p + 6)
                mm(bank[3][:, 0:T], con("rot"), qr[:, 0:T], True, True).then_inc(S("pair_rot"), 1)

            def mla_scores(u):
                p, hh, b = u // 8, u // 4 % 2, u % 4
                qn, qr, qrot, kn, vv = pairs[p % 2]
                rows, q = slice(64 * hh, 64 * hh + 64), slice(b * P, (b + 1) * P)
                if u % 8 == 0:
                    pe.wait_ge(S("pair_rope"), p + 1)
                    pe.wait_ge(S("pair_evac"), 7 * p + 7)
                A = bank[u % 2]
                if b < 2:
                    mm(A[:, :], qn[:, hh, q], kn[:, hh, :], True, False)
                    mm(A[:, 0:T], qrot[rows, q], dpj[rows, 6, 0:T], False, False)
                    return mm(A[:, T:2 * T], qr[rows, q], dpj[rows, 6, T:2 * T], False, True)
                mm(A[:, 0:T], qn[:, hh, q], kn[:, hh, T:2 * T], True, False)
                return mm(A[:, 0:T], qr[rows, q], dpj[rows, 6, T:2 * T], False, True)

            def mla_flips(u):
                for c in range(4 if u % 4 < 2 else 2):
                    last = nc.tensor.transpose(bank[4 + u % 2][:, c * P:(c + 1) * P],
                                               sbP[:, u % 2, c * P:(c + 1) * P], ident)
                return last

            def mla_products(u):
                p, hh, b = u // 8, u // 4 % 2, u % 4
                qn, qr, qrot, kn, vv = pairs[p % 2]
                nk = 4 if b < 2 else 2
                for c in range(nk):
                    last = mm(bank[6 + u % 2][:, 0:P], vv[:, c + 4 - nk, hh * P:(hh + 1) * P],
                              sbPT[:, u % 2, c * P:(c + 1) * P], c == 0, c == nk - 1)
                return last

            kr = take("key_rope", 1)
            pe.wait_ge(S("key_rope"), kr + 1)
            pair_tiles(0)
            pair_rot(0)
            ahead, turn, product = attention(32, mla_scores, mla_flips, mla_products)
            ahead(0)
            for u in range(33):
                if u % 8 == 1 and u // 8 < 3:
                    pair_tiles(u // 8 + 1)
                if u % 8 == 3 and u // 8 < 3:
                    pair_rot(u // 8 + 1)
                if u < 31:
                    ahead(u + 1)
                if u < 32:
                    turn(u)
                if u >= 1:
                    product(u - 1)
            o = take("att_out", 32)
            pe.wait_ge(S("att_out"), o + 32)
            project("mla_o", 2 * T)
            norm(KD, 2 * T, 1024)
            ffn2("m0b", 2 * T)
            norm(KD, 2 * T, 1024)
            ffn2("m1a", 2 * T)
            norm(KD, 2 * T, 1024)
            split_input(2 * T)()
            for n in range(7):
                w = panel("swa_qkv", n, 0)
                if 2 <= n <= 4:
                    pe.wait_ge(S("swa_evac"), min(n - 1 + n // 4, 4))
                for t in range(2):
                    if n < 4:
                        for k in range(KD):
                            last = mm3(bank[n % 2][:, t * T:(t + 1) * T], cols(w, (t * KD + k) * P),
                                       both(h, slice(None), k, slice(0, T)), k == 0, k == KD - 1)
                    elif n < 6:
                        for k in range(KD):
                            last = mm3(bank[2 * (n % 2) + t][:, :], cols(w, (t * KD + k) * P),
                                       both(h, slice(None), k), k == 0, k == KD - 1)
                    else:
                        for tb in range(2):
                            c = 2 * t + tb
                            for k in range(KD):
                                last = mm3(bank[4 + t][:, tb * T:(tb + 1) * T],
                                           both(h, slice(None), k, slice(c * P, (c + 1) * P)), cols(w, k * T, T),
                                           k == 0, k == KD - 1)
                last.then_inc(S("panels_used"), 1)
            for g in range(6):
                b = 6 + g % 2
                if g >= 2:
                    pe.wait_ge(S("swa_rope"), g - 1)
                for t in range(2):
                    src = sq_q[:, 2 * g + t, :] if g < 4 else sq_k[:, 2 * (g - 4) + t, 0:T]
                    pe.wait_ge(S("swa_evac"), g + 1)
                    last = mm(bank[b][:, t * T:(t + 1) * T], con("rot"), src, True, True)
                last.then_inc(S("swa_rot"), 1)
            pe.wait_ge(S("swa_evac"), 7)
            pe.wait_ge(S("swa_rope"), 6)

            def swa_scores(u):
                hh, b = u // 2, u % 2
                rows, q = slice(64 * (hh % 2), 64 * (hh % 2) + 64), slice(b * P, (b + 1) * P)
                A = bank[u % 2]
                mm(A[:, 0:T], sq_qrot[rows, hh // 2, q], sq_k[rows, hh // 4, 0:T], True, True)
                return mm(A[:, T:2 * T], sq_q[rows, hh // 2, q], sq_k[rows, hh // 4, T:2 * T], True, True)

            def swa_flips(u):
                for c in range(4):
                    last = nc.tensor.transpose(bank[4 + u % 2][:, c * P:(c + 1) * P],
                                               sbP[:, u % 2, c * P:(c + 1) * P], ident)
                return last

            def swa_products(u):
                hh, b = u // 2, u % 2
                rows = slice(64 * (hh % 2), 64 * (hh % 2) + 64)
                for c in range(4):
                    last = mm(bank[6 + u % 2][rows, 0:P], sq_v[:, c, (hh // 4) * 64:(hh // 4 + 1) * 64],
                              sbPT[:, u % 2, c * P:(c + 1) * P], c == 0, c == 3)
                return last

            ahead, turn, product = attention(32, swa_scores, swa_flips, swa_products)
            ahead(0)
            for u in range(33):
                if u < 31:
                    ahead(u + 1)
                if u < 32:
                    turn(u)
                if u >= 1:
                    product(u - 1)
            o = take("att_out", 32)
            pe.wait_ge(S("att_out"), o + 32)
            project("swa_o", T)
            norm(KD, T, 1024)
            ffn2("m1b", T)
            norm(KD, T, 1024)

        @block.scalar
        def _(act):
            take = Tally().take

            def run(out, in_, func, **kw):
                return nc.scalar.activation(out, in_, func, **kw)

            def panel_done(name, n):
                act.wait_ge(S("panels_used"), n + (FIRST_SPLIT[name] + 1))

            def high(name, j, i=0):
                act.wait_ge(S(f"landed{raw_slot(name, j)}"), landed_value(name, j, i))
                before = FIRST_SPLIT[name] + j - 1
                if before > 0 or not fixed(i):
                    act.wait_ge(S("panels_used"), i * RAW + before)
                w = WIDTH[name]
                run(w_hi[half_slot(name, j)][:, 0:w], raw[raw_slot(name, j)][:, 0:w], ACT.Copy).then_inc(S("high"), 1)

            def sweep(name, count, body, after=None, defer=False, unroll=RAW, loop=True):
                def step(n, j, i):
                    def ahead():
                        if not fixed(n) or n + 2 < count:
                            high(name, j + 2, i)
                        elif after and (n == count - 2 or not defer):
                            high(after, n + 2 - count)
                    body(n, j, i, ahead)

                if loop:
                    turns(act, count, RAW, step, peel=1, tail=2)
                else:
                    for n in range(count):
                        step(n, n, 0)

            def square(K, src, N):
                run(root_warm[:, :], eps[:, :], ACT.Sqrt)
                a = take("sq_added", max(K - 2, 0))
                c = take("norm_sum", 1)

                def one(k):
                    if k > 2:
                        act.wait_ge(S("sq_added"), a + k - 2)
                    out = sq_sum if k == 0 else sq[:, k % 2, :]
                    run(out[:, 0:N], src(k), ACT.Square).then_inc(S("norm_sq"), 1)
                    if k == K - 1:
                        act.wait_ge(S("norm_sum"), c + 1)
                        run(rstd[:, 0:N], bank[7][:, 0:N], ACT.Sqrt, bias=eps[:, :]).then_inc(S("rms_done"), 1)
                return one

            def res_square(N):
                b = take("res_done", KD)
                one = square(KD, lambda k: res[:, k, 0:N], N)

                def tile(k):
                    act.wait_ge(S("res_done"), b + k + 1)
                    one(k)
                return tile

            def high_input(N, shift=None, K=KD):
                b = take("norm_scaled", K * (N // T))
                h = h_of(N)[0]
                n = 0
                for k in range(K):
                    for s, at in streams(N):
                        n += 1
                        act.wait_ge(S("norm_scaled"), b + n)
                        if shift:
                            last = run(h[:, k, at:at + T], normed_f[:, k, at:at + T], ACT.Identity,
                                       bias=mod(*shift, k, s))
                        else:
                            last = run(h[:, k, at:at + T], normed_f[:, k, at:at + T], ACT.Copy)
                        last.then_inc(S("norm_high"), 1)

            def down(name, N, after=None, last=True):
                per = 2 * T // N
                tile = res_square(N) if last else take("res_done", KD)

                def body(n, j, i, ahead):
                    ahead()
                    if last and n % per == per - 1:
                        tile(n // per)

                sweep(name, KD * per, body, after, defer=last, loop=False)

            def project(name, N, after):
                tile = res_square(N)

                def body(n, j, i, ahead):
                    ahead()
                    tile(2 * n)
                    tile(2 * n + 1)

                sweep(name, KD // 2, body, after, defer=True, loop=False)

            def ffn1(l, after):
                name = f"l{l}"
                high_input(T)
                high(name + "_up", 1)
                b = take("ff_mid", FF1_TILES)
                g = take("gate_ready", FF1_TILES)
                w0 = PARAMS[f"ffn_conv{l}"][0]

                def tile(n, j, i, ahead):
                    panel_done(name + "_up", n)
                    if not (fixed(n) and n < 2):
                        act.wait_ge(S("ff_mid"), n + (b - 1))
                    run(ucv[:, j % 2, :, 2:2 + T], bank[j % 2][:, :].rearrange("p (a t) -> p a t", a=2), ACT.Copy)
                    for half in range(2):
                        w = params[:, bass.ds(n * 8 + (w0 + 4 * half + 2), 1)]
                        c = params[:, bass.ds(n * 8 + (w0 + 4 * half + 3), 1)]
                        last = run(cva[:, j % 2, half, :], bank[j % 2][:, half * T:(half + 1) * T], ACT.Identity,
                                   scale=w, bias=c)
                    last.then_inc(S("up_evac"), 1)
                    ahead()
                    act.wait_ge(S("gate_ready"), n + (g + 1))
                    run(sil[:, j % 2, 0:T], cva[:, j % 2, 0, :], ACT.Silu).then_inc(S("gate_act"), 1)

                sweep(name + "_up", FF1_TILES, tile, name + "_down")
                down(name + "_down", T, after)

            def up2(name, count, N, after):
                b = take("ff_mid", count)

                def tile(n, j, i, ahead):
                    panel_done(name, n)
                    if not (fixed(n) and n < 2):
                        act.wait_ge(S("ff_mid"), n + (b - 1))
                    run(sil[:, j % 2, 0:N], bank[2 * (j % 2)][:, 0:N], ACT.Silu).then_inc(S("gate_act"), 1)
                    ahead()

                sweep(name, count, tile, after)

            def ffn2(name, N, shift, after):
                high_input(N, shift)
                if N == T:
                    high(name + "_up", 1)
                    up2(name + "_up", FF2_TILES, N, name + "_down")
                    down(name + "_down", N, after)
                    return
                high(name + "_up0", 1)
                up2(name + "_up0", HALF_FF, N, name + "_down0")
                down(name + "_down0", N, name + "_up1", last=False)
                up2(name + "_up1", HALF_FF, N, name + "_down1")
                down(name + "_down1", N, after)

            def mixers(l):
                L = f"l{l}"
                high_input(T)
                high(L + "_in", 1)
                e = take("in_evac", 13)

                def pair(n, j, i, ahead):
                    panel_done(L + "_in", n)
                    if fixed(n) and n == 0:
                        for tb in range(2):
                            last = run(tm[:, tb, :], bank[2 + tb][:, 0:TM], ACT.Copy)
                    elif fixed(n) and n == 12:
                        last = run(U[:, 22, PAD:UW], bank[0][:, 0:T], ACT.Copy)
                    else:
                        last = run(U[:, bass.ds(n * 2 - 2, 2), PAD:UW],
                                   bank[j % 2][:, :].rearrange("p (a t) -> p a t", a=2), ACT.Copy)
                    last.then_inc(S("in_evac"), 1)
                    ahead()

                sweep(L + "_in", 13, pair)
                act.wait_ge(S("in_evac"), e + 13)
                x = take("dt_raw", 1)
                act.wait_ge(S("dt_raw"), x + 1)
                run(dtw[:, 1, :], dtw[:, 0, :], ACT.Exp, scale=-1.0).then_inc(S("dt_exp"), 1)
                run(gate[:, :, :], tm[:, :, 136:148], ACT.Exp, scale=-1.0).then_inc(S("dt_exp"), 1)
                run(ea[:, :], par(f"a_log{l}"), ACT.Exp).then_inc(S("dt_exp"), 1)
                x = take("xbc_conv", 8)
                for t in range(8):
                    act.wait_ge(S("xbc_conv"), x + t + 1)
                    run(xc[:, t, :], xc[:, t, :], ACT.Silu).then_inc(S("xbc_ready"), 1)
                run(U[:, U_Z:U_Z + 4, PAD:UW], U[:, U_Z:U_Z + 4, PAD:UW], ACT.Silu).then_inc(S("z_ready"), 1)
                act.wait_ge(S("raw_free"), FIRST_RAW[L + "_cmp"] + 2 + RAW)
                for r in range(2):
                    run(hid[:, r, :], bank[6 + r][:, 0:N_CMP], ACT.Gelu_apprx_tanh).then_inc(S("hid_ready"), 1)
                high(L + "_out", 0)
                high(L + "_out", 1)
                b = take("att", 8)

                def exps(u):
                    act.wait_ge(S("att_max"), b + u + 1)
                    if u >= 2:
                        act.wait_ge(S("att_flips"), b + u - 1)
                    for r in range(2):
                        run(sbP[:, u % 2, r * T:(r + 1) * T], sbS[:, u % 2, r * T:(r + 1) * T], ACT.Exp,
                            bias=stat[:, u % 2, 3 + r:4 + r], scale=0.125, accum_out=stat[:, u % 2, 6 + r:7 + r])
                    run(sbPC[:, u % 2, 0:N_CMP], sbPC[:, u % 2, 0:N_CMP], ACT.Exp,
                        bias=stat[:, u % 2, 5:6], scale=0.125).then_inc(S("att_exp"), 1)

                def copies(u):
                    act.wait_ge(S("att_flips"), b + u + 1)
                    if u >= 2:
                        act.wait_ge(S("att_prod"), b + u - 1)
                    run(sbPCT[0:N_CMP, u % 2, :], bank[2 + u % 2][0:N_CMP, P:2 * P], ACT.Copy)
                    run(sbPT[:, u % 2, :], bank[4 + u % 2][:, :], ACT.Copy).then_inc(S("att_turned"), 1)

                exps(0)
                for u in range(8):
                    if u < 7:
                        exps(u + 1)
                    copies(u)
                y = take("ssd", HEADS)
                for hh in range(HEADS):
                    act.wait_ge(S("ssd_diff"), y + hh + 1)
                    if hh >= 2:
                        act.wait_ge(S("ssd_y"), y + hh - 1)
                    run(sbP[:, hh % 2, 0:384], sbS[:, hh % 2, 0:384], ACT.Exp).then_inc(S("ssd_exp"), 1)
                o = take("ssd_out", 4)
                one = square(4, lambda k: yss[:, k, :], T)
                for k in range(4):
                    act.wait_ge(S("ssd_out"), o + k + 1)
                    one(k)
                high_y = take("ssd_scaled", 4)
                for k in range(4):
                    act.wait_ge(S("ssd_scaled"), high_y + k + 1)
                    run(h_thin[0][:, k, :], yss[:, k, :], ACT.Copy).then_inc(S("ssd_high"), 1)
                project(L + "_out", T, L + "_up")

            act.wait_ge(S("fills"), 5)
            act.wait_ge(S("params_in"), 16)
            run(cond[:, :, :], par("cond").rearrange("p (k s) -> p k s", s=2), ACT.Silu).then_inc(S("cond_act"), 1)
            high("mod", 0)
            high("mod", 1)

            def mod_row_copy(n, j, i, ahead):
                panel_done("mod", n)
                if not (fixed(n) and n < 2):
                    act.wait_ge(S("mod_cols"), n - 1)
                run(mod_row[0:4, j % 2, :], bank[j % 2][0:4, 0:MODW], ACT.Copy).then_inc(S("mod_row"), 1)
                ahead()

            sweep("mod", MOD_PANELS, mod_row_copy, "l0_in", defer=True)
            act.wait_ge(S("x_in"), 16)
            one = square(KD, lambda k: res[:, k, 0:T], T)
            for k in range(KD):
                one(k)
            for l in range(LAYERS):
                mixers(l)
                ffn1(l, f"l{l + 1}_in" if l + 1 < LAYERS else "m0a_up0")
            act.wait_ge(S("ctx_in"), 16)
            one = square(KD, lambda k: res[:, k, :], 2 * T)
            for k in range(KD):
                act.wait_ge(S("final1"), k + 1)
                one(k)
            ffn2("m0a", 2 * T, (0, 0), "mla_down")
            high_input(2 * T, (0, 3))
            high("mla_down", 1)
            for n in range(4):
                if n < 2:
                    panel_done("mla_down", n)
                    high("mla_down", n + 2)
                panel_done("mla_down", n)
                for t in range(2 if n < 3 else 1):
                    last = run(dpj[:, 2 * n + t, :], bank[2 * (n % 2) + t][:, :], ACT.Copy)
                last.then_inc(S("lat_evac"), 1)
            act.wait_ge(S("lat_evac"), 4)
            for at0, K in ((0, 4), (4, 2)):
                if at0:
                    act.wait_ge(S("lat_normed"), 4)
                one = square(K, lambda k: dpj[:, at0 + k, :], 2 * T)
                for k in range(K):
                    one(k)

            def pair_evac(p):
                qn, qr, qrot, kn, vv = pairs[p % 2]
                dst = [qn[:, 0, :], qn[:, 1, :], qr, kn[:, 0, :], kn[:, 1, :], vv[:, 0:2, :], vv[:, 2:4, :]]
                for t in range(7):
                    if t == 2:
                        act.wait_ge(S("raw_free"), FIRST_RAW["mla_pair"] + 2 * p + 1 + RAW)
                    elif t == 6:
                        act.wait_ge(S("raw_free"), FIRST_RAW["mla_pair"] + 2 * p + 2 + RAW)
                    else:
                        act.wait_ge(S("pair_tile"), 5 * p + t + (1 if t < 2 else 0))
                    src = bank[2 + t % 2][:, :]
                    if t >= 5:
                        src = src.rearrange("p (a t) -> p a t", a=2)
                    run(dst[t], src, ACT.Copy).then_inc(S("pair_evac"), 1)

            def attention(b, units, width, scores_at, scale, between=None):
                def exps(u):
                    act.wait_ge(S("att_max"), b + u + 1)
                    if u >= 2:
                        act.wait_ge(S("att_flips"), b + u - 1)
                    W = width(u)
                    run(sbP[:, u % 2, 0:W], scores_at(u)[:, 0:W], ACT.Exp, bias=stat[:, u % 2, 1:2], scale=scale,
                        accum_out=stat[:, u % 2, 2:3]).then_inc(S("att_exp"), 1)

                def copies(u):
                    act.wait_ge(S("att_flips"), b + u + 1)
                    if u >= 2:
                        act.wait_ge(S("att_prod"), b + u - 1)
                    W = width(u)
                    run(sbPT[:, u % 2, 0:W], bank[4 + u % 2][:, 0:W], ACT.Copy).then_inc(S("att_turned"), 1)

                exps(0)
                for u in range(units):
                    if between:
                        between(u)
                    if u < units - 1:
                        exps(u + 1)
                    copies(u)

            pair_evac(0)
            attention(take("att", 32), 32, lambda u: 512 if u % 4 < 2 else 256, lambda u: bank[u % 2], 192 ** -0.5,
                      lambda u: (pair_evac(u // 8 + 1) if u % 8 == 1 and u // 8 < 3
                                 else (high("mla_o", 0), high("mla_o", 1)) if u == 28 else None))
            project("mla_o", 2 * T, "m0b_up0")
            ffn2("m0b", 2 * T, (0, 6), "m1a_up0")
            ffn2("m1a", 2 * T, (1, 0), "swa_qkv")
            high_input(2 * T, (1, 3))
            high("swa_qkv", 1)
            for n in range(7):
                panel_done("swa_qkv", n)
                if n < 4:
                    last = run(sq_q[:, 2 * n:2 * n + 2, :], bank[n % 2][:, :].rearrange("p (a t) -> p a t", a=2), ACT.Copy)
                elif n < 6:
                    for t in range(2):
                        last = run(sq_k[:, 2 * (n - 4) + t, :], bank[2 * (n % 2) + t][:, :], ACT.Copy)
                else:
                    for t in range(2):
                        last = run(sq_v[:, 2 * t:2 * t + 2, :], bank[4 + t][:, :].rearrange("p (a t) -> p a t", a=2),
                                   ACT.Copy)
                last.then_inc(S("swa_evac"), 1)
                high(*(("swa_qkv", n + 2) if n < 5 else ("swa_o", n - 5)))
            b = take("att", 32)

            def swa_exps(u):
                act.wait_ge(S("att_max"), b + u + 1)
                if u >= 2:
                    act.wait_ge(S("att_flips"), b + u - 1)
                run(sbP[:, u % 2, :], sbS[:, u % 2, :], ACT.Exp, bias=stat[:, u % 2, 1:2], scale=0.125,
                    accum_out=stat[:, u % 2, 2:3])
                run(stat[:, u % 2, 3:4], par("sink", u // 2, u // 2 + 1), ACT.Exp,
                    bias=stat[:, u % 2, 1:2]).then_inc(S("att_exp"), 1)

            def swa_copies(u):
                act.wait_ge(S("att_flips"), b + u + 1)
                if u >= 2:
                    act.wait_ge(S("att_prod"), b + u - 1)
                run(sbPT[:, u % 2, :], bank[4 + u % 2][:, :], ACT.Copy).then_inc(S("att_turned"), 1)

            swa_exps(0)
            for u in range(32):
                if u < 31:
                    swa_exps(u + 1)
                swa_copies(u)
            project("swa_o", T, "m1b_up")
            ffn2("m1b", T, (1, 6), None)

        @block.vector
        def _(dve):
            take = Tally().take
            link = Chain(dve, S("dve_step"))
            V = nc.vector

            def panel_done(name, n):
                dve.wait_ge(S("panels_used"), n + (FIRST_SPLIT[name] + 1))

            def low(name, j, i=0):
                dve.wait_ge(S("high"), i * RAW + (FIRST_SPLIT[name] + j + 1))
                w, s = WIDTH[name], half_slot(name, j)
                V.tensor_tensor(w_lo[s][:, 0:w], raw[raw_slot(name, j)][:, 0:w], w_hi[s][:, 0:w].bitcast(F32),
                                ALU.subtract).then_inc(S("raw_free"), 1)

            def sweep(name, count, body, after=None, defer=False, loop=True, chain=None, links=0):
                def step(n, j, i):
                    def ahead():
                        if not fixed(n) or n + 2 < count:
                            low(name, j + 2, i)
                        elif after and (n == count - 2 or not defer):
                            low(after, n + 2 - count)
                    body(n, j, i, ahead)

                if loop:
                    turns(dve, count, RAW, step, peel=1, tail=2, chain=chain, links=links)
                else:
                    for n in range(count):
                        step(n, n, 0)

            def rms(K, N):
                c = take("rms_done", 1)
                dve.wait_ge(S("rms_done"), c + 1)
                link(V.reciprocal(rstd[:, 0:N], rstd[:, 0:N]))

            def low_input(N, gain, shift=None, K=KD):
                rms(K, N)
                per = N // T
                b = take("norm_high", K * per)
                done = take("norm_split", K * per) + K * per
                h, hl = h_of(N)
                at_ = [(k, s, at) for k in range(K) for s, at in streams(N)]
                for n in range(len(at_) + 2):
                    if n < len(at_):
                        k, s, at = at_[n]
                        V.scalar_tensor_tensor(normed_f[:, k, at:at + T], res[:, k, at:at + T], gain(k, s),
                                               rstd[:, at:at + T], ALU.mult, ALU.mult).then_inc(S("norm_scaled"), 1)
                    if n >= 2:
                        k, s, at = at_[n - 2]
                        dve.wait_ge(S("norm_high"), b + n - 1)
                        f, hi, lo = (x[:, k, at:at + T] for x in (normed_f, h, hl))
                        if shift:
                            ins = V.scalar_tensor_tensor(lo, f, mod(*shift, k, s), hi.bitcast(F32), ALU.add, ALU.subtract)
                        else:
                            ins = V.tensor_tensor(lo, f, hi.bitcast(F32), ALU.subtract)
                        ins.then_inc(S("norm_split"), 1)
                return done

            def normed(K, N, src, dst, gain, sem):
                rms(K, N)
                for k in range(K):
                    V.scalar_tensor_tensor(dst(k), src(k), gain(k), rstd[:, 0:N], ALU.mult,
                                           ALU.mult).then_inc(S(sem), 1)

            def split(hi, lo, src):
                link(V.tensor_copy(hi, src))
                return V.tensor_tensor(lo, src, hi.bitcast(F32), ALU.subtract)

            def residual_plain(k, src):
                return V.tensor_tensor(res[:, k, 0:T], src, res[:, k, 0:T], ALU.add)

            def residual_mod(k, b, l, c, N):
                for s, at in streams(N):
                    last = V.scalar_tensor_tensor(res[:, k, at:at + T], bank[b][:, at:at + T], mod(l, c, k, s),
                                                  res[:, k, at:at + T], ALU.mult, ALU.add)
                return last

            def add_tile(k, N, gate_of):
                b = 4 + k % 2
                ins = residual_mod(k, b, *gate_of, N) if gate_of else residual_plain(k, bank[b][:, 0:N])
                ins.then_inc(S("res_done"), 1)

            def project(name, N, after, gate_of=None):
                hp = take("half_panel", KD // 2)

                def body(n, j, i, ahead):
                    dve.wait_ge(S("half_panel"), hp + n + 1)
                    add_tile(2 * n, N, gate_of)
                    panel_done(name, n)
                    add_tile(2 * n + 1, N, gate_of)
                    ahead()

                sweep(name, KD // 2, body, after, defer=True, loop=False)

            def down(name, N, after, gate_of=None, last=True):
                per = 2 * T // N

                def body(n, j, i, ahead):
                    if n % per == per - 1:
                        panel_done(name, n)
                        add_tile(n // per, N, gate_of)
                    ahead()

                sweep(name, KD * per, body, after, defer=last, loop=False)

            def ffn1(l, after):
                name = f"l{l}"
                low_input(T, lambda k, s: par(f"ffn_norm{l}", k, k + 1))
                low(name + "_up", 1)
                link(V.memset(ucv[:, :, :, 0:2], 0.0))
                ub = take("up_evac", FF1_TILES)
                ga = take("gate_act", FF1_TILES)
                mb = take("ff_mid", FF1_TILES)
                w0 = PARAMS[f"ffn_conv{l}"][0]
                fh, fl = hidden(f_hi, T), hidden(f_lo, T)

                def tile(n, j, i, ahead):
                    dve.wait_ge(S("up_evac"), n + (ub + 1))
                    for tap in (1, 0):
                        for half in (1, 0):
                            c = cva[:, j % 2, half, :]
                            w = params[:, bass.ds(n * 8 + (w0 + 4 * half + tap), 1)]
                            ins = V.scalar_tensor_tensor(c, ucv[:, j % 2, half, tap:tap + T], w, c, ALU.mult, ALU.add)
                            if tap:
                                ins.then_inc(S("dve_tap"), 1)
                            elif half:
                                ins.then_inc(S("dve_tap"), 1)
                            else:
                                ins.then_inc(S("gate_ready"), 1)
                            if half:
                                continue
                        if tap:
                            dve.wait_ge(S("dve_tap"), n * 3 + (3 * mb + 2))
                    ahead()
                    dve.wait_ge(S("dve_tap"), n * 3 + (3 * mb + 3))
                    dve.wait_ge(S("gate_act"), n + (ga + 1))
                    if not (fixed(n) and n == 0):
                        dve.wait_ge(S("ff_mid"), n + mb)
                    v, g = cva[:, j % 2, 1, :], sil[:, j % 2, 0:T]
                    V.tensor_tensor(prod[:, 0:T], g, v, ALU.mult)
                    link(V.tensor_tensor(fh[:, bass.ds(n, 1), :], g.unsqueeze(1), v.unsqueeze(1), ALU.mult))
                    V.tensor_tensor(fl[:, bass.ds(n, 1), :], prod[:, 0:T].unsqueeze(1),
                                    fh[:, bass.ds(n, 1), :].bitcast(F32), ALU.subtract).then_inc(S("ff_mid"), 1)

                sweep(name + "_up", FF1_TILES, tile, name + "_down", chain=link, links=1)
                down(name + "_down", T, after)

            def up2(name, count, N, after):
                ga = take("gate_act", count)
                mb = take("ff_mid", count)
                fh, fl = hidden(f_hi, N), hidden(f_lo, N)

                def tile(n, j, i, ahead):
                    dve.wait_ge(S("gate_act"), n + (ga + 1))
                    if not (fixed(n) and n == 0):
                        dve.wait_ge(S("ff_mid"), n + mb)
                    v, g = bank[2 * (j % 2) + 1][:, 0:N], sil[:, j % 2, 0:N]
                    V.tensor_tensor(prod[:, 0:N], g, v, ALU.mult)
                    link(V.tensor_tensor(fh[:, bass.ds(n, 1), :], g.unsqueeze(1), v.unsqueeze(1), ALU.mult))
                    V.tensor_tensor(fl[:, bass.ds(n, 1), :], prod[:, 0:N].unsqueeze(1),
                                    fh[:, bass.ds(n, 1), :].bitcast(F32), ALU.subtract).then_inc(S("ff_mid"), 1)
                    ahead()

                sweep(name, count, tile, after, chain=link, links=1)

            def ffn2(name, N, l, c, after):
                low_input(N, lambda k, s: mod(l, c - 1, k, s), (l, c - 2))
                if N == T:
                    low(name + "_up", 1)
                    up2(name + "_up", FF2_TILES, N, name + "_down")
                    down(name + "_down", N, after, (l, c))
                    return
                low(name + "_up0", 1)
                up2(name + "_up0", HALF_FF, N, name + "_down0")
                down(name + "_down0", N, name + "_up1", (l, c), last=False)
                up2(name + "_up1", HALF_FF, N, name + "_down1")
                down(name + "_down1", N, after, (l, c))

            def rope(out, x, rot, cos, sin, n, sem, work):
                r = work[:, 0, 0:n * T].rearrange("p (a t) -> p a t", a=n)
                c = cos.unsqueeze(1).to_broadcast([P, n, T]) if n > 1 else cos.unsqueeze(1)
                s = sin.unsqueeze(1).to_broadcast([P, n, T]) if n > 1 else sin.unsqueeze(1)
                link(V.tensor_tensor(r, rot, s, ALU.mult))
                x2 = work[:, 1, 0:n * T].rearrange("p (a t) -> p a t", a=n)
                link(V.tensor_tensor(x2, x, c, ALU.mult))
                V.tensor_tensor(out, r, x2, ALU.add).then_inc(S(sem), 1)
                dve.wait_ge(S(sem), take(sem, 1) + 1)

            def mixers(l):
                split_done = low_input(T, lambda k, s: par(f"attn_norm{l}", k, k + 1))
                low(f"l{l}_in", 1)
                e = take("in_evac", 13)
                dve.wait_ge(S("norm_split"), split_done)
                link(V.memset(U[:, U_SCC:U_Z, 0:PAD], 0.0))
                sweep(f"l{l}_in", 13, lambda n, j, i, ahead: ahead())
                dve.wait_ge(S("in_evac"), e + 1)
                x = dtw[:, 2, :]
                b2 = par(f"dt_bias{l}").unsqueeze(1).to_broadcast([P, 2, HEADS])
                link(V.tensor_tensor(x.rearrange("p (b h) -> p b h", b=2), tm[:, :, 0:HEADS], b2, ALU.add))
                V.scalar_tensor_tensor(dtw[:, 0, :], x, -1.0, x, ALU.mult, ALU.max).then_inc(S("dt_raw"), 1)
                ro = take("rotated", 1)
                xb = dtw
                dve.wait_ge(S("in_evac"), e + 13)
                for t in range(8):
                    c = xc[:, t, :]
                    w = par(f"conv_w{l}", 4 * t, 4 * t + 4)
                    u = U[:, U_XBC + t, :]
                    link(V.tensor_scalar(c, u[:, 3:3 + T], w[:, 3:4], par(f"conv_b{l}", t, t + 1), ALU.mult, ALU.add))
                    link(V.scalar_tensor_tensor(c, u[:, 2:2 + T], w[:, 2:3], c, ALU.mult, ALU.add))
                    link(V.scalar_tensor_tensor(c, u[:, 1:1 + T], w[:, 1:2], c, ALU.mult, ALU.add))
                    V.scalar_tensor_tensor(c, u[:, 0:T], w[:, 0:1], c, ALU.mult, ALU.add).then_inc(S("xbc_conv"), 1)
                de = take("dt_exp", 3)
                dve.wait_ge(S("dt_exp"), de + 3)
                ex, z, z2, p, dt = (dtw[:, i, :] for i in (1, 3, 4, 5, 6))
                link(V.tensor_scalar(z, ex, 2.0, None, ALU.add))
                link(V.reciprocal(z, z))
                link(V.tensor_tensor(z, z, ex, ALU.mult))
                link(V.tensor_tensor(z2, z, z, ALU.mult))
                link(V.tensor_scalar(p, z2, 1.0 / 17, None, ALU.mult))
                for c in (15, 13, 11, 9, 7, 5, 3):
                    link(V.scalar_tensor_tensor(p, p, 1.0 / c, z2, ALU.add, ALU.mult))
                link(V.scalar_tensor_tensor(p, p, 1.0, z, ALU.add, ALU.mult))
                link(V.tensor_scalar(x, x, 0.0, None, ALU.max))
                link(V.scalar_tensor_tensor(dt, p, 2.0, x, ALU.mult, ALU.add))
                e2 = ea[:, :].unsqueeze(1).to_broadcast([P, 2, HEADS])
                V.scalar_tensor_tensor(dtw[:, 7, :].rearrange("p (b h) -> p b h", b=2),
                                       dt.rearrange("p (b h) -> p b h", b=2), -1.0, e2, ALU.mult,
                                       ALU.mult).then_inc(S("dt_ready"), 1)
                link(V.tensor_scalar(gate[:, :, :], gate[:, :, :], 1.0, None, ALU.add))
                link(V.reciprocal(gate[:, :, :], gate[:, :, :]))
                dve.wait_ge(S("rotated"), ro + 1)
                for lo, n, b, out in ((0, 2, 2, None), (2, 2, 3, None), (4, 1, 4, None)):
                    r = bank[b][:, 0:n * T].rearrange("p (a t) -> p a t", a=n)
                    sin = con("sin1").unsqueeze(1).to_broadcast([P, n, T])
                    cos = con("cos1").unsqueeze(1).to_broadcast([P, n, T])
                    rs = ropet[:, 0, 0:n * T].rearrange("p (a t) -> p a t", a=n)
                    xs = ropet[:, 1, 0:n * T].rearrange("p (a t) -> p a t", a=n)
                    link(V.tensor_tensor(rs, r, sin, ALU.mult))
                    link(V.tensor_tensor(xs, U[:, lo:lo + n, PAD:UW], cos, ALU.mult))
                    if lo == 0:
                        link(V.tensor_tensor(kvr[0:64, :], rs[0:64, 0, :], xs[0:64, 0, :], ALU.add))
                        link(V.tensor_copy(kvr[64:128, :], U[64:128, U_KCVC, PAD:UW]))
                        link(V.tensor_tensor(krq[:, 0, :], rs[:, 1, :], xs[:, 1, :], ALU.add))
                    else:
                        link(V.tensor_tensor(krq[:, lo - 1:lo - 1 + n, :], rs, xs, ALU.add))
                tok = kvr[:, :].rearrange("p (n j) -> p j n", j=CMP_STRIDE)
                pos = par(f"pos{l}")
                for half in range(2):
                    ph = pos[:, 16 * half:16 * half + 16].unsqueeze(2).to_broadcast([P, 16, N_CMP])
                    ins = V.tensor_tensor(tpos[:, 16 * half:16 * half + 16, :], tok[:, :, half:half + N_CMP], ph, ALU.add)
                    if half:
                        ins.then_inc(S("tpos_ready"), 1)
                cu = take("cumulated", 1)
                dve.wait_ge(S("cumulated"), cu + 1)
                V.tensor_copy(acs[:, :, :], bank[5][:, 0:16].rearrange("p (b h) -> p b h", b=2))
                link(V.tensor_copy(acsT[:, :], bank[5][0:HEADS, T:2 * T]))
                ck = take("cmp_kv", 1)
                dve.wait_ge(S("cmp_kv"), ck + 1)
                V.tensor_copy(kc[:, :], bank[6][:, 0:N_CMP])
                link(V.tensor_copy(vc[:, :], bank[6][0:N_CMP, 64:128]))
                xt = take("x_turned", 1)
                dve.wait_ge(S("x_turned"), xt + 1)
                for tb in range(2):
                    d8 = dt.rearrange("p (b h) -> p b h", b=2)[:, tb, :].unsqueeze(2).to_broadcast([P, HEADS, 64])
                    V.tensor_tensor(xdt[:, tb, :].rearrange("p (h d) -> p h d", h=HEADS),
                                    bank[2 + tb][:, :].rearrange("p (h d) -> p h d", h=HEADS), d8, ALU.mult)
                cb = take("cb_ready", 1)
                dve.wait_ge(S("cb_ready"), cb + 1)
                for g in range(GROUPS):
                    last = V.tensor_copy(cbT[:, g, :], bank[g][:, 0:384])
                last.then_inc(S("ssm_start"), 1)
                for t in range(2):
                    cc = U[:, U_SCC + t, :]
                    w = par(f"sc_w{l}", 3 * t, 3 * t + 3)
                    o = sct[:, t, :]
                    link(V.tensor_tensor(cc[:, PAD:UW], cc[:, PAD:UW], U[:, U_SCH + t, PAD:UW], ALU.mult))
                    link(V.tensor_scalar(o, cc[:, 3:3 + T], w[:, 2:3], None, ALU.mult))
                    link(V.scalar_tensor_tensor(o, cc[:, 2:2 + T], w[:, 1:2], o, ALU.mult, ALU.add))
                    link(V.scalar_tensor_tensor(o, cc[:, 1:1 + T], w[:, 0:1], o, ALU.mult, ALU.add))
                    link(V.tensor_tensor(o, o, U[:, U_SCB + t, PAD:UW], ALU.mult))
                    split(h_thin[0][:, 4 + t, :], h_thin[1][:, 4 + t, :], o).then_inc(S("mixed"), 1)
                low(f"l{l}_out", 0)
                low(f"l{l}_out", 1)
                b = take("att", 8)
                causal = con("causal").rearrange("p (b t) -> p b t", b=2)
                cadd = con("cmp_add").rearrange("p (b t) -> p b t", b=2)
                keep = con("cmp_keep").rearrange("p (b t) -> p b t", b=2)

                def maxes(u):
                    dve.wait_ge(S("att_scores"), b + u + 1)
                    s, q = stat[:, u % 2, :], u % 2
                    for r in range(2):
                        V.tensor_tensor_reduce(sbS[:, q, r * T:(r + 1) * T], bank[q][:, r * T:(r + 1) * T],
                                               causal[:, u % 2, :], 1.0, -3e38, ALU.add, ALU.max, s[:, r:r + 1])
                    link(V.tensor_tensor_reduce(sbPC[:, q, 0:N_CMP], bank[2 + q][:, 0:N_CMP], cadd[:, u % 2, 0:N_CMP],
                                                1.0, -3e38, ALU.add, ALU.max, s[:, 2:3]))
                    V.tensor_scalar(s[:, 3:6], s[:, 0:3], -0.125, None, ALU.mult).then_inc(S("att_max"), 1)

                def probs(u):
                    dve.wait_ge(S("att_exp"), b + u + 1)
                    s, q, hh = stat[:, u % 2, :], u % 2, u // 2
                    link(V.tensor_tensor_reduce(sbPC[:, q, 0:N_CMP], sbPC[:, q, 0:N_CMP], keep[:, u % 2, 0:N_CMP],
                                                1.0, 0.0, ALU.mult, ALU.add, s[:, 8:9]))
                    link(V.tensor_scalar(s[:, 8:9], s[:, 8:9], 1e-20, None, ALU.max))
                    link(V.reciprocal(s[:, 9:12], s[:, 6:9]))
                    g = gate[:, u % 2, 3 * hh:3 * hh + 3]
                    V.tensor_tensor(s[:, 12:14], s[:, 9:11], g[:, 1:3], ALU.mult)
                    link(V.tensor_tensor(s[:, 14:15], s[:, 11:12], g[:, 0:1], ALU.mult))
                    V.tensor_scalar(sbPC[:, q, 0:N_CMP], sbPC[:, q, 0:N_CMP], s[:, 14:15], None, ALU.mult)
                    V.tensor_scalar(sbP[:, q, 0:T], sbP[:, q, 0:T], s[:, 12:13], None, ALU.mult)
                    V.tensor_scalar(sbP[:, q, T:2 * T], sbP[:, q, T:2 * T], s[:, 13:14], None,
                                    ALU.mult).then_inc(S("att_probs"), 1)

                def outs(u):
                    dve.wait_ge(S("att_prod"), b + u + 1)
                    hh = u // 2
                    rows = slice(64 * (hh % 2), 64 * (hh % 2) + 64)
                    hi, lo = (x[rows, 6 + hh // 2, (u % 2) * P:(u % 2 + 1) * P] for x in h_thin)
                    split(hi, lo, bank[6 + u % 2][rows, 0:P]).then_inc(S("att_out"), 1)

                maxes(0)
                for u in range(9):
                    if u < 7:
                        maxes(u + 1)
                    if u < 8:
                        probs(u)
                    if u >= 1:
                        outs(u - 1)
                y = take("ssd", HEADS)
                mask = con("decay_mask")

                def diff(hh):
                    dve.wait_ge(S("ssd_spread"), y + hh + 1)
                    if hh >= 2:
                        dve.wait_ge(S("ssd_exp"), y + hh - 1)
                    o = sbS[:, hh % 2, :]
                    V.scalar_tensor_tensor(o[:, 0:T], bank[hh % 2][:, 0:T], acs[:, 0, hh:hh + 1], mask[:, 0:T],
                                           ALU.subtract, ALU.add)
                    V.scalar_tensor_tensor(o[:, T:384], bank[hh % 2][:, P:T], acs[:, 1, hh:hh + 1], mask[:, T:384],
                                           ALU.subtract, ALU.add).then_inc(S("ssd_diff"), 1)

                def mats(hh):
                    dve.wait_ge(S("ssd_exp"), y + hh + 1)
                    V.tensor_tensor(sbP[:, hh % 2, 0:384], sbP[:, hh % 2, 0:384], cbT[:, hh // 4, :],
                                    ALU.mult).then_inc(S("ssd_mat"), 1)

                def out(t):
                    dve.wait_ge(S("ssd_y"), y + 2 * t + 2)
                    link(V.scalar_tensor_tensor(yss[:, t, :], xc[:, t, :], par(f"d_skip{l}", t, t + 1),
                                                bank[2 + t % 2][:, 0:T], ALU.mult, ALU.add))
                    V.tensor_tensor(yss[:, t, :], yss[:, t, :], U[:, U_Z + t, PAD:UW], ALU.mult).then_inc(S("ssd_out"), 1)

                zr = take("z_ready", 1)
                dve.wait_ge(S("z_ready"), zr + 1)
                diff(0)
                for hh in range(HEADS):
                    if hh + 1 < HEADS:
                        diff(hh + 1)
                    mats(hh)
                    if hh % 2 == 0 and hh:
                        out(hh // 2 - 1)
                out(3)
                rms(4, T)
                y2 = take("ssd_high", 4)
                for k in range(4):
                    V.scalar_tensor_tensor(yss[:, k, :], yss[:, k, :], par(f"ssd_norm{l}", k, k + 1), rstd[:, 0:T],
                                           ALU.mult, ALU.mult).then_inc(S("ssd_scaled"), 1)
                for k in range(4):
                    dve.wait_ge(S("ssd_high"), y2 + k + 1)
                    V.tensor_tensor(h_thin[1][:, k, :], yss[:, k, :], h_thin[0][:, k, :].bitcast(F32),
                                    ALU.subtract).then_inc(S("mixed"), 1)
                project(f"l{l}_out", T, f"l{l}_up")

            dve.wait_ge(S("params_in"), 16)
            dve.wait_ge(S("consts_in"), 16)
            mb = PARAMS["mod_b"][0]

            dve.wait_ge(S("fills"), 5)
            dve.wait_ge(S("cond_act"), 1)
            split(cond_w[:, :, 0:2], cond_w[:, :, 2:4], cond[:, :, :]).then_inc(S("cond_ready"), 1)
            low("mod", 0)
            low("mod", 1)

            def mod_vec(n, j, i, ahead):
                if not (fixed(n) and n == MOD_PANELS):
                    dve.wait_ge(S("panels_used"), n + 1)
                ahead()
                if fixed(n) and n == 0:
                    return
                dve.wait_ge(S("mod_cols"), n)
                V.tensor_tensor(modT[:, bass.ds(n * 2 - 2, 2), :],
                                bank[2 + (j - 1) % 2][:, 0:4].rearrange("p (q s) -> p q s", s=2),
                                params[:, bass.ds(n * 2 + (mb - 2), 2)].unsqueeze(2).to_broadcast([P, 2, 2]),
                                ALU.add).then_inc(S("mod_vec"), 1)

            sweep("mod", MOD_PANELS, mod_vec, "l0_in", defer=True)
            mod_vec(MOD_PANELS, 0, 0, lambda: None)
            dve.wait_ge(S("mod_vec"), MOD_PANELS + 2)
            for l in range(LAYERS):
                for j in range(3):
                    q = (l * N_MOD + 3 * j + 1) * KD
                    g = par("mod_norm", (3 * l + j) * KD, (3 * l + j + 1) * KD).unsqueeze(2).to_broadcast([P, KD, 2])
                    link(V.scalar_tensor_tensor(modT[:, q:q + KD, :], modT[:, q:q + KD, :], 1.0, g, ALU.add, ALU.mult))
                    if j != 1:
                        link(V.tensor_scalar(modT[:, q + KD:q + 2 * KD, :], modT[:, q + KD:q + 2 * KD, :], 0.5, None,
                                             ALU.mult))
            dve.wait_ge(S("x_in"), 16)
            dve.wait_ge(S("ctx_in"), 16)
            for l in range(LAYERS):
                mixers(l)
                ffn1(l, f"l{l + 1}_in" if l + 1 < LAYERS else "m0a_up0")
            normed(KD, T, lambda k: res[:, k, 0:T], lambda k: res[:, k, 0:T], lambda k: par("final1", k, k + 1), "final1")
            ffn2("m0a", 2 * T, 0, 2, "mla_down")
            low_input(2 * T, lambda k, s: mod(0, 4, k, s), (0, 3))
            for n in range(1, 4):
                low("mla_down", n)
            dve.wait_ge(S("rotated"), LAYERS + 1)
            rope(dpj[:, 6:7, 0:T], dpj[:, 6:7, 0:T], bank[4][:, 0:T].unsqueeze(1), con("cos2"), con("sin2"), 1,
                 "key_rope", ropes)
            normed(4, 2 * T, lambda k: dpj[:, k, :], lambda k: dpj[:, k, :], lambda k: par("q_norm", k, k + 1), "lat_normed")
            dve.wait_ge(S("lat_normed"), 4)
            normed(2, 2 * T, lambda k: dpj[:, 4 + k, :], lambda k: dpj[:, 4 + k, :],
                   lambda k: par("kv_norm", k, k + 1), "lat_normed")

            def pair_rope(p):
                qn, qr, qrot, kn, vv = pairs[p % 2]
                dve.wait_ge(S("pair_rot"), p + 1)
                rope(qrot.unsqueeze(1), qr[:, 0:T].unsqueeze(1), bank[3][:, 0:T].unsqueeze(1), con("cos2"), con("sin2"),
                     1, "pair_rope", ropes)

            def attention(units, maxes, total, outs, width, between=None):
                b = take("att", units)

                def probs(u):
                    dve.wait_ge(S("att_exp"), b + u + 1)
                    W, q = width(u), u % 2
                    link(V.reciprocal(stat[:, q, 4:5], total(u)))
                    V.tensor_scalar(sbP[:, q, 0:W], sbP[:, q, 0:W], stat[:, q, 4:5], None,
                                    ALU.mult).then_inc(S("att_probs"), 1)

                maxes(0, b)
                for u in range(units + 1):
                    if between:
                        between(u)
                    if u < units - 1:
                        maxes(u + 1, b)
                    if u < units:
                        probs(u)
                    if u >= 1:
                        outs(u - 1, b)

            def mla_max(u, b):
                dve.wait_ge(S("att_scores"), b + u + 1)
                q = u % 2
                link(V.tensor_reduce(stat[:, q, 0:1], bank[q][:, 0:512 if u % 4 < 2 else 256], AXX, ALU.max))
                V.tensor_scalar(stat[:, q, 1:2], stat[:, q, 0:1], -(192 ** -0.5), None, ALU.mult).then_inc(S("att_max"), 1)

            def mla_out(u, b):
                dve.wait_ge(S("att_prod"), b + u + 1)
                hi, lo = (x[:, u // 4, (u % 4) * P:(u % 4 + 1) * P] for x in h_wide)
                split(hi, lo, bank[6 + u % 2][:, 0:P]).then_inc(S("att_out"), 1)

            pair_rope(0)
            attention(32, mla_max, lambda u: stat[:, u % 2, 2:3], mla_out, lambda u: 512 if u % 4 < 2 else 256,
                      lambda u: (pair_rope(u // 8 + 1) if u % 8 == 3 and u // 8 < 3
                                 else (low("mla_o", 0), low("mla_o", 1)) if u == 29 else None))
            project("mla_o", 2 * T, "m0b_up0", (0, 5))
            ffn2("m0b", 2 * T, 0, 8, "m1a_up0")
            ffn2("m1a", 2 * T, 1, 2, "swa_qkv")
            low_input(2 * T, lambda k, s: mod(1, 4, k, s), (1, 3))
            for n in range(1, 7):
                low("swa_qkv", n)
            low("swa_o", 0)
            low("swa_o", 1)
            for g in range(6):
                dve.wait_ge(S("swa_rot"), g + 1)
                rot = bank[6 + g % 2][:, :].rearrange("p (a t) -> p a t", a=2)
                if g < 4:
                    src, dst = sq_q[:, 2 * g:2 * g + 2, :], sq_qrot[:, 2 * g:2 * g + 2, :]
                else:
                    src = dst = sq_k[:, 2 * (g - 4):2 * (g - 4) + 2, 0:T]
                rope(dst, src, rot, con("cos2"), con("sin2"), 2, "swa_rope", ropet)
            window = con("window").rearrange("p (b t) -> p b t", b=2)

            def swa_max(u, b):
                dve.wait_ge(S("att_scores"), b + u + 1)
                q = u % 2
                s = stat[:, q, :]
                V.tensor_tensor_reduce(sbS[:, q, 0:T], bank[q][:, 0:T], window[:, u % 2, :], 1.0, -3e38, ALU.add,
                                       ALU.max, s[:, 5:6])
                V.tensor_copy(sbS[:, q, T:2 * T], bank[q][:, T:2 * T])
                link(V.tensor_reduce(s[:, 6:7], bank[q][:, T:2 * T], AXX, ALU.max))
                link(V.tensor_tensor(s[:, 0:1], s[:, 5:6], s[:, 6:7], ALU.max))
                link(V.tensor_scalar(s[:, 0:1], s[:, 0:1], 0.125, par("sink", u // 2, u // 2 + 1), ALU.mult, ALU.max))
                V.tensor_scalar(s[:, 1:2], s[:, 0:1], -1.0, None, ALU.mult).then_inc(S("att_max"), 1)

            def swa_total(u):
                s = stat[:, u % 2, :]
                link(V.tensor_tensor(s[:, 7:8], s[:, 2:3], s[:, 3:4], ALU.add))
                return s[:, 7:8]

            def swa_out(u, b):
                dve.wait_ge(S("att_prod"), b + u + 1)
                hh = u // 2
                rows = slice(64 * (hh % 2), 64 * (hh % 2) + 64)
                hi, lo = (x[rows, hh // 2, (u % 2) * P:(u % 2 + 1) * P] for x in h_thin)
                split(hi, lo, bank[6 + u % 2][rows, 0:P]).then_inc(S("att_out"), 1)

            attention(32, swa_max, swa_total, swa_out, lambda u: 512)
            project("swa_o", T, "m1b_up", (1, 5))
            ffn2("m1b", T, 1, 8, None)
            normed(KD, T, lambda k: res[:, k, 0:T], lambda k: normed_f[:, k, 0:T], lambda k: par("final2", k, k + 1),
                   "final_out")


def tiles_of(w):
    K, M = w.shape
    k, m = -(-K // P), -(-M // P)
    full = np.zeros((k * P, m * P), np.float32)
    full[:K, :M] = w
    return full.reshape(k, P, m, P).transpose(2, 1, 0, 3)


def pair_panels(t):
    if len(t) % 2:
        t = np.concatenate([t, np.zeros_like(t[:1])])
    n, p, k, m = t.shape
    return t.reshape(n // 2, 2, p, k, m).transpose(0, 2, 1, 3, 4).reshape(n // 2, p, 2 * k * m)


def down_panels(w):
    return tiles_of(w).reshape(KD, P, 2, DOWN).transpose(0, 2, 1, 3).reshape(2 * KD, P, DOWN)


def columns(v):
    v = np.asarray(v)
    n = -(-v.shape[-1] // P) * P
    out = np.zeros(v.shape[:-1] + (n,), np.float32)
    out[..., :v.shape[-1]] = v
    return np.moveaxis(out.reshape(v.shape[:-1] + (n // P, P)), -1, 0)


def constants():
    c = np.zeros((P, CONST_W), np.float32)

    def put(name, v):
        at, w = CONSTS[name]
        v = np.asarray(v, np.float32)
        c[:v.shape[0], at:at + w] = v.reshape(v.shape[0], -1)

    i, t = np.arange(P), np.arange(T)
    put("ident", np.eye(P))
    tok = np.arange(2)[None, :, None] * P + i[:, None, None]
    put("tri", tok <= t)
    put("rot", (i[:, None] ^ 32) == i[None, :])
    f32 = np.float32
    half = 32
    inv1 = f32(1.0) / (f32(10000.0) ** (np.arange(half, dtype=f32) / f32(half)))
    ang1 = t.astype(f32)[:, None] * inv1[None, :]
    n = 16
    inv2 = np.exp(f32(-np.log(10000.0)) * np.arange(n, dtype=f32) / f32(n)).astype(f32)
    ang2 = np.concatenate([(t // 64).astype(f32)[:, None] * inv2, (t % 64).astype(f32)[:, None] * inv2], -1)
    for name, ang in (("1", ang1), ("2", ang2)):
        ang = ang.astype(f32).T
        put("cos" + name, np.tile(np.cos(ang), (4, 1)))
        s = np.sin(ang)
        put("sin" + name, np.concatenate([-s, s, -s, s]))
    put("causal", np.where(t <= tok, 0, NEG))
    m = np.where(tok <= t, 0, NEG)
    put("decay_mask", np.concatenate([m[:, 0], m[:, 1, P:]], -1))
    end = np.arange(16) * CMP_STRIDE + CMP_BLOCK - 1
    put("cmp_add", np.where(end <= tok, 0, NEG))
    put("cmp_keep", end <= tok)
    put("window", np.where(np.abs(t - tok) <= 128, 0, NEG))
    put("fold", np.tile(np.eye(2), (2, 1)))
    return c


def kernel(**inputs):
    import concourse.bacc as bacc
    from concourse.bass_utils import run_bass_kernel_spmd

    a = {k: np.asarray(v) for k, v in inputs.items()}
    par = np.zeros((P, PARAM_W), np.float32)

    def put(name, v):
        at, w = PARAMS[name]
        par[:v.shape[0], at:at + w] = v.reshape(v.shape[0], -1)

    def rows(v):
        return np.broadcast_to(v, (P,) + v.shape)

    w = {}
    w["mod"] = a["mod_w_2"].reshape(LAYERS, KD, P, N_MOD * DM // MODW, MODW).transpose(0, 3, 2, 1, 4).reshape(
        MOD_PANELS, P, KD * MODW)
    for l in range(LAYERS):
        wi = a["w_in"][l]
        cuts = np.cumsum([INNER, XBC, HEADS, SC, SC, SC, 256] + [64] * 6 + [12])
        z, xbc, dt, scb, scc, sch, q, kc, vc, ks, vs, kw, vw, g = np.split(wi, cuts[:-1], axis=1)
        t = tiles_of(np.concatenate([kc, vc, ks, ks, kw, kw, q, scb, scc, sch, xbc, z], axis=1))
        tmw = np.concatenate([dt, vs, vw, g], axis=1).reshape(KD, P, TM).transpose(1, 0, 2).reshape(P, KD * TM)
        tmw = np.concatenate([tmw, np.zeros((P, PANEL - KD * TM), np.float32)], axis=1)
        w[f"l{l}_in"] = np.concatenate([tmw[None], pair_panels(t)])
        kv = np.concatenate([a["cmp_k_w1"][l].reshape(CMP_BLOCK, 64, P), a["cmp_v_w1"][l].reshape(CMP_BLOCK, 64, P)], axis=1)
        w[f"l{l}_cmp"] = kv.reshape(2, 16, P, P).transpose(0, 2, 1, 3).reshape(2, P, 16 * P)
        w[f"l{l}_out"] = pair_panels(tiles_of(a["w_out"][l]))
        g, v = tiles_of(a["ffn_w_up"][l][:, :FF1]), tiles_of(a["ffn_w_up"][l][:, FF1:])
        w[f"l{l}_up"] = pair_panels(np.stack([g, v], 1).reshape((2 * FF1_TILES,) + g.shape[1:]))
        w[f"l{l}_down"] = down_panels(a["ffn_w_down"][l])
        put(f"attn_norm{l}", columns(a["attn_norm_w"][l]))
        put(f"ffn_norm{l}", columns(a["ffn_norm_w"][l]))
        put(f"conv_w{l}", columns(a["ssd_conv_w"][l]).transpose(0, 2, 1))
        put(f"conv_b{l}", columns(a["ssd_conv_b"][l]))
        put(f"dt_bias{l}", rows(a["ssd_dt_bias"][l]))
        put(f"a_log{l}", rows(a["ssd_a_log"][l]))
        put(f"d_skip{l}", columns(np.repeat(a["ssd_d"][l], HDIM)))
        put(f"ssd_norm{l}", columns(a["ssd_norm_w"][l]))
        put(f"sc_w{l}", columns(a["sc_conv_w"][l]).transpose(0, 2, 1))
        put(f"pos{l}", np.concatenate([a["cmp_k_pos"][l].T, a["cmp_v_pos"][l].T]))
        put(f"k_w2{l}", np.concatenate([a["cmp_k_w2"][l]] * 2, axis=1))
        put(f"v_w2{l}", a["cmp_v_w2"][l])
        cw = np.concatenate([a["ffn_conv_w"][l], a["ffn_conv_b"][l][None]])
        cw = np.stack([columns(cw[:, :FF1]), columns(cw[:, FF1:])], 1)
        put(f"ffn_conv{l}", cw.transpose(0, 3, 1, 2))
        for j, s in enumerate("ab"):
            wi = a["ffn_w_in_2"][l, j]
            g, v = tiles_of(wi[:, :FF2_TILES * P]), tiles_of(wi[:, FF2_TILES * P:])
            gv = pair_panels(np.stack([g, v], 1).reshape((2 * FF2_TILES,) + g.shape[1:]))
            dn = down_panels(a["ffn_w_out_2"][l, j])
            if (l, s) == (1, "b"):
                w["m1b_up"], w["m1b_down"] = gv, dn
            else:
                for part in range(2):
                    w[f"m{l}{s}_up{part}"] = gv[part * HALF_FF:(part + 1) * HALF_FF]
                    w[f"m{l}{s}_down{part}"] = dn[part::2]
    put("final1", columns(a["final_norm_w"]))
    put("cond", np.stack([columns(a["c_2"][0]), columns(a["c_ctx_2"])], -1))
    put("mod_norm", columns(a["norm_g_2"]))
    put("mod_b", columns(a["mod_b_2"]))
    put("final2", columns(a["final_norm_g_2"]))
    put("q_norm", columns(a["mla_q_norm_2"][0]))
    put("kv_norm", columns(a["mla_kv_norm_2"][0]))
    put("sink", rows(a["swa_sink_2"][0]))
    wd = a["mla_w_down_2"][0]
    w["mla_down"] = pair_panels(tiles_of(np.concatenate([wd, wd[:, 768:]], axis=1)))
    uq = a["mla_w_uq_2"][0].reshape(4, P, MLA_HEADS, 192)
    ukv = a["mla_w_ukv_2"][0].reshape(2, P, MLA_HEADS, 256)
    panels = []
    for p in range(4):
        hs = (2 * p, 2 * p + 1)
        qn = [uq[:, :, x, :128].transpose(1, 0, 2).reshape(P, -1) for x in hs]
        qr = [np.concatenate([uq[:, :, x, 128:] for x in hs], -1).transpose(1, 0, 2).reshape(P, -1)]
        kn = [ukv[:, :, x, :128].transpose(1, 0, 2).reshape(P, -1) for x in hs]
        vv = [np.concatenate([ukv[:, :, x, 128:] for x in hs], -1).transpose(1, 0, 2).reshape(P, -1)]
        panels.append(np.concatenate(qn + qr, axis=1))
        panels.append(np.concatenate(kn + vv + [np.zeros((P, 512), np.float32)], axis=1))
    w["mla_pair"] = np.stack(panels)
    w["mla_o"] = pair_panels(tiles_of(a["mla_w_o_2"][0]))
    qkv = a["swa_w_qkv_2"][0]
    k = qkv[:, 1024:1280].reshape(DM, SWA_KV, 1, 64)
    k = np.concatenate([k, k], axis=2).reshape(DM, SWA_KV * P)
    v = qkv[:, 1280:].reshape(KD, P, T).transpose(1, 0, 2).reshape(1, P, KD * T)
    w["swa_qkv"] = np.concatenate([pair_panels(tiles_of(np.concatenate([qkv[:, :1024], k], axis=1))), v])
    w["swa_o"] = pair_panels(tiles_of(a["swa_w_o_2"][0]))

    def tokens(x):
        return np.ascontiguousarray(x.reshape(T, KD, P).transpose(2, 1, 0))

    arrays = {"x": tokens(a["x"]), "ctx": tokens(a["ctx_2"]), "params": par, "consts": constants()}
    for name, count, width, _ in STREAM:
        arrays["w_" + name] = np.ascontiguousarray(w[name])
        assert arrays["w_" + name].shape == (count, P, width), name
    nc = bacc.Bacc("TRN2", target_bir_lowering=False, num_devices=1)
    t = {n: nc.dram_tensor(n, v.shape, F32, kind="ExternalInput").ap() for n, v in arrays.items()}
    out = nc.dram_tensor("out", (P, KD, T), F32, kind="ExternalOutput").ap()
    two_blocks(nc, t["x"], t["ctx"], t["params"], t["consts"], {n: t["w_" + n] for n, _, _, _ in STREAM}, out)
    r = run_bass_kernel_spmd(nc, [arrays], core_ids=[0])
    y = np.asarray(r.results[0]["out"])
    return y.transpose(2, 1, 0).reshape(1, T, DM)
```

```python
from contextlib import ExitStack

import concourse.bass as bass
import numpy as np
from concourse import mybir

F32 = mybir.dt.float32
F32R = mybir.dt.float32r
ALU = mybir.AluOpType
ACT = mybir.ActivationFunctionType
AXX = mybir.AxisListType.X

P = 128
DM = 1024
KD = DM // P
T = 256
EPS = 1e-6
NEG = -1e30
LAYERS = 2

HEADS, HDIM, GROUPS, STATE = 8, 64, 2, 128
INNER = HEADS * HDIM
XBC = INNER + 2 * GROUPS * STATE
SC = 256
FF1, FF1_TILES = 2752, 22
CMP_BLOCK, CMP_STRIDE, N_CMP = 32, 16, 15
TM = HEADS + 64 + 64 + 12
U_KCVC, U_VCKC, U_KS, U_KW, U_Q, U_SCB, U_SCC, U_SCH, U_XBC, U_Z, U_TILES = 0, 1, 2, 3, 4, 6, 8, 10, 12, 20, 24
PAD = 3
UW = PAD + T

FF2_TILES = 22
N_MOD = 9
MLA_HEADS, SWA_HEADS, SWA_KV = 8, 16, 4

RAW = 4
HALVES = 2
PANEL = 2048
MODW = 256
MOD_PANELS = LAYERS * N_MOD * DM // MODW
HALF_FF = 11
DOWN = HALF_FF * P

STREAM = []
for _l in range(LAYERS):
    STREAM += [(f"l{_l}_in", 13, PANEL, True), (f"mod{_l}a", 2, PANEL, True), (f"l{_l}_cmp", 2, PANEL, False),
               (f"mod{_l}b", 16, PANEL, True), (f"l{_l}_out", 4, PANEL, True),
               (f"l{_l}_up", FF1_TILES, PANEL, True), (f"l{_l}_down", 2 * KD, DOWN, True)]


def ffn_stream(name):
    return [(name + "_up0", HALF_FF, PANEL, True), (name + "_down0", KD, DOWN, True),
            (name + "_up1", HALF_FF, PANEL, True), (name + "_down1", KD, DOWN, True)]


STREAM += ffn_stream("m0a") + [("mla_down", 4, PANEL, True), ("mla_pair0", 2, 1536, False), ("mla_pair1", 2, 1536, False),
                               ("mod2a", 6, PANEL, True), ("mla_pair2", 2, 1536, False), ("mod2b", 6, PANEL, True),
                               ("mla_pair3", 2, 1536, False), ("mod2c", 8, PANEL, True), ("mla_o", 4, PANEL, True)]
STREAM += ffn_stream("m0b") + ffn_stream("m1a")
STREAM += [("swa_qkv", 7, PANEL, True), ("mod3", 16, PANEL, True), ("swa_o", 4, PANEL, True)]
STREAM += [("m1b_up", FF2_TILES, PANEL, True), ("m1b_down", 2 * KD, DOWN, True)]
FIRST_RAW, FIRST_SPLIT, WIDTH, _raw, _split = {}, {}, {}, 0, 0
for _name, _count, _width, _is_split in STREAM:
    FIRST_RAW[_name], FIRST_SPLIT[_name], WIDTH[_name] = _raw, _split, _width
    _raw += _count
    _split += _count * _is_split

MOD_FIRST, _raw = {}, 0
for _name, _count, _width, _ in STREAM:
    if _name.startswith("mod"):
        MOD_FIRST[_name] = _raw
        _raw += _count
assert _raw == MOD_PANELS
MOD_COUNT = {n: c for n, c, _, _ in STREAM}
MOD_RUNS = [[("mod0a", None), ("mod0b", "l0_out")], [("mod1a", None), ("mod1b", "l1_out")],
            [("mod2a", None), ("mod2b", None), ("mod2c", "mla_o")], [("mod3", "swa_o")]]

VECTOR_LOWS = [(f"mod{l}b", HEADS + 1 + hh) for l in range(LAYERS) for hh in (2, 4, 6)]

NORMS = ([(KD, T), 0, (4, T), "l0_out", (KD, T), (KD, T), 1, (4, T), "l1_out", (KD, T), (KD, T)]
         + [(KD, 2 * T)] * 2 + [(4, 2 * T), (2, 2 * T), 2] + [(KD, 2 * T)] * 3 + [3] + [(KD, T)] * 2)


def table(widths):
    out, at = {}, 0
    for name, w in widths:
        out[name] = (at, w)
        at += w
    return out, at


PARAMS, PARAM_W = table(
    [(f"{n}{l}", w) for l in range(LAYERS) for n, w in (
        ("attn_norm", KD), ("ffn_norm", KD), ("conv_w", 32), ("conv_b", 8), ("dt_bias", HEADS), ("a_log", HEADS),
        ("d_skip", 4), ("ssd_norm", 4), ("sc_w", 6), ("pos", CMP_BLOCK), ("k_w2", P), ("v_w2", 64),
        ("ffn_conv", FF1_TILES * 8))]
    + [("final1", KD), ("cond", KD * 2), ("mod_norm", LAYERS * 3 * KD), ("mod_b", LAYERS * N_MOD * KD),
       ("final2", KD), ("q_norm", 4), ("kv_norm", 2), ("sink", SWA_HEADS)])
CONSTS, CONST_W = table([("ident", P), ("tri", 2 * T), ("rot", P), ("cos1", T), ("sin1", T), ("cos2", T), ("sin2", T),
                         ("causal", 2 * T), ("decay_mask", 384), ("cmp_add", 32), ("cmp_keep", 32),
                         ("window", 2 * T), ("fold", 2)])


class Tally:

    def __init__(self):
        self.at = {}

    def take(self, name, n):
        base = self.at.get(name, 0)
        self.at[name] = base + n
        return base


class Chain:

    def __init__(self, eng, sem):
        self.eng, self.sem, self.n, self.extra = eng, sem, 0, 0

    def __call__(self, ins):
        self.n += 1
        ins.then_inc(self.sem, 1)
        self.eng.wait_ge(self.sem, self.extra + self.n)


def turns(eng, count, unroll, body, chain=None, links=0, peel=0, tail=0):
    full = (count - tail) // unroll
    for n in range(peel * unroll):
        body(n, n % unroll, n // unroll)
    at = chain.n if chain else 0
    with eng.Fori(peel, full) as i:
        if chain:
            chain.extra = (i - peel) * (links * unroll) if peel else i * (links * unroll)
        for j in range(unroll):
            body(i * unroll + j, j, i)
    if chain:
        assert chain.n - at == links * unroll
        chain.n, chain.extra = at + links * unroll * (full - peel), 0
    for n in range(full * unroll, count):
        body(n, n % unroll, n // unroll)


def fixed(n):
    return isinstance(n, int)


def raw_slot(name, j):
    return (FIRST_RAW[name] + j) % RAW


def landed_value(name, j, i):
    return i * 16 + (FIRST_RAW[name] + j) // RAW * 16 + 16


def half_slot(name, j):
    return (FIRST_SPLIT[name] + j) % HALVES


def two_blocks(nc, xT, ctxT, params_d, consts_d, weights, out_d):
    ctx = ExitStack()
    with ctx:
        bytes_at = [nc.sbuf_base + 31 & ~31]

        def sb(name, shape, dt=F32, at=None):
            off = bytes_at[0] if at is None else at
            size = 4 * int(np.prod(shape[1:])) + 31 & ~31
            if at is None:
                bytes_at[0] += size
            assert off + size <= nc.sbuf_usable_end, name
            return nc.alloc_sbuf_tensor_at("sb_" + name, shape, dt, offset=off)

        sems = {}

        def S(name):
            if name not in sems:
                sems[name] = ctx.enter_context(nc.semaphore(name))
            return sems[name]

        raw = [sb(f"raw{s}", [P, PANEL]) for s in range(RAW)]
        w_hi = [sb(f"w_hi{s}", [P, PANEL], F32R) for s in range(HALVES)]
        w_lo = [sb(f"w_lo{s}", [P, PANEL], F32R) for s in range(HALVES)]
        res = sb("res", [P, KD, 2 * T])
        H = bytes_at[0]
        bytes_at[0] += 32768
        h_wide = [sb(f"h_{n}", [P, KD, 2 * T], F32R, at=H + 16384 * i) for i, n in enumerate(("hi", "lo"))]
        h_thin = [sb(f"hx_{n}", [P, KD, T], F32R, at=H + 8192 * i) for i, n in enumerate(("hi", "lo"))]
        ropet = sb("ropet", [P, 2, 2 * T], at=H + 16384)
        cbT = sb("cbT", [P, GROUPS, 384], at=H + 20480)
        tpos = sb("tpos", [P, 2, CMP_BLOCK // 2, N_CMP], at=H + 23552)
        kvr = sb("kvr", [P, T], at=H + 25600)
        kvv = sb("kvv", [P, T], at=H + 28672)
        hidT = sb("hidT", [N_CMP, 2, P], at=H + 29696)
        sct = sb("sct", [P, 2, T], at=H + 26624)
        M = bytes_at[0]
        bytes_at[0] += 4 * 22 * 512
        f_hi = sb("f_hi", [P, HALF_FF * 512], F32R, at=M)
        f_lo = sb("f_lo", [P, HALF_FF * 512], F32R, at=M + 4 * HALF_FF * 512)
        mid = sb("mid", [P, 22 * 512], at=M)
        normed_f = sb("normed", [P, KD, 2 * T], at=M)
        params = sb("params", [P, PARAM_W])
        consts = sb("consts", [P, CONST_W])
        modT = sb("modT", [P, LAYERS * N_MOD * KD, 2])
        cond = sb("cond", [P, KD, 2])
        mod_row = sb("mod_row", [4, 2, MODW])
        cond_w = sb("cond_w", [P, 4 * KD + P], F32R)
        sq = sb("sq", [P, 2, 2 * T])
        sq_sum = sb("sq_sum", [P, 2 * T])
        eps = sb("eps", [P, 1])
        root_warm = sb("root_warm", [P, 1])
        rstd = sb("rstd", [P, 2 * T])
        inv = {n: sb(f"inv{n}", [P, P]) for n in (1024, 512, 256)}
        A = bytes_at[0]
        bytes_at[0] += 12288
        sbS = sb("sbS", [P, 2, 512], at=A)
        sbP = sb("sbP", [P, 2, 512], at=A + 4096)
        sbPT = sb("sbPT", [P, 2, 512], at=A + 8192)
        ropes = sb("ropes", [P, 2, T], at=A)
        sil = sb("sil", [P, 2, 2 * T], at=A)
        prod = sb("prod", [P, 2 * T], at=A + 4096)
        ucv = sb("ucv", [P, 2, 2, 2 + T], at=A + 6144)
        cva = sb("cva", [P, 2, 2, T])
        sbPC = sb("sbPC", [P, 2, 16])
        sbPCT = sb("sbPCT", [16, 2, P])
        stat = sb("stat", [P, 2, 16])
        tm = sb("tm", [P, 2, TM])
        gate = sb("gate", [P, 2, 12])
        dtw = sb("dtw", [P, 8, 16])
        ea = sb("ea", [P, HEADS])
        acs = sb("acs", [P, 2, HEADS])
        acsT = sb("acsT", [HEADS, T])
        hid = sb("hid", [P, 2, N_CMP])
        kc = sb("kc", [P, N_CMP])
        vc = sb("vc", [N_CMP, 64])
        bank = [ctx.enter_context(nc.psum_tensor(f"bank{b}", [P, 512], F32)) for b in range(8)]

        def par(name, a=0, b=None):
            at, w = PARAMS[name]
            return params[:, at + a:at + (w if b is None else b)]

        def con(name, a=0, b=None):
            at, w = CONSTS[name]
            return consts[:, at + a:at + (w if b is None else b)]

        def region(at, *shape):
            n = int(np.prod(shape))
            v = mid[:, at:at + n]
            return (v.rearrange("p (a b) -> p a b", a=shape[0]) if len(shape) == 2 else v), at + n

        ident = con("ident")
        U, at = region(0, U_TILES, UW)
        xc, at = region(at, 8, T)
        xdt, at = region(at, 2, INNER)
        yss = U[:, 0:4, PAD:UW]
        krq, at = region(at, 4, T)
        dpj, at = region(0, 7, 512)
        pairs = []
        for _ in range(2):
            qn, at = region(at, 2, 512)
            qr, at = region(at, 512)
            qrot, at = region(at, T)
            kn, at = region(at, 2, 512)
            vv, at = region(at, 4, T)
            pairs.append((qn, qr, qrot, kn, vv))
        sq_q, at = region(0, 8, T)
        sq_qrot, at = region(at, 8, T)
        sq_k, at = region(at, SWA_KV, 512)
        sq_v, at = region(at, 4, T)

        def h_of(N):
            return h_wide if N > T else h_thin

        def hidden(half, N):
            return half[:, :].rearrange("p (n t) -> p n t", t=N)

        def mod(l, c, k, s):
            q = (l * N_MOD + c) * KD + k
            return modT[:, q, s:s + 1]

        def streams(n):
            return [(s, s * T) for s in range(n // T)]

        def mla_fill(u):
            p, r = divmod(u, 8)
            if p == 3:
                return [("mod2c", 6 + r)] if r < 2 else []
            return [("mod2" + "abc"[p], r - 2)] if r >= 2 else []

        def swa_fill(u):
            return [("mod3", u // 2)] if u % 2 == 0 else []

        block = ctx.enter_context(nc.Block())

        @block.sync
        def _(sp):
            sp.dma_start(res[:, :, 0:T], xT).then_inc(S("x_in"), 16)
            sp.dma_start(params[:, :], params_d).then_inc(S("params_in"), 16)
            sp.sem_inc(S("raw_free"), RAW)
            for name, count, width, _ in STREAM:
                def load(n, j, i):
                    if name == "l0_in" and fixed(n) and n == 2:
                        sp.dma_start(consts[:, :], consts_d).then_inc(S("consts_in"), 16)
                    sp.wait_ge(S("raw_free"), n + (FIRST_RAW[name] + 1))
                    slot = raw_slot(name, j)
                    sp.dma_start(raw[slot][:, 0:width], weights[name][n]).then_inc(S(f"landed{slot}"), 16)

                if count >= 2 * RAW:
                    turns(sp, count, RAW, load, peel=int(name == "l0_in"))
                else:
                    for n in range(count):
                        load(n, n, 0)
                if name == "l0_in":
                    sp.dma_start(res[:, :, T:2 * T], ctxT).then_inc(S("ctx_in"), 16)
            sp.wait_ge(S("final_out"), KD)
            sp.dma_start(out_d, normed_f[:, :, 0:T]).then_inc(S("stored"), 16)
            sp.wait_ge(S("stored"), 16)

        @block.gpsimd
        def _(pool):
            for n in inv:
                nc.gpsimd.memset(inv[n][:, :], 1.0 / n).then_inc(S("fills"), 1)
            nc.gpsimd.memset(eps[:, :], EPS).then_inc(S("fills"), 1)
            nc.gpsimd.memset(cond_w[:, :].bitcast(F32), 0.0).then_inc(S("fills"), 1)
            squares_at, added = 0, 0

            def low(name, n):
                pool.wait_ge(S("high"), FIRST_SPLIT[name] + n + 1)
                pool.wait_ge(S("raw_free"), FIRST_RAW[name] + n + RAW)
                w, s = WIDTH[name], half_slot(name, n)
                nc.gpsimd.tensor_tensor(w_lo[s][:, 0:w], raw[raw_slot(name, n)][:, 0:w], w_hi[s][:, 0:w].bitcast(F32),
                                        ALU.subtract).then_inc(S("raw_free"), 1)

            for item in NORMS:
                if fixed(item):
                    for name, after in MOD_RUNS[item]:
                        for n in range(MOD_COUNT[name]):
                            if (name, n) not in VECTOR_LOWS:
                                low(name, n)
                        if after:
                            low(after, 0)
                            if after not in NORMS:
                                low(after, 1)
                    continue
                if isinstance(item, str):
                    low(item, 1)
                    continue
                K, N = item
                for k in range(1, K - 1):
                    pool.wait_ge(S("norm_sq"), squares_at + k + 1)
                    if added:
                        pool.wait_ge(S("sq_added"), added)
                    nc.gpsimd.tensor_tensor(sq_sum[:, 0:N], sq[:, k % 2, 0:N], sq_sum[:, 0:N],
                                            ALU.add).then_inc(S("sq_added"), 1)
                    added += 1
                squares_at += K

        @block.tensor
        def _(pe):
            tally = Tally()
            take = tally.take

            def mm(out, lhsT, rhs, start, stop):
                return nc.tensor.matmul(out, lhsT, rhs, start=start, stop=stop, skip_group_check=True)

            def mm3(out, w, x, start, stop):
                (wh, wl), (xh, xl) = w, x
                mm(out, wh, xh, start, False)
                mm(out, wh, xl, False, False)
                return mm(out, wl, xh, False, stop)

            def panel(name, j, i):
                pe.wait_ge(S("raw_free"), i * RAW + (FIRST_RAW[name] + j + 1 + RAW))
                slot = half_slot(name, j)
                return w_hi[slot], w_lo[slot]

            def whole(name, n):
                slot = raw_slot(name, n)
                pe.wait_ge(S(f"landed{slot}"), landed_value(name, n, 0))
                return raw[slot]

            def both(pair, *index):
                return tuple(x[index] for x in pair)

            def cols(w, a, n=P):
                return both(w, slice(None), slice(a, a + n))

            def norm(K, N, const):
                b = take("norm_sq", K)
                a = take("sq_added", max(K - 2, 0))
                c = take("rms_done", 1)
                if c:
                    pe.wait_ge(S("rms_done"), c)
                pe.wait_ge(S("norm_sq"), b + K - 1)
                if K > 2:
                    pe.wait_ge(S("sq_added"), a + K - 2)
                mm(bank[7][:, 0:N], inv[const][:, :], sq_sum[:, 0:N], True, False)
                pe.wait_ge(S("norm_sq"), b + K)
                mm(bank[7][:, 0:N], inv[const][:, :], sq[:, (K - 1) % 2, 0:N], False, True).then_inc(S("norm_sum"), 1)

            def split_input(N, K=KD):
                per = N // T
                b = take("norm_split", K * per)

                def ready(k=K - 1):
                    pe.wait_ge(S("norm_split"), b + (k + 1) * per)
                return ready

            def mod_rows(name, n):
                g = MOD_FIRST[name] + n
                w = panel(name, n, 0)
                if g:
                    pe.wait_ge(S("mod_vec"), g)
                for k in range(KD):
                    c = cond_w[:, 4 * k:4 * k + P]
                    mm(bank[7][:, 0:MODW], c, w[0][:, k * MODW:(k + 1) * MODW], k == 0, False)
                    last = mm(bank[7][:, 0:MODW], c, w[1][:, k * MODW:(k + 1) * MODW], False, k == KD - 1)
                last.then_inc(S("panels_used"), 1)

            def mod_cols(name, n):
                pe.wait_ge(S("mod_row"), MOD_FIRST[name] + n + 1)
                for t in range(2):
                    last = mm(bank[7][:, 2 * t:2 * t + 2], mod_row[0:4, (MOD_FIRST[name] + n) % 2, t * P:(t + 1) * P],
                              con("fold")[0:4, :], True, True)
                last.then_inc(S("mod_cols"), 1)

            def mod_done(name):
                pe.wait_ge(S("mod_vec"), MOD_FIRST[name] + MOD_COUNT[name])

            def project(name, N):
                b = take("res_done", KD)
                h = h_of(N)
                for n in range(KD // 2):
                    w = panel(name, n, 0)
                    for t in range(2):
                        m = 2 * n + t
                        if m >= 2:
                            pe.wait_ge(S("res_done"), b + m - 1)
                        for k in range(KD):
                            last = mm3(bank[4 + t][:, 0:N], cols(w, (t * KD + k) * P), both(h, slice(None), k),
                                       k == 0, k == KD - 1)
                        last.then_inc(S("panels_used" if t else "half_panel"), 1)

            def down(name, N, mid_base):
                b = take("res_done", KD)
                f = [hidden(x, N) for x in (f_hi, f_lo)]
                per = 2 * T // N

                def tile(n, j, i):
                    w = panel(name, j, i)
                    m, part = j // per, j % per
                    if part == 0 and not (fixed(n) and n < 2 * per):
                        pe.wait_ge(S("res_done"), n // per + (b - 1) if fixed(n) else i * (RAW // per) + (m + b - 1))
                    for k in range(HALF_FF):
                        if fixed(n) and n < per and (k in (0, HALF_FF - 1)):
                            pe.wait_ge(S("ff_mid"), mid_base + part * HALF_FF + HALF_FF - (0 if k else 1))
                        last = mm3(bank[4 + m % 2][:, 0:N], cols(w, k * P),
                                   both(f, slice(None), part * HALF_FF + k),
                                   part == 0 and k == 0, part == per - 1 and k == HALF_FF - 1)
                    last.then_inc(S("panels_used"), 1)

                turns(pe, KD * per, RAW, tile, peel=1)

            def up(name, count, N, sem, ready=None):
                b = take(sem, count)
                h = h_of(N)

                def tile(n, j, i):
                    w = panel(name, j, i)
                    if not (fixed(n) and n < 2):
                        pe.wait_ge(S(sem), n + (b - 1))
                    for half in range(2):
                        if sem == "up_evac":
                            o = bank[j % 2][:, half * T:(half + 1) * T]
                        else:
                            o = bank[2 * (j % 2) + half][:, 0:N]
                        for k in range(KD):
                            if ready and fixed(n) and n == 0 and half == 0:
                                ready(k)
                            last = mm3(o, cols(w, (half * KD + k) * P), both(h, slice(None), k), k == 0, k == KD - 1)
                    last.then_inc(S("panels_used"), 1)

                turns(pe, count, RAW, tile, peel=1)
                return b

            def ffn1(name):
                up(name + "_up", FF1_TILES, T, "up_evac", split_input(T))
                m = take("ff_mid", FF1_TILES)
                down(name + "_down", T, m)

            def ffn2(name, N):
                ready = split_input(N)
                if N == T:
                    b = up(name + "_up", FF2_TILES, N, "ff_mid", ready)
                    down(name + "_down", N, b)
                    return
                for part in range(2):
                    b = up(f"{name}_up{part}", HALF_FF, N, "ff_mid", ready if part == 0 else None)
                    down(f"{name}_down{part}", N, b)

            def attention(units, scores, flips, products, lead, fill, shared=False, between=None):
                b = take("att_scores", units)

                def ahead(u):
                    if u >= 2:
                        pe.wait_ge(S("att_exp"), b + u - 1)
                    if u >= 2 and shared:
                        pe.wait_ge(S("att_turned"), b + u - 1)
                    scores(u).then_inc(S("att_scores"), 1)

                def turn(u):
                    pe.wait_ge(S("att_probs"), b + u + 1)
                    if u >= 2:
                        pe.wait_ge(S("att_turned"), b + u - 1)
                    flips(u).then_inc(S("att_flips"), 1)

                def product(u):
                    pe.wait_ge(S("att_turned"), b + u + 1)
                    if u >= 1:
                        pe.wait_ge(S("att_out"), b + u)
                    products(u).then_inc(S("att_prod"), 1)

                for u in range(lead):
                    ahead(u)
                for u in range(units + 1):
                    if between:
                        between(u)
                    if u + lead < units:
                        ahead(u + lead)
                    for f in fill(u - 1) if u else ():
                        mod_cols(*f)
                    if u < units:
                        turn(u)
                        for f in fill(u):
                            mod_rows(*f)
                    if u >= 1:
                        product(u - 1)

            def mixers(l):
                L = f"l{l}"
                norm(KD, T, 1024)
                ready = split_input(T)
                h = h_thin
                w = panel(L + "_in", 0, 0)
                for tb in range(2):
                    for k in range(KD):
                        ready(k)
                        last = mm3(bank[2 + tb][:, 0:TM], both(h, slice(None), k, slice(tb * P, (tb + 1) * P)),
                                   cols(w, k * TM, TM), k == 0, k == KD - 1)
                last.then_inc(S("panels_used"), 1)
                e = take("in_evac", 13)

                def pair(n, j, i):
                    if fixed(n) and n == 0:
                        return
                    wp = panel(L + "_in", j, i)
                    if not (fixed(n) and n < 3):
                        pe.wait_ge(S("in_evac"), n + (e - 1))
                    for t in range(2):
                        for k in range(KD):
                            last = mm3(bank[j % 2][:, t * T:(t + 1) * T], cols(wp, (t * KD + k) * P),
                                       both(h, slice(None), k), k == 0, k == KD - 1)
                    last.then_inc(S("panels_used"), 1)
                    if fixed(n) and n == 3:
                        pe.wait_ge(S("consts_in"), 16)
                        for t in range(6):
                            pe.wait_ge(S("in_evac"), e + (3 if t < 4 else 4))
                            last = mm(bank[2 + t // 2][:, (t % 2) * T:(t % 2 + 1) * T], con("rot"),
                                      U[:, t, PAD:UW], True, True)
                        last.then_inc(S("rotated"), 1)

                turns(pe, 13, RAW, pair, peel=1)
                if l == 0:
                    pe.wait_ge(S("cond_ready"), 1)
                mod_rows(f"mod{l}a", 0)
                a = dtw[:, 7, :].rearrange("p (b h) -> p b h", b=2)
                d = take("dt_ready", 1)
                pe.wait_ge(S("dt_ready"), d + 1)
                tri = con("tri").rearrange("p (b t) -> p b t", b=2)
                mm(bank[5][:, 0:HEADS], tri[:, 0, 0:P], a[:, 0, :], True, True)
                mm(bank[5][:, 8:16], tri[:, 0, P:T], a[:, 0, :], True, False)
                mm(bank[5][:, 8:16], tri[:, 1, P:T], a[:, 1, :], False, True)
                mm(bank[5][0:HEADS, T:2 * T], a[:, 0, :], tri[:, 0, :], True, False)
                mm(bank[5][0:HEADS, T:2 * T], a[:, 1, :], tri[:, 1, :], False, True).then_inc(S("cumulated"), 1)
                mod_cols(f"mod{l}a", 0)
                mod_rows(f"mod{l}a", 1)
                tk = take("tpos_ready", 1)
                pe.wait_ge(S("tpos_ready"), tk + 1)
                pe.wait_ge(S("in_evac"), e + 13)
                mod_cols(f"mod{l}a", 1)
                for c in range(2):
                    w = whole(L + "_cmp", c)
                    for i in range(CMP_BLOCK // 2):
                        last = mm(bank[6][0:N_CMP, c * P:(c + 1) * P], tpos[:, c, i, :], w[:, i * P:(i + 1) * P],
                                  i == 0, i == CMP_BLOCK // 2 - 1)
                    last.then_inc(S("raw_free"), 1)
                x = take("xbc_ready", 8)
                pe.wait_ge(S("xbc_ready"), x + 8)
                for tb in range(2):
                    for t in range(4):
                        last = nc.tensor.transpose(bank[2 + tb][:, t * P:(t + 1) * P], xc[:, t, tb * P:(tb + 1) * P],
                                                   ident)
                last.then_inc(S("x_turned"), 1)
                for g in range(GROUPS):
                    B, C = xc[:, 4 + g, :], xc[:, 6 + g, :]
                    mm(bank[g][:, 0:T], B[:, 0:P], C, True, True)
                    last = mm(bank[g][:, T:384], B[:, P:T], C[:, P:T], True, True)
                last.then_inc(S("cb_ready"), 1)
                pe.wait_ge(S("hid_act"), l + 1)
                for c in range(2):
                    last = mm(bank[4][:, c * 16:c * 16 + N_CMP], hidT[:, c, :], ident[0:N_CMP, 0:N_CMP], True, True)
                last.then_inc(S("hid_turned"), 1)
                mod_rows(f"mod{l}b", 0)
                pe.wait_ge(S("hid_ready"), l + 1)
                mm(bank[6][:, 0:N_CMP], par(f"k_w2{l}"), hid[:, 0, :], True, True)
                mm(bank[6][0:N_CMP, 64:128], hid[:, 1, :], par(f"v_w2{l}"), True, True).then_inc(S("cmp_kv"), 1)
                s = take("ssm_start", 1)
                pe.wait_ge(S("ssm_start"), s + 1)

                def where(u):
                    hh, b = u // 2, u % 2
                    return slice(64 * (hh % 2), 64 * (hh % 2) + 64), hh, b

                def scores(u):
                    rows, hh, b = where(u)
                    q = krq[rows, 2 + hh // 2, b * P:(b + 1) * P]
                    mm(bank[2 + u % 2][:, 0:N_CMP], q, kc[rows, :], True, True)
                    mm(bank[u % 2][:, 0:T], q, krq[rows, 0, :], True, True)
                    return mm(bank[u % 2][:, T:2 * T], q, krq[rows, 1, :], True, True)

                def flips(u):
                    nc.tensor.transpose(bank[2 + u % 2][0:N_CMP, P:2 * P], sbPC[:, u % 2, 0:N_CMP], ident)
                    for c in range(4):
                        last = nc.tensor.transpose(bank[4 + u % 2][:, c * P:(c + 1) * P],
                                                   sbP[:, u % 2, c * P:(c + 1) * P], ident)
                    return last

                def products(u):
                    rows, hh, b = where(u)
                    o = bank[6][rows, 0:P]
                    mm(o, vc[:, :], sbPCT[0:N_CMP, u % 2, :], True, False)
                    for c in range(4):
                        v = tm[:, c % 2, 8 + 64 * (c // 2):72 + 64 * (c // 2)]
                        last = mm(o, v, sbPT[:, u % 2, c * P:(c + 1) * P], False, c == 3)
                    return last

                attention(8, scores, flips, products, 1, lambda u: [(f"mod{l}b", u + 1)], shared=True,
                          between=lambda u: mod_cols(f"mod{l}b", 0) if u == 0 else None)
                y = take("ssd_y", HEADS)
                yo = take("ssd_out", 4)
                at_start = take("att_out", 8)
                pe.wait_ge(S("att_out"), at_start + 8)

                def spread(hh):
                    if hh >= 2:
                        pe.wait_ge(S("ssd_diff"), y + hh - 1)
                    mm(bank[hh % 2][:, 0:T], ident[0:HEADS, hh:hh + 1].to_broadcast([HEADS, P]), acsT[:, :],
                       True, True).then_inc(S("ssd_spread"), 1)

                spread(0)
                spread(1)
                for hh in range(HEADS):
                    if hh:
                        mod_cols(f"mod{l}b", HEADS + hh)
                    pe.wait_ge(S("ssd_mat"), y + hh + 1)
                    t = hh // 2
                    rows = slice(64 * (hh % 2), 64 * (hh % 2) + 64)
                    o = bank[2 + t % 2]
                    if hh % 2 == 0 and t >= 2:
                        pe.wait_ge(S("ssd_out"), yo + t - 1)
                    mm(o[rows, 0:T], xdt[:, 0, hh * 64:(hh + 1) * 64], sbP[:, hh % 2, 0:T], True, False)
                    mm(o[rows, P:T], xdt[:, 1, hh * 64:(hh + 1) * 64], sbP[:, hh % 2, T:384], False,
                       True).then_inc(S("ssd_y"), 1)
                    if hh + 2 < HEADS:
                        spread(hh + 2)
                    if hh < HEADS - 1:
                        mod_rows(f"mod{l}b", HEADS + 1 + hh)
                mod_done(f"mod{l}b")
                norm(4, T, 512)
                m = take("mixed", 6)
                pe.wait_ge(S("mixed"), m + 6)
                project(L + "_out", T)

            pe.wait_ge(S("fills"), 5)
            for l in range(LAYERS):
                mixers(l)
                norm(KD, T, 1024)
                ffn1(f"l{l}")
            norm(KD, T, 1024)
            norm(KD, 2 * T, 1024)
            ffn2("m0a", 2 * T)
            norm(KD, 2 * T, 1024)
            ready = split_input(2 * T)
            h = h_wide
            d = take("lat_evac", 4)
            for n in range(4):
                w = panel("mla_down", n, 0)
                if n >= 2:
                    pe.wait_ge(S("lat_evac"), d + n - 1)
                for t in range(2 if n < 3 else 1):
                    for k in range(KD):
                        if n == t == 0:
                            ready(k)
                        last = mm3(bank[2 * (n % 2) + t][:, :], cols(w, (t * KD + k) * P), both(h, slice(None), k),
                                   k == 0, k == KD - 1)
                last.then_inc(S("panels_used"), 1)
            pe.wait_ge(S("lat_evac"), d + 4)
            mm(bank[4][:, 0:T], con("rot"), dpj[:, 6, 0:T], True, True).then_inc(S("rotated"), 1)
            norm(4, 2 * T, 512)
            norm(2, 2 * T, 256)
            pe.wait_ge(S("lat_normed"), 6)

            def pair_tiles(p):
                w = whole(f"mla_pair{p}", 0)
                qn, qr, qrot, kn, vv = pairs[p % 2]

                def free(t):
                    if t >= 2:
                        pe.wait_ge(S("pair_evac"), 7 * p + t - 1)
                    elif p:
                        pe.wait_ge(S("pair_evac"), 7 * p)
                        if t == 1:
                            pe.wait_ge(S("pair_rope"), p)

                for t in range(5):
                    free(t)
                    if t == 3:
                        w = whole(f"mla_pair{p}", 1)
                    K, at0, src = (4, t * 512, 0) if t < 3 else (2, (t - 3) * 256, 4)
                    for k in range(K):
                        last = mm(bank[2 + t % 2][:, :], w[:, at0 + k * P:at0 + (k + 1) * P], dpj[:, src + k, :],
                                  k == 0, k == K - 1)
                    last.then_inc(S("raw_free" if t == 2 else "pair_tile"), 1)
                for t in range(5, 7):
                    free(t)
                    for tb in range(2):
                        b4 = 2 * (t - 5) + tb
                        for k in range(2):
                            last = mm(bank[2 + t % 2][:, tb * T:(tb + 1) * T], dpj[:, 4 + k, b4 * P:(b4 + 1) * P],
                                      w[:, 512 + k * T:512 + (k + 1) * T], k == 0, k == 1)
                    last.then_inc(S("pair_tile" if t == 5 else "raw_free"), 1)

            def pair_rot(p):
                qn, qr, qrot, kn, vv = pairs[p % 2]
                pe.wait_ge(S("pair_evac"), 7 * p + 6)
                mm(bank[3][:, 0:T], con("rot"), qr[:, 0:T], True, True).then_inc(S("pair_rot"), 1)

            def mla_scores(u):
                p, hh, b = u // 8, u // 4 % 2, u % 4
                qn, qr, qrot, kn, vv = pairs[p % 2]
                rows, q = slice(64 * hh, 64 * hh + 64), slice(b * P, (b + 1) * P)
                if u % 8 == 0:
                    pe.wait_ge(S("pair_rope"), p + 1)
                    pe.wait_ge(S("pair_evac"), 7 * p + 7)
                A = bank[u % 2]
                if b < 2:
                    mm(A[:, :], qn[:, hh, q], kn[:, hh, :], True, False)
                    mm(A[:, 0:T], qrot[rows, q], dpj[rows, 6, 0:T], False, False)
                    return mm(A[:, T:2 * T], qr[rows, q], dpj[rows, 6, T:2 * T], False, True)
                mm(A[:, 0:T], qn[:, hh, q], kn[:, hh, T:2 * T], True, False)
                return mm(A[:, 0:T], qr[rows, q], dpj[rows, 6, T:2 * T], False, True)

            def mla_flips(u):
                for c in range(4 if u % 4 < 2 else 2):
                    last = nc.tensor.transpose(bank[4 + u % 2][:, c * P:(c + 1) * P],
                                               sbP[:, u % 2, c * P:(c + 1) * P], ident)
                return last

            def mla_products(u):
                p, hh, b = u // 8, u // 4 % 2, u % 4
                qn, qr, qrot, kn, vv = pairs[p % 2]
                nk = 4 if b < 2 else 2
                for c in range(nk):
                    last = mm(bank[6][:, 0:P], vv[:, c + 4 - nk, hh * P:(hh + 1) * P],
                              sbPT[:, u % 2, c * P:(c + 1) * P], c == 0, c == nk - 1)
                return last

            kr = take("key_rope", 1)
            pe.wait_ge(S("key_rope"), kr + 1)
            pair_tiles(0)
            pair_rot(0)

            def mla_between(u):
                if u % 8 == 1 and u // 8 < 3:
                    pair_tiles(u // 8 + 1)
                if u % 8 == 3 and u // 8 < 3:
                    pair_rot(u // 8 + 1)

            attention(32, mla_scores, mla_flips, mla_products, 2, mla_fill, between=mla_between)
            o = take("att_out", 32)
            pe.wait_ge(S("att_out"), o + 32)
            mod_done("mod2c")
            project("mla_o", 2 * T)
            norm(KD, 2 * T, 1024)
            ffn2("m0b", 2 * T)
            norm(KD, 2 * T, 1024)
            ffn2("m1a", 2 * T)
            norm(KD, 2 * T, 1024)
            ready = split_input(2 * T)
            for n in range(7):
                w = panel("swa_qkv", n, 0)
                if 2 <= n <= 4:
                    pe.wait_ge(S("swa_evac"), min(n - 1 + n // 4, 4))
                for t in range(2):
                    if n < 4:
                        for k in range(KD):
                            if n == t == 0:
                                ready(k)
                            last = mm3(bank[n % 2][:, t * T:(t + 1) * T], cols(w, (t * KD + k) * P),
                                       both(h, slice(None), k, slice(0, T)), k == 0, k == KD - 1)
                    elif n < 6:
                        for k in range(KD):
                            last = mm3(bank[2 * (n % 2) + t][:, :], cols(w, (t * KD + k) * P),
                                       both(h, slice(None), k), k == 0, k == KD - 1)
                    else:
                        for tb in range(2):
                            c = 2 * t + tb
                            for k in range(KD):
                                last = mm3(bank[4 + t][:, tb * T:(tb + 1) * T],
                                           both(h, slice(None), k, slice(c * P, (c + 1) * P)), cols(w, k * T, T),
                                           k == 0, k == KD - 1)
                last.then_inc(S("panels_used"), 1)
            for g in range(6):
                b = 6 + g % 2
                if g >= 2:
                    pe.wait_ge(S("swa_rope"), g - 1)
                for t in range(2):
                    src = sq_q[:, 2 * g + t, :] if g < 4 else sq_k[:, 2 * (g - 4) + t, 0:T]
                    pe.wait_ge(S("swa_evac"), g + 1)
                    last = mm(bank[b][:, t * T:(t + 1) * T], con("rot"), src, True, True)
                last.then_inc(S("swa_rot"), 1)
            pe.wait_ge(S("swa_evac"), 7)
            pe.wait_ge(S("swa_rope"), 6)

            def swa_scores(u):
                hh, b = u // 2, u % 2
                rows, q = slice(64 * (hh % 2), 64 * (hh % 2) + 64), slice(b * P, (b + 1) * P)
                A = bank[u % 2]
                mm(A[:, 0:T], sq_qrot[rows, hh // 2, q], sq_k[rows, hh // 4, 0:T], True, True)
                return mm(A[:, T:2 * T], sq_q[rows, hh // 2, q], sq_k[rows, hh // 4, T:2 * T], True, True)

            def swa_flips(u):
                for c in range(4):
                    last = nc.tensor.transpose(bank[4 + u % 2][:, c * P:(c + 1) * P],
                                               sbP[:, u % 2, c * P:(c + 1) * P], ident)
                return last

            def swa_products(u):
                hh, b = u // 2, u % 2
                rows = slice(64 * (hh % 2), 64 * (hh % 2) + 64)
                for c in range(4):
                    last = mm(bank[6][rows, 0:P], sq_v[:, c, (hh // 4) * 64:(hh // 4 + 1) * 64],
                              sbPT[:, u % 2, c * P:(c + 1) * P], c == 0, c == 3)
                return last

            attention(32, swa_scores, swa_flips, swa_products, 2, swa_fill)
            o = take("att_out", 32)
            pe.wait_ge(S("att_out"), o + 32)
            mod_done("mod3")
            project("swa_o", T)
            norm(KD, T, 1024)
            ffn2("m1b", T)
            norm(KD, T, 1024)

        @block.scalar
        def _(act):
            take = Tally().take

            def run(out, in_, func, **kw):
                return nc.scalar.activation(out, in_, func, **kw)

            def panel_done(name, n):
                act.wait_ge(S("panels_used"), n + (FIRST_SPLIT[name] + 1))

            def high(name, j, i=0):
                act.wait_ge(S(f"landed{raw_slot(name, j)}"), landed_value(name, j, i))
                before = FIRST_SPLIT[name] + j - 1
                if before > 0 or not fixed(i):
                    act.wait_ge(S("panels_used"), i * RAW + before)
                w = WIDTH[name]
                run(w_hi[half_slot(name, j)][:, 0:w], raw[raw_slot(name, j)][:, 0:w], ACT.Copy).then_inc(S("high"), 1)

            def sweep(name, count, body, after=None, defer=False, unroll=RAW, loop=True):
                def step(n, j, i):
                    def ahead():
                        if not fixed(n) or n + 2 < count:
                            high(name, j + 2, i)
                        elif after and (n == count - 2 or not defer):
                            high(after, n + 2 - count)
                    body(n, j, i, ahead)

                if loop:
                    turns(act, count, RAW, step, peel=1, tail=2)
                else:
                    for n in range(count):
                        step(n, n, 0)

            mod_after = {a[0]: b[0] for run_ in MOD_RUNS for a, b in zip(run_, run_[1:])}
            mod_after.update({run_[-1][0]: run_[-1][1] for run_ in MOD_RUNS})

            def mod_evac(name, n, ahead=True):
                g = MOD_FIRST[name] + n
                panel_done(name, n)
                if g >= 2:
                    act.wait_ge(S("mod_cols"), g - 1)
                run(mod_row[0:4, g % 2, :], bank[7][0:4, 0:MODW], ACT.Copy).then_inc(S("mod_row"), 1)
                left = MOD_COUNT[name] - n - 2
                if ahead:
                    high(*((name, n + 2) if left > 0 else (mod_after[name], -left)))

            def square(K, src, N):
                run(root_warm[:, :], eps[:, :], ACT.Sqrt)
                a = take("sq_added", max(K - 2, 0))
                c = take("norm_sum", 1)

                def one(k):
                    if k > 2:
                        act.wait_ge(S("sq_added"), a + k - 2)
                    out = sq_sum if k == 0 else sq[:, k % 2, :]
                    run(out[:, 0:N], src(k), ACT.Square).then_inc(S("norm_sq"), 1)
                    if k == K - 1:
                        act.wait_ge(S("norm_sum"), c + 1)
                        run(rstd[:, 0:N], bank[7][:, 0:N], ACT.Sqrt, bias=eps[:, :]).then_inc(S("rms_done"), 1)
                return one

            def res_square(N):
                b = take("res_done", KD)
                one = square(KD, lambda k: res[:, k, 0:N], N)

                def tile(k):
                    act.wait_ge(S("res_done"), b + k + 1)
                    one(k)
                return tile

            def high_input(N, shift=None, K=KD):
                b = take("norm_scaled", K * (N // T))
                h = h_of(N)[0]
                n = 0
                for k in range(K):
                    for s, at in streams(N):
                        n += 1
                        act.wait_ge(S("norm_scaled"), b + n)
                        if shift:
                            last = run(h[:, k, at:at + T], normed_f[:, k, at:at + T], ACT.Identity,
                                       bias=mod(*shift, k, s))
                        else:
                            last = run(h[:, k, at:at + T], normed_f[:, k, at:at + T], ACT.Copy)
                        last.then_inc(S("norm_high"), 1)

            def down(name, N, after=None, last=True):
                per = 2 * T // N
                tile = res_square(N) if last else take("res_done", KD)

                def body(n, j, i, ahead):
                    ahead()
                    if last and n % per == per - 1:
                        tile(n // per)

                sweep(name, KD * per, body, after, defer=last, loop=False)

            def project(name, N, after):
                tile = res_square(N)

                def body(n, j, i, ahead):
                    ahead()
                    tile(2 * n)
                    tile(2 * n + 1)

                sweep(name, KD // 2, body, after, defer=True, loop=False)

            def ffn1(l, after):
                name = f"l{l}"
                high_input(T)
                high(name + "_up", 1)
                b = take("ff_mid", FF1_TILES)
                g = take("gate_ready", FF1_TILES)
                w0 = PARAMS[f"ffn_conv{l}"][0]

                def tile(n, j, i, ahead):
                    panel_done(name + "_up", n)
                    if not (fixed(n) and n < 2):
                        act.wait_ge(S("ff_mid"), n + (b - 1))
                    run(ucv[:, j % 2, :, 2:2 + T], bank[j % 2][:, :].rearrange("p (a t) -> p a t", a=2), ACT.Copy)
                    for half in range(2):
                        w = params[:, bass.ds(n * 8 + (w0 + 4 * half + 2), 1)]
                        c = params[:, bass.ds(n * 8 + (w0 + 4 * half + 3), 1)]
                        last = run(cva[:, j % 2, half, :], bank[j % 2][:, half * T:(half + 1) * T], ACT.Identity,
                                   scale=w, bias=c)
                    last.then_inc(S("up_evac"), 1)
                    ahead()
                    act.wait_ge(S("gate_ready"), n + (g + 1))
                    run(sil[:, j % 2, 0:T], cva[:, j % 2, 0, :], ACT.Silu).then_inc(S("gate_act"), 1)

                sweep(name + "_up", FF1_TILES, tile, name + "_down")
                down(name + "_down", T, after)

            def up2(name, count, N, after):
                b = take("ff_mid", count)

                def tile(n, j, i, ahead):
                    panel_done(name, n)
                    if not (fixed(n) and n < 2):
                        act.wait_ge(S("ff_mid"), n + (b - 1))
                    run(sil[:, j % 2, 0:N], bank[2 * (j % 2)][:, 0:N], ACT.Silu).then_inc(S("gate_act"), 1)
                    ahead()

                sweep(name, count, tile, after)

            def ffn2(name, N, shift, after):
                high_input(N, shift)
                if N == T:
                    high(name + "_up", 1)
                    up2(name + "_up", FF2_TILES, N, name + "_down")
                    down(name + "_down", N, after)
                    return
                high(name + "_up0", 1)
                up2(name + "_up0", HALF_FF, N, name + "_down0")
                down(name + "_down0", N, name + "_up1", last=False)
                up2(name + "_up1", HALF_FF, N, name + "_down1")
                down(name + "_down1", N, after)

            def mixers(l):
                L = f"l{l}"
                high_input(T)
                high(L + "_in", 1)
                e = take("in_evac", 13)

                def pair(n, j, i, ahead):
                    panel_done(L + "_in", n)
                    if fixed(n) and n == 0:
                        for tb in range(2):
                            last = run(tm[:, tb, :], bank[2 + tb][:, 0:TM], ACT.Copy)
                    else:
                        last = run(U[:, bass.ds(n * 2 - 2, 2), PAD:UW],
                                   bank[j % 2][:, :].rearrange("p (a t) -> p a t", a=2), ACT.Copy)
                    last.then_inc(S("in_evac"), 1)
                    ahead()
                    if l == 0 and n == 1:
                        act.wait_ge(S("params_in"), 16)
                        run(cond[:, :, :], par("cond").rearrange("p (k s) -> p k s", s=2), ACT.Silu).then_inc(
                            S("cond_act"), 1)
                    if n == 2:
                        act.wait_ge(S("dt_raw"), l + 1)
                        run(dtw[:, 1, :], dtw[:, 0, :], ACT.Exp, scale=-1.0).then_inc(S("dt_exp"), 1)
                        run(gate[:, :, :], tm[:, :, 136:148], ACT.Exp, scale=-1.0).then_inc(S("dt_exp"), 1)
                        run(ea[:, :], par(f"a_log{l}"), ACT.Exp).then_inc(S("dt_exp"), 1)
                    for t in {9: (0, 1), 10: (2, 3), 11: (4, 5)}.get(n, ()):
                        silu_xbc(t)

                x = take("xbc_conv", 8)

                def silu_xbc(t):
                    act.wait_ge(S("xbc_conv"), x + t + 1)
                    run(xc[:, t, :], xc[:, t, :], ACT.Silu).then_inc(S("xbc_ready"), 1)

                sweep(L + "_in", 13, pair, f"mod{l}a", loop=False)
                mod_evac(f"mod{l}a", 0)
                act.wait_ge(S("in_evac"), e + 13)
                silu_xbc(6)
                silu_xbc(7)
                run(U[:, U_Z:U_Z + 4, PAD:UW], U[:, U_Z:U_Z + 4, PAD:UW], ACT.Silu).then_inc(S("z_ready"), 1)
                mod_evac(f"mod{l}a", 1)
                act.wait_ge(S("raw_free"), FIRST_RAW[L + "_cmp"] + 2 + RAW)
                run(hidT[:, :, :], bank[6][0:N_CMP, 0:2 * P].rearrange("p (c h) -> p c h", c=2),
                    ACT.Gelu_apprx_tanh).then_inc(S("hid_act"), 1)
                act.wait_ge(S("hid_turned"), l + 1)
                run(hid[:, :, :], bank[4][:, 0:32].rearrange("p (c n) -> p c n", c=2)[:, :, 0:N_CMP],
                    ACT.Copy).then_inc(S("hid_ready"), 1)
                mod_evac(f"mod{l}b", 0)
                b = take("att", 8)

                def exps(u):
                    act.wait_ge(S("att_max"), b + u + 1)
                    if u >= 2:
                        act.wait_ge(S("att_flips"), b + u - 1)
                    for r in range(2):
                        run(sbP[:, u % 2, r * T:(r + 1) * T], sbS[:, u % 2, r * T:(r + 1) * T], ACT.Exp,
                            bias=stat[:, u % 2, 3 + r:4 + r], scale=0.125, accum_out=stat[:, u % 2, 6 + r:7 + r])
                    run(sbPC[:, u % 2, 0:N_CMP], sbPC[:, u % 2, 0:N_CMP], ACT.Exp,
                        bias=stat[:, u % 2, 5:6], scale=0.125).then_inc(S("att_exp"), 1)

                def copies(u):
                    act.wait_ge(S("att_flips"), b + u + 1)
                    if u >= 2:
                        act.wait_ge(S("att_prod"), b + u - 1)
                    run(sbPCT[0:N_CMP, u % 2, :], bank[2 + u % 2][0:N_CMP, P:2 * P], ACT.Copy)
                    run(sbPT[:, u % 2, :], bank[4 + u % 2][:, :], ACT.Copy).then_inc(S("att_turned"), 1)

                exps(0)
                for u in range(8):
                    if u < 7:
                        exps(u + 1)
                    copies(u)
                    mod_evac(f"mod{l}b", u + 1)
                y = take("ssd", HEADS)

                def ssd_exp(hh):
                    act.wait_ge(S("ssd_diff"), y + hh + 1)
                    if hh >= 2:
                        act.wait_ge(S("ssd_y"), y + hh - 1)
                    run(sbP[:, hh % 2, 0:384], sbS[:, hh % 2, 0:384], ACT.Exp).then_inc(S("ssd_exp"), 1)

                ssd_exp(0)
                for hh in range(HEADS):
                    if hh < HEADS - 1:
                        ssd_exp(hh + 1)
                    if hh:
                        mod_evac(f"mod{l}b", HEADS + hh, ahead=hh < HEADS - 1)
                o = take("ssd_out", 4)
                one = square(4, lambda k: yss[:, k, :], T)
                for k in range(4):
                    act.wait_ge(S("ssd_out"), o + k + 1)
                    one(k)
                high(L + "_out", 1)
                high_y = take("ssd_scaled", 4)
                for k in range(4):
                    act.wait_ge(S("ssd_scaled"), high_y + k + 1)
                    run(h_thin[0][:, k, :], yss[:, k, :], ACT.Copy).then_inc(S("ssd_high"), 1)
                project(L + "_out", T, L + "_up")

            act.wait_ge(S("fills"), 5)
            act.wait_ge(S("x_in"), 16)
            one = square(KD, lambda k: res[:, k, 0:T], T)
            for k in range(KD - 1):
                one(k)
            high("l0_in", 0)
            one(KD - 1)
            for l in range(LAYERS):
                mixers(l)
                ffn1(l, f"l{l + 1}_in" if l + 1 < LAYERS else "m0a_up0")
            act.wait_ge(S("ctx_in"), 16)
            one = square(KD, lambda k: res[:, k, :], 2 * T)
            for k in range(KD):
                act.wait_ge(S("final1"), k + 1)
                one(k)
            ffn2("m0a", 2 * T, (0, 0), "mla_down")
            high_input(2 * T, (0, 3))
            high("mla_down", 1)
            for n in range(4):
                if n < 2:
                    panel_done("mla_down", n)
                    high("mla_down", n + 2)
                panel_done("mla_down", n)
                for t in range(2 if n < 3 else 1):
                    last = run(dpj[:, 2 * n + t, :], bank[2 * (n % 2) + t][:, :], ACT.Copy)
                last.then_inc(S("lat_evac"), 1)
            act.wait_ge(S("lat_evac"), 4)
            for at0, K in ((0, 4), (4, 2)):
                if at0:
                    act.wait_ge(S("lat_normed"), 4)
                one = square(K, lambda k: dpj[:, at0 + k, :], 2 * T)
                for k in range(K):
                    one(k)

            def pair_evac(p):
                qn, qr, qrot, kn, vv = pairs[p % 2]
                dst = [qn[:, 0, :], qn[:, 1, :], qr, kn[:, 0, :], kn[:, 1, :], vv[:, 0:2, :], vv[:, 2:4, :]]
                for t in range(7):
                    if t == 2:
                        act.wait_ge(S("raw_free"), FIRST_RAW[f"mla_pair{p}"] + 1 + RAW)
                    elif t == 6:
                        act.wait_ge(S("raw_free"), FIRST_RAW[f"mla_pair{p}"] + 2 + RAW)
                    else:
                        act.wait_ge(S("pair_tile"), 5 * p + t + (1 if t < 2 else 0))
                    src = bank[2 + t % 2][:, :]
                    if t >= 5:
                        src = src.rearrange("p (a t) -> p a t", a=2)
                    run(dst[t], src, ACT.Copy).then_inc(S("pair_evac"), 1)

            def attention(b, units, width, scores_at, scale, fill, between=None):
                def exps(u):
                    act.wait_ge(S("att_max"), b + u + 1)
                    if u >= 2:
                        act.wait_ge(S("att_flips"), b + u - 1)
                    W = width(u)
                    run(sbP[:, u % 2, 0:W], scores_at(u)[:, 0:W], ACT.Exp, bias=stat[:, u % 2, 1:2], scale=scale,
                        accum_out=stat[:, u % 2, 2:3]).then_inc(S("att_exp"), 1)

                def copies(u):
                    act.wait_ge(S("att_flips"), b + u + 1)
                    if u >= 2:
                        act.wait_ge(S("att_prod"), b + u - 1)
                    W = width(u)
                    run(sbPT[:, u % 2, 0:W], bank[4 + u % 2][:, 0:W], ACT.Copy).then_inc(S("att_turned"), 1)

                exps(0)
                exps(1)
                for u in range(units):
                    if between:
                        between(u)
                    copies(u)
                    if u < units - 2:
                        exps(u + 2)
                    for f in fill(u):
                        mod_evac(*f)

            pair_evac(0)
            high("mod2a", 0)
            high("mod2a", 1)
            attention(take("att", 32), 32, lambda u: 512 if u % 4 < 2 else 256, lambda u: bank[u % 2], 192 ** -0.5,
                      mla_fill, lambda u: pair_evac(u // 8 + 1) if u % 8 == 1 and u // 8 < 3 else None)
            project("mla_o", 2 * T, "m0b_up0")
            ffn2("m0b", 2 * T, (0, 6), "m1a_up0")
            ffn2("m1a", 2 * T, (1, 0), "swa_qkv")
            high_input(2 * T, (1, 3))
            high("swa_qkv", 1)
            for n in range(7):
                panel_done("swa_qkv", n)
                if n < 4:
                    last = run(sq_q[:, 2 * n:2 * n + 2, :], bank[n % 2][:, :].rearrange("p (a t) -> p a t", a=2), ACT.Copy)
                elif n < 6:
                    for t in range(2):
                        last = run(sq_k[:, 2 * (n - 4) + t, :], bank[2 * (n % 2) + t][:, :], ACT.Copy)
                else:
                    for t in range(2):
                        last = run(sq_v[:, 2 * t:2 * t + 2, :], bank[4 + t][:, :].rearrange("p (a t) -> p a t", a=2),
                                   ACT.Copy)
                last.then_inc(S("swa_evac"), 1)
                high(*(("swa_qkv", n + 2) if n < 5 else ("mod3", n - 5)))
            b = take("att", 32)

            def swa_exps(u):
                act.wait_ge(S("att_max"), b + u + 1)
                if u >= 2:
                    act.wait_ge(S("att_flips"), b + u - 1)
                run(sbP[:, u % 2, :], sbS[:, u % 2, :], ACT.Exp, bias=stat[:, u % 2, 1:2], scale=0.125,
                    accum_out=stat[:, u % 2, 2:3])
                run(stat[:, u % 2, 3:4], par("sink", u // 2, u // 2 + 1), ACT.Exp,
                    bias=stat[:, u % 2, 1:2]).then_inc(S("att_exp"), 1)

            def swa_copies(u):
                act.wait_ge(S("att_flips"), b + u + 1)
                if u >= 2:
                    act.wait_ge(S("att_prod"), b + u - 1)
                run(sbPT[:, u % 2, :], bank[4 + u % 2][:, :], ACT.Copy).then_inc(S("att_turned"), 1)

            swa_exps(0)
            swa_exps(1)
            for u in range(32):
                swa_copies(u)
                if u < 30:
                    swa_exps(u + 2)
                for f in swa_fill(u):
                    mod_evac(*f)
            project("swa_o", T, "m1b_up")
            ffn2("m1b", T, (1, 6), None)

        @block.vector
        def _(dve):
            take = Tally().take
            link = Chain(dve, S("dve_step"))
            V = nc.vector

            def panel_done(name, n):
                dve.wait_ge(S("panels_used"), n + (FIRST_SPLIT[name] + 1))

            def low(name, j, i=0):
                dve.wait_ge(S("high"), i * RAW + (FIRST_SPLIT[name] + j + 1))
                if fixed(i):
                    dve.wait_ge(S("raw_free"), FIRST_RAW[name] + j + i * RAW + RAW)
                w, s = WIDTH[name], half_slot(name, j)
                V.tensor_tensor(w_lo[s][:, 0:w], raw[raw_slot(name, j)][:, 0:w], w_hi[s][:, 0:w].bitcast(F32),
                                ALU.subtract).then_inc(S("raw_free"), 1)

            def sweep(name, count, body, after=None, defer=False, loop=True, chain=None, links=0):
                def step(n, j, i):
                    def ahead():
                        if not fixed(n) or n + 2 < count:
                            low(name, j + 2, i)
                        elif after and (n == count - 2 or not defer):
                            low(after, n + 2 - count)
                    body(n, j, i, ahead)

                if loop:
                    turns(dve, count, RAW, step, peel=1, tail=2, chain=chain, links=links)
                else:
                    for n in range(count):
                        step(n, n, 0)

            mb_at = PARAMS["mod_b"][0]

            def mod_vec(name, n):
                g = MOD_FIRST[name] + n
                dve.wait_ge(S("mod_cols"), g + 1)
                V.tensor_tensor(modT[:, 2 * g:2 * g + 2, :], bank[7][:, 0:4].rearrange("p (q s) -> p q s", s=2),
                                params[:, mb_at + 2 * g:mb_at + 2 * g + 2].unsqueeze(2).to_broadcast([P, 2, 2]),
                                ALU.add).then_inc(S("mod_vec"), 1)

            def mod_gains(l, parts):
                for j in parts:
                    q = (l * N_MOD + 3 * j + 1) * KD
                    g = par("mod_norm", (3 * l + j) * KD, (3 * l + j + 1) * KD).unsqueeze(2).to_broadcast([P, KD, 2])
                    link(V.scalar_tensor_tensor(modT[:, q:q + KD, :], modT[:, q:q + KD, :], 1.0, g, ALU.add, ALU.mult))
                    if j != 1:
                        link(V.tensor_scalar(modT[:, q + KD:q + 2 * KD, :], modT[:, q + KD:q + 2 * KD, :], 0.5, None,
                                             ALU.mult))

            def rms(K, N):
                c = take("rms_done", 1)
                dve.wait_ge(S("rms_done"), c + 1)
                link(V.reciprocal(rstd[:, 0:N], rstd[:, 0:N]))

            def low_input(N, gain, shift=None, K=KD):
                rms(K, T)
                per = N // T
                b = take("norm_high", K * per)
                done = take("norm_split", K * per) + K * per
                h, hl = h_of(N)
                at_ = [(k, s, at) for k in range(K) for s, at in streams(N)]
                for n in range(len(at_) + 2):
                    if n < len(at_):
                        k, s, at = at_[n]
                        if n == s == 1:
                            link(V.reciprocal(rstd[:, T:2 * T], rstd[:, T:2 * T]))
                        V.scalar_tensor_tensor(normed_f[:, k, at:at + T], res[:, k, at:at + T], gain(k, s),
                                               rstd[:, at:at + T], ALU.mult, ALU.mult).then_inc(S("norm_scaled"), 1)
                    if n >= 2:
                        k, s, at = at_[n - 2]
                        dve.wait_ge(S("norm_high"), b + n - 1)
                        f, hi, lo = (x[:, k, at:at + T] for x in (normed_f, h, hl))
                        if shift:
                            ins = V.scalar_tensor_tensor(lo, f, mod(*shift, k, s), hi.bitcast(F32), ALU.add, ALU.subtract)
                        else:
                            ins = V.tensor_tensor(lo, f, hi.bitcast(F32), ALU.subtract)
                        ins.then_inc(S("norm_split"), 1)
                return done

            def normed(K, N, src, dst, gain, sem):
                rms(K, N)
                for k in range(K):
                    V.scalar_tensor_tensor(dst(k), src(k), gain(k), rstd[:, 0:N], ALU.mult,
                                           ALU.mult).then_inc(S(sem), 1)

            def split(hi, lo, src):
                link(V.tensor_copy(hi, src))
                return V.tensor_tensor(lo, src, hi.bitcast(F32), ALU.subtract)

            def residual_plain(k, src):
                return V.tensor_tensor(res[:, k, 0:T], src, res[:, k, 0:T], ALU.add)

            def residual_mod(k, b, l, c, N):
                for s, at in streams(N):
                    last = V.scalar_tensor_tensor(res[:, k, at:at + T], bank[b][:, at:at + T], mod(l, c, k, s),
                                                  res[:, k, at:at + T], ALU.mult, ALU.add)
                return last

            def add_tile(k, N, gate_of):
                b = 4 + k % 2
                ins = residual_mod(k, b, *gate_of, N) if gate_of else residual_plain(k, bank[b][:, 0:N])
                ins.then_inc(S("res_done"), 1)

            def project(name, N, after, gate_of=None):
                hp = take("half_panel", KD // 2)

                def body(n, j, i, ahead):
                    dve.wait_ge(S("half_panel"), hp + n + 1)
                    add_tile(2 * n, N, gate_of)
                    panel_done(name, n)
                    add_tile(2 * n + 1, N, gate_of)
                    ahead()

                sweep(name, KD // 2, body, after, defer=True, loop=False)

            def down(name, N, after, gate_of=None, last=True):
                per = 2 * T // N

                def body(n, j, i, ahead):
                    if n % per == per - 1:
                        panel_done(name, n)
                        add_tile(n // per, N, gate_of)
                    ahead()

                sweep(name, KD * per, body, after, defer=last, loop=False)

            def ffn1(l, after):
                name = f"l{l}"
                low_input(T, lambda k, s: par(f"ffn_norm{l}", k, k + 1))
                low(name + "_up", 1)
                link(V.memset(ucv[:, :, :, 0:2], 0.0))
                ub = take("up_evac", FF1_TILES)
                ga = take("gate_act", FF1_TILES)
                mb = take("ff_mid", FF1_TILES)
                w0 = PARAMS[f"ffn_conv{l}"][0]
                fh, fl = hidden(f_hi, T), hidden(f_lo, T)

                def tile(n, j, i, ahead):
                    dve.wait_ge(S("up_evac"), n + (ub + 1))
                    for tap in (1, 0):
                        for half in (1, 0):
                            c = cva[:, j % 2, half, :]
                            w = params[:, bass.ds(n * 8 + (w0 + 4 * half + tap), 1)]
                            ins = V.scalar_tensor_tensor(c, ucv[:, j % 2, half, tap:tap + T], w, c, ALU.mult, ALU.add)
                            if tap:
                                ins.then_inc(S("dve_tap"), 1)
                            elif half:
                                ins.then_inc(S("dve_tap"), 1)
                            else:
                                ins.then_inc(S("gate_ready"), 1)
                            if half:
                                continue
                        if tap:
                            dve.wait_ge(S("dve_tap"), n * 3 + (3 * mb + 2))
                    ahead()
                    dve.wait_ge(S("dve_tap"), n * 3 + (3 * mb + 3))
                    dve.wait_ge(S("gate_act"), n + (ga + 1))
                    if not (fixed(n) and n == 0):
                        dve.wait_ge(S("ff_mid"), n + mb)
                    v, g = cva[:, j % 2, 1, :], sil[:, j % 2, 0:T]
                    V.tensor_tensor(prod[:, 0:T], g, v, ALU.mult)
                    link(V.tensor_tensor(fh[:, bass.ds(n, 1), :], g.unsqueeze(1), v.unsqueeze(1), ALU.mult))
                    V.tensor_tensor(fl[:, bass.ds(n, 1), :], prod[:, 0:T].unsqueeze(1),
                                    fh[:, bass.ds(n, 1), :].bitcast(F32), ALU.subtract).then_inc(S("ff_mid"), 1)

                sweep(name + "_up", FF1_TILES, tile, name + "_down", chain=link, links=1)
                down(name + "_down", T, after)

            def up2(name, count, N, after):
                ga = take("gate_act", count)
                mb = take("ff_mid", count)
                fh, fl = hidden(f_hi, N), hidden(f_lo, N)

                def tile(n, j, i, ahead):
                    dve.wait_ge(S("gate_act"), n + (ga + 1))
                    if not (fixed(n) and n == 0):
                        dve.wait_ge(S("ff_mid"), n + mb)
                    v, g = bank[2 * (j % 2) + 1][:, 0:N], sil[:, j % 2, 0:N]
                    V.tensor_tensor(prod[:, 0:N], g, v, ALU.mult)
                    link(V.tensor_tensor(fh[:, bass.ds(n, 1), :], g.unsqueeze(1), v.unsqueeze(1), ALU.mult))
                    V.tensor_tensor(fl[:, bass.ds(n, 1), :], prod[:, 0:N].unsqueeze(1),
                                    fh[:, bass.ds(n, 1), :].bitcast(F32), ALU.subtract).then_inc(S("ff_mid"), 1)
                    ahead()

                sweep(name, count, tile, after, chain=link, links=1)

            def ffn2(name, N, l, c, after):
                low_input(N, lambda k, s: mod(l, c - 1, k, s), (l, c - 2))
                if N == T:
                    low(name + "_up", 1)
                    up2(name + "_up", FF2_TILES, N, name + "_down")
                    down(name + "_down", N, after, (l, c))
                    return
                low(name + "_up0", 1)
                up2(name + "_up0", HALF_FF, N, name + "_down0")
                down(name + "_down0", N, name + "_up1", (l, c), last=False)
                up2(name + "_up1", HALF_FF, N, name + "_down1")
                down(name + "_down1", N, after, (l, c))

            def rope(out, x, rot, cos, sin, n, sem, work):
                r = work[:, 0, 0:n * T].rearrange("p (a t) -> p a t", a=n)
                c = cos.unsqueeze(1).to_broadcast([P, n, T]) if n > 1 else cos.unsqueeze(1)
                s = sin.unsqueeze(1).to_broadcast([P, n, T]) if n > 1 else sin.unsqueeze(1)
                link(V.tensor_tensor(r, rot, s, ALU.mult))
                x2 = work[:, 1, 0:n * T].rearrange("p (a t) -> p a t", a=n)
                link(V.tensor_tensor(x2, x, c, ALU.mult))
                V.tensor_tensor(out, r, x2, ALU.add).then_inc(S(sem), 1)
                dve.wait_ge(S(sem), take(sem, 1) + 1)

            def mixers(l):
                split_done = low_input(T, lambda k, s: par(f"attn_norm{l}", k, k + 1))
                low(f"l{l}_in", 1)
                e = take("in_evac", 13)
                dve.wait_ge(S("norm_split"), split_done)
                link(V.memset(U[:, U_SCC:U_Z, 0:PAD], 0.0))
                ex, x, z, z2, p, dt = (dtw[:, i, :] for i in (1, 2, 3, 4, 5, 6))

                def condition():
                    dve.wait_ge(S("fills"), 5)
                    dve.wait_ge(S("cond_act"), 1)
                    cw = cond_w[:, 0:4 * KD].rearrange("p (k c) -> p k c", c=4)
                    split(cw[:, :, 0:2], cw[:, :, 2:4], cond[:, :, :]).then_inc(S("cond_ready"), 1)
                    dve.wait_ge(S("consts_in"), 16)

                def dt_biased():
                    dve.wait_ge(S("in_evac"), e + 1)
                    b2 = par(f"dt_bias{l}").unsqueeze(1).to_broadcast([P, 2, HEADS])
                    link(V.tensor_tensor(x.rearrange("p (b h) -> p b h", b=2), tm[:, :, 0:HEADS], b2, ALU.add))
                    V.scalar_tensor_tensor(dtw[:, 0, :], x, -1.0, x, ALU.mult, ALU.max).then_inc(S("dt_raw"), 1)

                def dt_soft():
                    dve.wait_ge(S("dt_exp"), 3 * l + 3)
                    link(V.tensor_scalar(z, ex, 2.0, None, ALU.add))
                    link(V.reciprocal(z, z))
                    link(V.tensor_tensor(z, z, ex, ALU.mult))
                    link(V.tensor_tensor(z2, z, z, ALU.mult))
                    link(V.tensor_scalar(p, z2, 1.0 / 17, None, ALU.mult))
                    for c in (15, 13, 11, 9, 7, 5, 3):
                        link(V.scalar_tensor_tensor(p, p, 1.0 / c, z2, ALU.add, ALU.mult))
                    link(V.scalar_tensor_tensor(p, p, 1.0, z, ALU.add, ALU.mult))
                    link(V.tensor_scalar(x, x, 0.0, None, ALU.max))
                    link(V.scalar_tensor_tensor(dt, p, 2.0, x, ALU.mult, ALU.add))
                    e2 = ea[:, :].unsqueeze(1).to_broadcast([P, 2, HEADS])
                    V.scalar_tensor_tensor(dtw[:, 7, :].rearrange("p (b h) -> p b h", b=2),
                                           dt.rearrange("p (b h) -> p b h", b=2), -1.0, e2, ALU.mult,
                                           ALU.mult).then_inc(S("dt_ready"), 1)
                    link(V.tensor_scalar(gate[:, :, :], gate[:, :, :], 1.0, None, ALU.add))
                    link(V.reciprocal(gate[:, :, :], gate[:, :, :]))

                def keys():
                    dve.wait_ge(S("rotated"), l + 1)
                    for at0 in (0, 2, 4):
                        r = bank[2 + at0 // 2][:, :].rearrange("p (a t) -> p a t", a=2)
                        sin = con("sin1").unsqueeze(1).to_broadcast([P, 2, T])
                        cos = con("cos1").unsqueeze(1).to_broadcast([P, 2, T])
                        rs = ropet[:, 0, :].rearrange("p (a t) -> p a t", a=2)
                        xs = ropet[:, 1, :].rearrange("p (a t) -> p a t", a=2)
                        V.tensor_tensor(rs, r, sin, ALU.mult)
                        link(V.tensor_tensor(xs, U[:, at0:at0 + 2, PAD:UW], cos, ALU.mult))
                        if at0 == 0:
                            V.tensor_tensor(kvr[0:64, :], rs[0:64, 0, :], xs[0:64, 0, :], ALU.add)
                            V.tensor_tensor(kvr[64:128, 0:T - 1], rs[64:128, 1, 1:T], xs[64:128, 1, 1:T], ALU.add)
                            V.tensor_copy(kvv[0:64, :], U[0:64, U_VCKC, PAD:UW])
                            link(V.tensor_copy(kvv[64:128, 0:T - 1], U[64:128, U_KCVC, PAD + 1:UW]))
                        else:
                            link(V.tensor_tensor(krq[:, at0 - 2:at0, :], rs, xs, ALU.add))
                    for c, kv in enumerate((kvr, kvv)):
                        tok = kv[:, :].rearrange("p (n j) -> p j n", j=CMP_STRIDE)
                        for half in range(2):
                            i = slice(8 * half, 8 * half + 8)
                            ps = par(f"pos{l}", 16 * c, 16 * c + 16)[:, i].unsqueeze(2).to_broadcast([P, 8, N_CMP])
                            ins = V.tensor_tensor(tpos[:, c, i, :], tok[:, 0:CMP_STRIDE:2, half:half + N_CMP], ps,
                                                  ALU.add)
                    ins.then_inc(S("tpos_ready"), 1)

                def conv(t):
                    dve.wait_ge(S("in_evac"), e + (U_XBC + t) // 2 + 2)
                    c = xc[:, t, :]
                    w = par(f"conv_w{l}", 4 * t, 4 * t + 4)
                    u = U[:, U_XBC + t, :]
                    link(V.tensor_scalar(c, u[:, 3:3 + T], w[:, 3:4], par(f"conv_b{l}", t, t + 1), ALU.mult, ALU.add))
                    link(V.scalar_tensor_tensor(c, u[:, 2:2 + T], w[:, 2:3], c, ALU.mult, ALU.add))
                    link(V.scalar_tensor_tensor(c, u[:, 1:1 + T], w[:, 1:2], c, ALU.mult, ALU.add))
                    V.scalar_tensor_tensor(c, u[:, 0:T], w[:, 0:1], c, ALU.mult, ALU.add).then_inc(S("xbc_conv"), 1)

                def short_conv(t):
                    dve.wait_ge(S("in_evac"), e + (U_SCH + t) // 2 + 2)
                    cc = U[:, U_SCC + t, :]
                    w = par(f"sc_w{l}", 3 * t, 3 * t + 3)
                    o = sct[:, t, :]
                    link(V.tensor_tensor(cc[:, PAD:UW], cc[:, PAD:UW], U[:, U_SCH + t, PAD:UW], ALU.mult))
                    link(V.tensor_scalar(o, cc[:, 3:3 + T], w[:, 2:3], None, ALU.mult))
                    link(V.scalar_tensor_tensor(o, cc[:, 2:2 + T], w[:, 1:2], o, ALU.mult, ALU.add))
                    link(V.scalar_tensor_tensor(o, cc[:, 1:1 + T], w[:, 0:1], o, ALU.mult, ALU.add))
                    link(V.tensor_tensor(o, o, U[:, U_SCB + t, PAD:UW], ALU.mult))

                meanwhile = {1: [dt_biased], 2: [condition] if l == 0 else [], 3: [dt_soft], 5: [keys], 6: [lambda: short_conv(0)],
                             7: [lambda: conv(0)], 8: [lambda: conv(1), lambda: conv(2)],
                             9: [lambda: conv(3), lambda: conv(4)], 10: [lambda: conv(5), lambda: conv(6)],
                             11: [lambda: conv(7)], 12: [lambda: short_conv(1)]}

                def in_panel(n, j, i, ahead):
                    ahead()
                    for work in meanwhile.get(n, ()):
                        work()

                sweep(f"l{l}_in", 13, in_panel, loop=False)
                mod_vec(f"mod{l}a", 0)
                mod_vec(f"mod{l}a", 1)
                cu = take("cumulated", 1)
                dve.wait_ge(S("cumulated"), cu + 1)
                V.tensor_copy(acs[:, :, :], bank[5][:, 0:16].rearrange("p (b h) -> p b h", b=2))
                link(V.tensor_copy(acsT[:, :], bank[5][0:HEADS, T:2 * T]))
                xt = take("x_turned", 1)
                dve.wait_ge(S("x_turned"), xt + 1)
                for tb in range(2):
                    d8 = dt.rearrange("p (b h) -> p b h", b=2)[:, tb, :].unsqueeze(2).to_broadcast([P, HEADS, 64])
                    V.tensor_tensor(xdt[:, tb, :].rearrange("p (h d) -> p h d", h=HEADS),
                                    bank[2 + tb][:, :].rearrange("p (h d) -> p h d", h=HEADS), d8, ALU.mult)
                cb = take("cb_ready", 1)
                dve.wait_ge(S("cb_ready"), cb + 1)
                for g in range(GROUPS):
                    V.tensor_copy(cbT[:, g, :], bank[g][:, 0:384])
                ck = take("cmp_kv", 1)
                dve.wait_ge(S("cmp_kv"), ck + 1)
                V.tensor_copy(kc[:, :], bank[6][:, 0:N_CMP])
                V.tensor_copy(vc[:, :], bank[6][0:N_CMP, 64:128]).then_inc(S("ssm_start"), 1)
                for t in range(2):
                    split(h_thin[0][:, 4 + t, :], h_thin[1][:, 4 + t, :], sct[:, t, :]).then_inc(S("mixed"), 1)
                b = take("att", 8)
                causal = con("causal").rearrange("p (b t) -> p b t", b=2)
                cadd = con("cmp_add").rearrange("p (b t) -> p b t", b=2)
                keep = con("cmp_keep").rearrange("p (b t) -> p b t", b=2)

                def maxes(u):
                    dve.wait_ge(S("att_scores"), b + u + 1)
                    s, q = stat[:, u % 2, :], u % 2
                    for r in range(2):
                        V.tensor_tensor_reduce(sbS[:, q, r * T:(r + 1) * T], bank[q][:, r * T:(r + 1) * T],
                                               causal[:, u % 2, :], 1.0, -3e38, ALU.add, ALU.max, s[:, r:r + 1])
                    link(V.tensor_tensor_reduce(sbPC[:, q, 0:N_CMP], bank[2 + q][:, 0:N_CMP], cadd[:, u % 2, 0:N_CMP],
                                                1.0, -3e38, ALU.add, ALU.max, s[:, 2:3]))
                    V.tensor_scalar(s[:, 3:6], s[:, 0:3], -0.125, None, ALU.mult).then_inc(S("att_max"), 1)

                def probs(u):
                    dve.wait_ge(S("att_exp"), b + u + 1)
                    s, q, hh = stat[:, u % 2, :], u % 2, u // 2
                    link(V.tensor_tensor_reduce(sbPC[:, q, 0:N_CMP], sbPC[:, q, 0:N_CMP], keep[:, u % 2, 0:N_CMP],
                                                1.0, 0.0, ALU.mult, ALU.add, s[:, 8:9]))
                    link(V.tensor_scalar(s[:, 8:9], s[:, 8:9], 1e-20, None, ALU.max))
                    link(V.reciprocal(s[:, 9:12], s[:, 6:9]))
                    g = gate[:, u % 2, 3 * hh:3 * hh + 3]
                    V.tensor_tensor(s[:, 12:14], s[:, 9:11], g[:, 1:3], ALU.mult)
                    link(V.tensor_tensor(s[:, 14:15], s[:, 11:12], g[:, 0:1], ALU.mult))
                    V.tensor_scalar(sbPC[:, q, 0:N_CMP], sbPC[:, q, 0:N_CMP], s[:, 14:15], None, ALU.mult)
                    V.tensor_scalar(sbP[:, q, 0:T], sbP[:, q, 0:T], s[:, 12:13], None, ALU.mult)
                    V.tensor_scalar(sbP[:, q, T:2 * T], sbP[:, q, T:2 * T], s[:, 13:14], None,
                                    ALU.mult).then_inc(S("att_probs"), 1)

                def outs(u):
                    dve.wait_ge(S("att_prod"), b + u + 1)
                    hh = u // 2
                    rows = slice(64 * (hh % 2), 64 * (hh % 2) + 64)
                    hi, lo = (x[rows, 6 + hh // 2, (u % 2) * P:(u % 2 + 1) * P] for x in h_thin)
                    split(hi, lo, bank[6][rows, 0:P]).then_inc(S("att_out"), 1)

                maxes(0)
                for u in range(10):
                    if u < 8:
                        probs(u)
                    if u < 7:
                        maxes(u + 1)
                    if u >= 2:
                        outs(u - 2)
                    if u < 9:
                        mod_vec(f"mod{l}b", u)
                y = take("ssd", HEADS)
                mask = con("decay_mask")

                def diff(hh):
                    dve.wait_ge(S("ssd_spread"), y + hh + 1)
                    if hh >= 2:
                        dve.wait_ge(S("ssd_exp"), y + hh - 1)
                    o = sbS[:, hh % 2, :]
                    V.scalar_tensor_tensor(o[:, 0:T], bank[hh % 2][:, 0:T], acs[:, 0, hh:hh + 1], mask[:, 0:T],
                                           ALU.subtract, ALU.add)
                    V.scalar_tensor_tensor(o[:, T:384], bank[hh % 2][:, P:T], acs[:, 1, hh:hh + 1], mask[:, T:384],
                                           ALU.subtract, ALU.add).then_inc(S("ssd_diff"), 1)

                def mats(hh):
                    dve.wait_ge(S("ssd_exp"), y + hh + 1)
                    V.tensor_tensor(sbP[:, hh % 2, 0:384], sbP[:, hh % 2, 0:384], cbT[:, hh // 4, :],
                                    ALU.mult).then_inc(S("ssd_mat"), 1)

                def out(t):
                    dve.wait_ge(S("ssd_y"), y + 2 * t + 2)
                    link(V.scalar_tensor_tensor(yss[:, t, :], xc[:, t, :], par(f"d_skip{l}", t, t + 1),
                                                bank[2 + t % 2][:, 0:T], ALU.mult, ALU.add))
                    V.tensor_tensor(yss[:, t, :], yss[:, t, :], U[:, U_Z + t, PAD:UW], ALU.mult).then_inc(S("ssd_out"), 1)

                zr = take("z_ready", 1)
                dve.wait_ge(S("z_ready"), zr + 1)
                diff(0)
                for hh in range(HEADS):
                    if hh + 1 < HEADS:
                        diff(hh + 1)
                    mats(hh)
                    if (f"mod{l}b", HEADS + 1 + hh) in VECTOR_LOWS:
                        low(f"mod{l}b", HEADS + 1 + hh)
                    if hh % 2 == 0 and hh:
                        out(hh // 2 - 1)
                    if hh:
                        mod_vec(f"mod{l}b", HEADS + hh)
                out(3)
                rms(4, T)
                y2 = take("ssd_high", 4)
                for k in range(4):
                    V.scalar_tensor_tensor(yss[:, k, :], yss[:, k, :], par(f"ssd_norm{l}", k, k + 1), rstd[:, 0:T],
                                           ALU.mult, ALU.mult).then_inc(S("ssd_scaled"), 1)
                for k in range(4):
                    dve.wait_ge(S("ssd_high"), y2 + k + 1)
                    V.tensor_tensor(h_thin[1][:, k, :], yss[:, k, :], h_thin[0][:, k, :].bitcast(F32),
                                    ALU.subtract).then_inc(S("mixed"), 1)
                project(f"l{l}_out", T, f"l{l}_up")

            dve.wait_ge(S("params_in"), 16)
            dve.wait_ge(S("x_in"), 16)
            low("l0_in", 0)
            for l in range(LAYERS):
                mixers(l)
                ffn1(l, f"l{l + 1}_in" if l + 1 < LAYERS else "m0a_up0")
                if l == 1:
                    dve.wait_ge(S("mod_vec"), MOD_FIRST["mod2a"])
                    mod_gains(0, range(3))
            normed(KD, T, lambda k: res[:, k, 0:T], lambda k: res[:, k, 0:T], lambda k: par("final1", k, k + 1), "final1")
            dve.wait_ge(S("ctx_in"), 16)
            ffn2("m0a", 2 * T, 0, 2, "mla_down")
            low_input(2 * T, lambda k, s: mod(0, 4, k, s), (0, 3))
            for n in range(1, 4):
                low("mla_down", n)
            dve.wait_ge(S("rotated"), LAYERS + 1)
            rope(dpj[:, 6:7, 0:T], dpj[:, 6:7, 0:T], bank[4][:, 0:T].unsqueeze(1), con("cos2"), con("sin2"), 1,
                 "key_rope", ropes)
            normed(4, 2 * T, lambda k: dpj[:, k, :], lambda k: dpj[:, k, :], lambda k: par("q_norm", k, k + 1), "lat_normed")
            dve.wait_ge(S("lat_normed"), 4)
            normed(2, 2 * T, lambda k: dpj[:, 4 + k, :], lambda k: dpj[:, 4 + k, :],
                   lambda k: par("kv_norm", k, k + 1), "lat_normed")

            def pair_rope(p):
                qn, qr, qrot, kn, vv = pairs[p % 2]
                dve.wait_ge(S("pair_rot"), p + 1)
                rope(qrot.unsqueeze(1), qr[:, 0:T].unsqueeze(1), bank[3][:, 0:T].unsqueeze(1), con("cos2"), con("sin2"),
                     1, "pair_rope", ropes)

            def attention(units, maxes, total, outs, width, fill, between=None):
                b = take("att", units)

                def probs(u):
                    dve.wait_ge(S("att_exp"), b + u + 1)
                    W, q = width(u), u % 2
                    link(V.reciprocal(stat[:, q, 4:5], total(u)))
                    V.tensor_scalar(sbP[:, q, 0:W], sbP[:, q, 0:W], stat[:, q, 4:5], None,
                                    ALU.mult).then_inc(S("att_probs"), 1)

                maxes(0, b)
                maxes(1, b)
                for u in range(units + 2):
                    if between:
                        between(u)
                    if u < units:
                        probs(u)
                    if u >= 2:
                        outs(u - 2, b)
                    if 1 <= u <= units:
                        for f in fill(u - 1):
                            mod_vec(*f)
                    if u < units - 2:
                        maxes(u + 2, b)

            def mla_max(u, b):
                dve.wait_ge(S("att_scores"), b + u + 1)
                q = u % 2
                link(V.tensor_reduce(stat[:, q, 0:1], bank[q][:, 0:512 if u % 4 < 2 else 256], AXX, ALU.max))
                V.tensor_scalar(stat[:, q, 1:2], stat[:, q, 0:1], -(192 ** -0.5), None, ALU.mult).then_inc(S("att_max"), 1)

            def mla_out(u, b):
                dve.wait_ge(S("att_prod"), b + u + 1)
                hi, lo = (x[:, u // 4, (u % 4) * P:(u % 4 + 1) * P] for x in h_wide)
                split(hi, lo, bank[6][:, 0:P]).then_inc(S("att_out"), 1)

            pair_rope(0)
            attention(32, mla_max, lambda u: stat[:, u % 2, 2:3], mla_out, lambda u: 512 if u % 4 < 2 else 256,
                      mla_fill, lambda u: pair_rope(u // 8 + 1) if u % 8 == 3 and u // 8 < 3 else None)
            dve.wait_ge(S("mod_vec"), MOD_FIRST["mod3"])
            mod_gains(1, range(2))
            project("mla_o", 2 * T, "m0b_up0", (0, 5))
            ffn2("m0b", 2 * T, 0, 8, "m1a_up0")
            ffn2("m1a", 2 * T, 1, 2, "swa_qkv")
            low_input(2 * T, lambda k, s: mod(1, 4, k, s), (1, 3))
            for n in range(1, 7):
                low("swa_qkv", n)
            for g in range(6):
                dve.wait_ge(S("swa_rot"), g + 1)
                rot = bank[6 + g % 2][:, :].rearrange("p (a t) -> p a t", a=2)
                if g < 4:
                    src, dst = sq_q[:, 2 * g:2 * g + 2, :], sq_qrot[:, 2 * g:2 * g + 2, :]
                else:
                    src = dst = sq_k[:, 2 * (g - 4):2 * (g - 4) + 2, 0:T]
                rope(dst, src, rot, con("cos2"), con("sin2"), 2, "swa_rope", ropet)
            window = con("window").rearrange("p (b t) -> p b t", b=2)
            V.tensor_copy(sq[:, :, 0:T], window)
            link(V.memset(sq[:, :, T:2 * T], 0.0))

            def swa_max(u, b):
                dve.wait_ge(S("att_scores"), b + u + 1)
                q = u % 2
                s = stat[:, q, :]
                link(V.tensor_tensor_reduce(sbS[:, q, :], bank[q][:, :], sq[:, u % 2, :], 1.0, -3e38, ALU.add,
                                            ALU.max, s[:, 0:1]))
                link(V.tensor_scalar(s[:, 0:1], s[:, 0:1], 0.125, par("sink", u // 2, u // 2 + 1), ALU.mult, ALU.max))
                V.tensor_scalar(s[:, 1:2], s[:, 0:1], -1.0, None, ALU.mult).then_inc(S("att_max"), 1)

            def swa_total(u):
                s = stat[:, u % 2, :]
                link(V.tensor_tensor(s[:, 7:8], s[:, 2:3], s[:, 3:4], ALU.add))
                return s[:, 7:8]

            def swa_out(u, b):
                dve.wait_ge(S("att_prod"), b + u + 1)
                hh = u // 2
                rows = slice(64 * (hh % 2), 64 * (hh % 2) + 64)
                hi, lo = (x[rows, hh // 2, (u % 2) * P:(u % 2 + 1) * P] for x in h_thin)
                split(hi, lo, bank[6][rows, 0:P]).then_inc(S("att_out"), 1)

            attention(32, swa_max, swa_total, swa_out, lambda u: 512, swa_fill)
            dve.wait_ge(S("mod_vec"), MOD_PANELS)
            mod_gains(1, (2,))
            project("swa_o", T, "m1b_up", (1, 5))
            ffn2("m1b", T, 1, 8, None)
            normed(KD, T, lambda k: res[:, k, 0:T], lambda k: normed_f[:, k, 0:T], lambda k: par("final2", k, k + 1),
                   "final_out")


def tiles_of(w):
    K, M = w.shape
    k, m = -(-K // P), -(-M // P)
    full = np.zeros((k * P, m * P), np.float32)
    full[:K, :M] = w
    return full.reshape(k, P, m, P).transpose(2, 1, 0, 3)


def pair_panels(t):
    if len(t) % 2:
        t = np.concatenate([t, np.zeros_like(t[:1])])
    n, p, k, m = t.shape
    return t.reshape(n // 2, 2, p, k, m).transpose(0, 2, 1, 3, 4).reshape(n // 2, p, 2 * k * m)


def down_panels(w):
    return tiles_of(w).reshape(KD, P, 2, DOWN).transpose(0, 2, 1, 3).reshape(2 * KD, P, DOWN)


def columns(v):
    v = np.asarray(v)
    n = -(-v.shape[-1] // P) * P
    out = np.zeros(v.shape[:-1] + (n,), np.float32)
    out[..., :v.shape[-1]] = v
    return np.moveaxis(out.reshape(v.shape[:-1] + (n // P, P)), -1, 0)


def constants():
    c = np.zeros((P, CONST_W), np.float32)

    def put(name, v):
        at, w = CONSTS[name]
        v = np.asarray(v, np.float32)
        c[:v.shape[0], at:at + w] = v.reshape(v.shape[0], -1)

    i, t = np.arange(P), np.arange(T)
    put("ident", np.eye(P))
    tok = np.arange(2)[None, :, None] * P + i[:, None, None]
    put("tri", tok <= t)
    put("rot", (i[:, None] ^ 32) == i[None, :])
    f32 = np.float32
    half = 32
    inv1 = f32(1.0) / (f32(10000.0) ** (np.arange(half, dtype=f32) / f32(half)))
    ang1 = t.astype(f32)[:, None] * inv1[None, :]
    n = 16
    inv2 = np.exp(f32(-np.log(10000.0)) * np.arange(n, dtype=f32) / f32(n)).astype(f32)
    ang2 = np.concatenate([(t // 64).astype(f32)[:, None] * inv2, (t % 64).astype(f32)[:, None] * inv2], -1)
    for name, ang in (("1", ang1), ("2", ang2)):
        ang = ang.astype(f32).T
        put("cos" + name, np.tile(np.cos(ang), (4, 1)))
        s = np.sin(ang)
        put("sin" + name, np.concatenate([-s, s, -s, s]))
    put("causal", np.where(t <= tok, 0, NEG))
    m = np.where(tok <= t, 0, NEG)
    put("decay_mask", np.concatenate([m[:, 0], m[:, 1, P:]], -1))
    end = np.arange(16) * CMP_STRIDE + CMP_BLOCK - 1
    put("cmp_add", np.where(end <= tok, 0, NEG))
    put("cmp_keep", end <= tok)
    put("window", np.where(np.abs(t - tok) <= 128, 0, NEG))
    put("fold", np.tile(np.eye(2), (2, 1)))
    return c


def kernel(**inputs):
    import concourse.bacc as bacc
    from concourse.bass_utils import run_bass_kernel_spmd

    a = {k: np.asarray(v) for k, v in inputs.items()}
    par = np.zeros((P, PARAM_W), np.float32)

    def put(name, v):
        at, w = PARAMS[name]
        par[:v.shape[0], at:at + w] = v.reshape(v.shape[0], -1)

    def rows(v):
        return np.broadcast_to(v, (P,) + v.shape)

    w = {}
    mods = a["mod_w_2"].reshape(LAYERS, KD, P, N_MOD * DM // MODW, MODW).transpose(0, 3, 2, 1, 4).reshape(
        MOD_PANELS, P, KD * MODW)
    for name, first in MOD_FIRST.items():
        w[name] = mods[first:first + MOD_COUNT[name]]
    for l in range(LAYERS):
        wi = a["w_in"][l]
        cuts = np.cumsum([INNER, XBC, HEADS, SC, SC, SC, 256] + [64] * 6 + [12])
        z, xbc, dt, scb, scc, sch, q, kc, vc, ks, vs, kw, vw, g = np.split(wi, cuts[:-1], axis=1)
        t = tiles_of(np.concatenate([kc, vc, vc, kc, ks, ks, kw, kw, q, scb, scc, sch, xbc, z], axis=1))
        tmw = np.concatenate([dt, vs, vw, g], axis=1).reshape(KD, P, TM).transpose(1, 0, 2).reshape(P, KD * TM)
        tmw = np.concatenate([tmw, np.zeros((P, PANEL - KD * TM), np.float32)], axis=1)
        w[f"l{l}_in"] = np.concatenate([tmw[None], pair_panels(t)])
        w[f"l{l}_cmp"] = np.stack([a[n][l].reshape(CMP_BLOCK // 2, 2, 64, P).transpose(1, 2, 0, 3).reshape(P, PANEL)
                                   for n in ("cmp_k_w1", "cmp_v_w1")])
        w[f"l{l}_out"] = pair_panels(tiles_of(a["w_out"][l]))
        g, v = tiles_of(a["ffn_w_up"][l][:, :FF1]), tiles_of(a["ffn_w_up"][l][:, FF1:])
        w[f"l{l}_up"] = pair_panels(np.stack([g, v], 1).reshape((2 * FF1_TILES,) + g.shape[1:]))
        w[f"l{l}_down"] = down_panels(a["ffn_w_down"][l])
        put(f"attn_norm{l}", columns(a["attn_norm_w"][l]))
        put(f"ffn_norm{l}", columns(a["ffn_norm_w"][l]))
        put(f"conv_w{l}", columns(a["ssd_conv_w"][l]).transpose(0, 2, 1))
        put(f"conv_b{l}", columns(a["ssd_conv_b"][l]))
        put(f"dt_bias{l}", rows(a["ssd_dt_bias"][l]))
        put(f"a_log{l}", rows(a["ssd_a_log"][l]))
        put(f"d_skip{l}", columns(np.repeat(a["ssd_d"][l], HDIM)))
        put(f"ssd_norm{l}", columns(a["ssd_norm_w"][l]))
        put(f"sc_w{l}", columns(a["sc_conv_w"][l]).transpose(0, 2, 1))
        put(f"pos{l}", np.concatenate([a[n][l].reshape(CMP_BLOCK // 2, 2, 64).transpose(1, 2, 0).reshape(P, -1)
                                       for n in ("cmp_k_pos", "cmp_v_pos")], axis=1))
        put(f"k_w2{l}", np.concatenate([a["cmp_k_w2"][l]] * 2, axis=1))
        put(f"v_w2{l}", a["cmp_v_w2"][l])
        cw = np.concatenate([a["ffn_conv_w"][l], a["ffn_conv_b"][l][None]])
        cw = np.stack([columns(cw[:, :FF1]), columns(cw[:, FF1:])], 1)
        put(f"ffn_conv{l}", cw.transpose(0, 3, 1, 2))
        for j, s in enumerate("ab"):
            wi = a["ffn_w_in_2"][l, j]
            g, v = tiles_of(wi[:, :FF2_TILES * P]), tiles_of(wi[:, FF2_TILES * P:])
            gv = pair_panels(np.stack([g, v], 1).reshape((2 * FF2_TILES,) + g.shape[1:]))
            dn = down_panels(a["ffn_w_out_2"][l, j])
            if (l, s) == (1, "b"):
                w["m1b_up"], w["m1b_down"] = gv, dn
            else:
                for part in range(2):
                    w[f"m{l}{s}_up{part}"] = gv[part * HALF_FF:(part + 1) * HALF_FF]
                    w[f"m{l}{s}_down{part}"] = dn[part::2]
    put("final1", columns(a["final_norm_w"]))
    put("cond", np.stack([columns(a["c_2"][0]), columns(a["c_ctx_2"])], -1))
    put("mod_norm", columns(a["norm_g_2"]))
    put("mod_b", columns(a["mod_b_2"]))
    put("final2", columns(a["final_norm_g_2"]))
    put("q_norm", columns(a["mla_q_norm_2"][0]))
    put("kv_norm", columns(a["mla_kv_norm_2"][0]))
    put("sink", rows(a["swa_sink_2"][0]))
    wd = a["mla_w_down_2"][0]
    w["mla_down"] = pair_panels(tiles_of(np.concatenate([wd, wd[:, 768:]], axis=1)))
    uq = a["mla_w_uq_2"][0].reshape(4, P, MLA_HEADS, 192)
    ukv = a["mla_w_ukv_2"][0].reshape(2, P, MLA_HEADS, 256)
    panels = []
    for p in range(4):
        hs = (2 * p, 2 * p + 1)
        qn = [uq[:, :, x, :128].transpose(1, 0, 2).reshape(P, -1) for x in hs]
        qr = [np.concatenate([uq[:, :, x, 128:] for x in hs], -1).transpose(1, 0, 2).reshape(P, -1)]
        kn = [ukv[:, :, x, :128].transpose(1, 0, 2).reshape(P, -1) for x in hs]
        vv = [np.concatenate([ukv[:, :, x, 128:] for x in hs], -1).transpose(1, 0, 2).reshape(P, -1)]
        panels.append(np.concatenate(qn + qr, axis=1))
        panels.append(np.concatenate(kn + vv + [np.zeros((P, 512), np.float32)], axis=1))
    for p in range(4):
        w[f"mla_pair{p}"] = np.stack(panels[2 * p:2 * p + 2])
    w["mla_o"] = pair_panels(tiles_of(a["mla_w_o_2"][0]))
    qkv = a["swa_w_qkv_2"][0]
    k = qkv[:, 1024:1280].reshape(DM, SWA_KV, 1, 64)
    k = np.concatenate([k, k], axis=2).reshape(DM, SWA_KV * P)
    v = qkv[:, 1280:].reshape(KD, P, T).transpose(1, 0, 2).reshape(1, P, KD * T)
    w["swa_qkv"] = np.concatenate([pair_panels(tiles_of(np.concatenate([qkv[:, :1024], k], axis=1))), v])
    w["swa_o"] = pair_panels(tiles_of(a["swa_w_o_2"][0]))

    def tokens(x):
        return np.ascontiguousarray(x.reshape(T, KD, P).transpose(2, 1, 0))

    arrays = {"x": tokens(a["x"]), "ctx": tokens(a["ctx_2"]), "params": par, "consts": constants()}
    for name, count, width, _ in STREAM:
        arrays["w_" + name] = np.ascontiguousarray(w[name])
        assert arrays["w_" + name].shape == (count, P, width), name
    nc = bacc.Bacc("TRN2", target_bir_lowering=False, num_devices=1)
    t = {n: nc.dram_tensor(n, v.shape, F32, kind="ExternalInput").ap() for n, v in arrays.items()}
    out = nc.dram_tensor("out", (P, KD, T), F32, kind="ExternalOutput").ap()
    two_blocks(nc, t["x"], t["ctx"], t["params"], t["consts"], {n: t["w_" + n] for n, _, _, _ in STREAM}, out)
    r = run_bass_kernel_spmd(nc, [arrays], core_ids=[0])
    y = np.asarray(r.results[0]["out"])
    return y.transpose(2, 1, 0).reshape(1, T, DM)
```
